# Optimizing a Trainium2 kernel written in Bass

```python
import math
import jax, jax.numpy as jnp
from jax import lax
import numpy as np
import jax
import jax.numpy as jnp

D_MODEL = 1024
BATCH = 1
SEQ = 256
DEPTH = 2

CHUNK = 64
N_A_LAYERS = DEPTH // 2
N_B_LAYERS = DEPTH - N_A_LAYERS

A_HEADS = 8
A_HEAD_K = 128
A_HEAD_V = 128
A_QK_WIDTH = A_HEADS * A_HEAD_K
A_V_WIDTH = A_HEADS * A_HEAD_V
A_CONV = 4
A_CONV_WIDTH = 2 * A_QK_WIDTH + A_V_WIDTH
A_IN_WIDTH = 2 * A_QK_WIDTH + 2 * A_V_WIDTH + 2 * A_HEADS

B_HEADS = 16
B_HEAD_DIM = 64
B_WIDTH = B_HEADS * B_HEAD_DIM
LEFT_CHUNKS = 8
BAND = (LEFT_CHUNKS + 1) * CHUNK
REL_CLIP = 256

FFN_DIM = 2816
FFN_CONV = 3

EPS = 1e-6
NEG_INF = -1e30


def rmsnorm(x, g):
    xf = x.astype(jnp.float32)
    y = xf * lax.rsqrt(jnp.mean(xf * xf, axis=-1, keepdims=True) + EPS)
    return (y * g.astype(jnp.float32)).astype(x.dtype)

def causal_dwconv(x, w):
    width = w.shape[0]
    return lax.conv_general_dilated(
        x, w[:, None, :].astype(x.dtype), window_strides=(1,), padding=[(width - 1, 0)],
        dimension_numbers=("NWC", "WIO", "NWC"), feature_group_count=x.shape[-1])

def _l2norm(t):
    return t * lax.rsqrt(jnp.sum(t * t, axis=-1, keepdims=True) + EPS)

def chunk_gated_delta_rule(q, k, v, beta, g):
    bsz, seq, nh, dk = q.shape
    dv = v.shape[-1]
    nc = seq // CHUNK

    def chunks(t):
        return t.reshape(bsz, nc, CHUNK, nh, -1).transpose(0, 3, 1, 2, 4)

    q, k, v = chunks(q), chunks(k), chunks(v)
    beta = chunks(beta[..., None])[..., 0]
    gcum = jnp.cumsum(chunks(g[..., None])[..., 0], axis=-1)

    causal = jnp.tril(jnp.ones((CHUNK, CHUNK), dtype=bool))
    strict = jnp.tril(jnp.ones((CHUNK, CHUNK), dtype=bool), k=-1)
    diff = gcum[..., :, None] - gcum[..., None, :]
    decay = jnp.where(causal, jnp.exp(jnp.where(causal, diff, 0.0)), 0.0)

    k_beta = k * beta[..., None]
    m = jnp.where(strict, jnp.einsum("bhnid,bhnjd->bhnij", k_beta, k) * decay, 0.0)
    eye = jnp.eye(CHUNK, dtype=m.dtype)
    rhs = jnp.concatenate([v * beta[..., None], k_beta * jnp.exp(gcum)[..., None]], axis=-1)
    uw = lax.linalg.triangular_solve(m + eye, rhs, left_side=True, lower=True, unit_diagonal=True)
    u, w = uw[..., :dv], uw[..., dv:]

    attn_qk = jnp.einsum("bhnid,bhnjd->bhnij", q, k) * decay
    q_dec = q * jnp.exp(gcum)[..., None]
    k_end = k * jnp.exp(gcum[..., -1:] - gcum)[..., None]
    chunk_decay = jnp.exp(gcum[..., -1])

    xs = tuple(jnp.moveaxis(t, 2, 0) for t in (q_dec, k_end, u, w, attn_qk, chunk_decay))

    def step(state, inp):
        qd, ke, u_c, w_c, a_c, dec = inp
        v_new = u_c - jnp.einsum("bhcd,bhdv->bhcv", w_c, state)
        o_c = jnp.einsum("bhcd,bhdv->bhcv", qd, state) + jnp.einsum("bhcj,bhjv->bhcv", a_c, v_new)
        state = state * dec[..., None, None] + jnp.einsum("bhcd,bhcv->bhdv", ke, v_new)
        return state, o_c

    state0 = jnp.zeros((bsz, nh, dk, dv), jnp.float32)
    _, o = lax.scan(step, state0, xs)
    return o.transpose(1, 0, 3, 2, 4).reshape(bsz, seq, nh, dv)

def gated_deltanet(xn, w_in, conv_w, A_log, dt_bias, out_norm_w, w_out):
    bsz, seq, _ = xn.shape
    proj = xn @ w_in
    qkv = jax.nn.silu(causal_dwconv(proj[..., :A_CONV_WIDTH], conv_w))
    z = proj[..., A_CONV_WIDTH:A_CONV_WIDTH + A_V_WIDTH]
    b_raw = proj[..., A_CONV_WIDTH + A_V_WIDTH:A_CONV_WIDTH + A_V_WIDTH + A_HEADS]
    a_raw = proj[..., A_CONV_WIDTH + A_V_WIDTH + A_HEADS:]
    f32 = jnp.float32
    q = _l2norm(qkv[..., :A_QK_WIDTH].reshape(bsz, seq, A_HEADS, A_HEAD_K).astype(f32)) * (A_HEAD_K ** -0.5)
    k = _l2norm(qkv[..., A_QK_WIDTH:2 * A_QK_WIDTH].reshape(bsz, seq, A_HEADS, A_HEAD_K).astype(f32))
    v = qkv[..., 2 * A_QK_WIDTH:].reshape(bsz, seq, A_HEADS, A_HEAD_V).astype(f32)
    beta = jax.nn.sigmoid(b_raw.astype(f32))
    g = -jnp.exp(A_log.astype(f32)) * jax.nn.softplus(a_raw.astype(f32) + dt_bias.astype(f32))
    o = chunk_gated_delta_rule(q, k, v, beta, g).astype(xn.dtype)
    o = rmsnorm(o, out_norm_w) * jax.nn.silu(z.reshape(bsz, seq, A_HEADS, A_HEAD_V))
    return o.reshape(bsz, seq, A_V_WIDTH) @ w_out

def chunk_attention(xn, w_q, rel_bias, w_out, k_pad, v_pad):
    bsz, seq, _ = xn.shape
    nc = seq // CHUNK
    q = (xn @ w_q).reshape(bsz, nc, CHUNK, B_HEADS, B_HEAD_DIM).transpose(1, 0, 2, 3, 4)
    rel = jnp.arange(CHUNK)[:, None] + LEFT_CHUNKS * CHUNK - jnp.arange(BAND)[None, :]
    bias = rel_bias[:, jnp.clip(rel, -REL_CLIP, REL_CLIP) + REL_CLIP].astype(jnp.float32)
    scale = B_HEAD_DIM ** -0.5

    def one_chunk(args):
        n, q_n = args
        k_band = lax.dynamic_slice_in_dim(k_pad, n * CHUNK, BAND, axis=1)
        v_band = lax.dynamic_slice_in_dim(v_pad, n * CHUNK, BAND, axis=1)
        s = jnp.einsum("bqhd,bkhd->bhqk", q_n, k_band).astype(jnp.float32) * scale + bias
        valid = jnp.arange(BAND) >= (LEFT_CHUNKS - n) * CHUNK
        s = jnp.where(valid, s, NEG_INF)
        p = jax.nn.softmax(s, axis=-1).astype(v_band.dtype)
        return jnp.einsum("bhqk,bkhd->bqhd", p, v_band)

    o = lax.map(one_chunk, (jnp.arange(nc, dtype=jnp.int32), q))
    o = o.transpose(1, 0, 2, 3, 4).reshape(bsz, seq, B_WIDTH)
    return o @ w_out

def conv_ffn(xn, w_up, conv_w, conv_b, w_down):
    h = causal_dwconv(xn @ w_up, conv_w) + conv_b
    gate, val = h[..., :FFN_DIM], h[..., FFN_DIM:]
    return (jax.nn.silu(gate) * val) @ w_down

def first_inputs(seed: int = 0) -> dict:
    key = jax.random.key(seed)
    ks = jax.random.split(key, 22)

    def nrm(k, shape, scale):
        return jax.random.normal(k, shape, jnp.float32) * scale

    dt = jnp.exp(jax.random.uniform(ks[5], (N_A_LAYERS, A_HEADS), jnp.float32,
                                    minval=math.log(1e-3), maxval=math.log(1e-1)))
    return {
        "x": nrm(ks[0], (BATCH, SEQ, D_MODEL), 1.0),
        "a_norm": 1.0 + nrm(ks[1], (N_A_LAYERS, D_MODEL), 0.02),
        "a_w_in": nrm(ks[2], (N_A_LAYERS, D_MODEL, A_IN_WIDTH), D_MODEL ** -0.5),
        "a_conv": nrm(ks[3], (N_A_LAYERS, A_CONV, A_CONV_WIDTH), A_CONV ** -0.5),
        "a_A_log": jnp.log(jax.random.uniform(ks[4], (N_A_LAYERS, A_HEADS), jnp.float32, minval=1.0, maxval=16.0)),
        "a_dt_bias": dt + jnp.log(-jnp.expm1(-dt)),
        "a_out_norm": 1.0 + nrm(ks[6], (N_A_LAYERS, A_HEAD_V), 0.02),
        "a_w_out": nrm(ks[7], (N_A_LAYERS, A_V_WIDTH, D_MODEL), A_V_WIDTH ** -0.5),
        "kv_norm": 1.0 + nrm(ks[8], (D_MODEL,), 0.02),
        "w_kv": nrm(ks[9], (D_MODEL, 2 * B_WIDTH), D_MODEL ** -0.5),
        "b_norm": 1.0 + nrm(ks[10], (N_B_LAYERS, D_MODEL), 0.02),
        "b_w_q": nrm(ks[11], (N_B_LAYERS, D_MODEL, B_WIDTH), D_MODEL ** -0.5),
        "b_rel_bias": nrm(ks[12], (N_B_LAYERS, B_HEADS, 2 * REL_CLIP + 1), 0.1),
        "b_w_out": nrm(ks[13], (N_B_LAYERS, B_WIDTH, D_MODEL), B_WIDTH ** -0.5),
        "f_norm": 1.0 + nrm(ks[14], (DEPTH, D_MODEL), 0.02),
        "f_w_up": nrm(ks[15], (DEPTH, D_MODEL, 2 * FFN_DIM), D_MODEL ** -0.5),
        "f_conv": nrm(ks[16], (DEPTH, FFN_CONV, 2 * FFN_DIM), FFN_CONV ** -0.5),
        "f_conv_b": nrm(ks[17], (DEPTH, 2 * FFN_DIM), 0.01),
        "f_w_down": nrm(ks[18], (DEPTH, FFN_DIM, D_MODEL), FFN_DIM ** -0.5),
        "final_norm": 1.0 + nrm(ks[19], (D_MODEL,), 0.02),
    }

def first_block(x, a_norm, a_w_in, a_conv, a_A_log, a_dt_bias, a_out_norm, a_w_out,
              kv_norm, w_kv, b_norm, b_w_q, b_rel_bias, b_w_out,
              f_norm, f_w_up, f_conv, f_conv_b, f_w_down, final_norm):
    bsz, seq, _ = x.shape
    h = x
    k_pad = None
    v_pad = None
    for layer in range(DEPTH):
        if layer < N_A_LAYERS:
            i = layer
            h = h + gated_deltanet(rmsnorm(h, a_norm[i]), a_w_in[i], a_conv[i], a_A_log[i],
                                   a_dt_bias[i], a_out_norm[i], a_w_out[i])
        else:
            if layer == N_A_LAYERS:
                kv = rmsnorm(h, kv_norm) @ w_kv
                pad = ((0, 0), (LEFT_CHUNKS * CHUNK, 0), (0, 0), (0, 0))
                k_pad = jnp.pad(kv[..., :B_WIDTH].reshape(bsz, seq, B_HEADS, B_HEAD_DIM), pad)
                v_pad = jnp.pad(kv[..., B_WIDTH:].reshape(bsz, seq, B_HEADS, B_HEAD_DIM), pad)
            j = layer - N_A_LAYERS
            h = h + chunk_attention(rmsnorm(h, b_norm[j]), b_w_q[j], b_rel_bias[j], b_w_out[j], k_pad, v_pad)
        h = h + conv_ffn(rmsnorm(h, f_norm[layer]), f_w_up[layer], f_conv[layer], f_conv_b[layer], f_w_down[layer])
    return rmsnorm(h, final_norm)


DEPTH_2 = 1

CTX_LEN = 256
GRID_W = 64

RET_HEADS = 4
RET_DK = 128
RET_DV = 128
RET_CHUNK = 128
RET_W = RET_HEADS * RET_DV
RET_SCALE = RET_DK ** -0.5

ATT_HEADS = 8
ATT_KV_HEADS = 2
ATT_GROUP = ATT_HEADS // ATT_KV_HEADS
ATT_HD = 64
ATT_W = ATT_HEADS * ATT_HD
ATT_SCALE = ATT_HD ** -0.5
Q_BLOCK = 128

MIX_W = RET_W + ATT_W
D_FF = 4 * D_MODEL
ROPE_BASE = 10000.0

RQ_OFF = 0
RK_OFF = RQ_OFF + RET_HEADS * RET_DK
RV_OFF = RK_OFF + RET_HEADS * RET_DK
RG_OFF = RV_OFF + RET_W
AQ_OFF = RG_OFF + RET_W
AK_OFF = AQ_OFF + ATT_W
AV_OFF = AK_OFF + ATT_KV_HEADS * ATT_HD
D_IN = AV_OFF + ATT_KV_HEADS * ATT_HD
SPLIT_IDX = [RK_OFF, RV_OFF, RG_OFF, AQ_OFF, AK_OFF, AV_OFF]


def _rmsnorm(x, g):
    xf = x.astype(jnp.float32)
    y = xf * lax.rsqrt(jnp.mean(xf * xf, axis=-1, keepdims=True) + EPS)
    return (y * g.astype(jnp.float32)).astype(x.dtype)

def _modulate(h, shift, scale):
    return h * (1 + scale) + shift

def _freqs(n_pairs):
    return ROPE_BASE ** (-jnp.arange(n_pairs, dtype=jnp.float32) / n_pairs)

def _apply_rope(x, cos, sin):
    x1, x2 = jnp.split(x, 2, axis=-1)
    return jnp.concatenate([x1 * cos - x2 * sin, x1 * sin + x2 * cos], axis=-1).astype(x.dtype)

def _heads(t, n_heads):
    B, L, W = t.shape
    return t.reshape(B, L, n_heads, W // n_heads).transpose(0, 2, 1, 3)

def _retention_chunkwise(q, k, v, log_gamma, s0):
    B, H, L, dk = q.shape
    dv = v.shape[-1]
    n_chunks = L // RET_CHUNK

    def chunks(t):
        return jnp.moveaxis(t.reshape(B, H, n_chunks, RET_CHUNK, t.shape[-1]), 2, 0)

    idx = jnp.arange(RET_CHUNK, dtype=jnp.float32)
    lg = log_gamma.astype(jnp.float32)[:, None]
    rel = idx[:, None] - idx[None, :]
    intra = jnp.where(rel >= 0, jnp.exp(lg[:, :, None] * jnp.maximum(rel, 0.0)), 0.0)
    q_dec = jnp.exp(lg * (idx + 1.0))[:, :, None]
    k_dec = jnp.exp(lg * (RET_CHUNK - 1.0 - idx))[:, :, None]
    c_dec = jnp.exp(lg * RET_CHUNK)[:, :, None]

    def step(state, qkv):
        qf, kf, vf = (t.astype(jnp.float32) for t in qkv)
        scores = jnp.einsum('bhid,bhjd->bhij', qf, kf) * intra
        o = (jnp.einsum('bhij,bhjv->bhiv', scores, vf)
             + jnp.einsum('bhid,bhdv->bhiv', qf, state) * q_dec)
        state = state * c_dec + jnp.einsum('bhjd,bhjv->bhdv', kf * k_dec, vf)
        return state, o

    s_fin, o = lax.scan(step, s0, (chunks(q), chunks(k), chunks(v)))
    o = jnp.moveaxis(o, 0, 2).reshape(B, H, L, dv)
    return o, s_fin

def _retention_final_state(k, v, log_gamma):
    L = k.shape[2]
    pos = jnp.arange(L, dtype=jnp.float32)
    w = jnp.exp(log_gamma.astype(jnp.float32)[:, None] * (L - 1.0 - pos))
    return jnp.einsum('bhld,bhlv->bhdv', k.astype(jnp.float32) * w[:, :, None], v.astype(jnp.float32))

def _flip(t):
    return jnp.flip(t, axis=2)

def _bidir_retention(q, k, v, log_gamma, s0_fwd, s0_bwd):
    o_f, s_f = _retention_chunkwise(q, k, v, log_gamma[0], s0_fwd)
    o_b, s_b = _retention_chunkwise(_flip(q), _flip(k), _flip(v), log_gamma[1], s0_bwd)
    return o_f + _flip(o_b), s_f, s_b

def _ret_out(o, gate, gn_g):
    B, H, L, dv = o.shape
    mu = jnp.mean(o, axis=-1, keepdims=True)
    var = jnp.mean(jnp.square(o - mu), axis=-1, keepdims=True)
    o = ((o - mu) * lax.rsqrt(var + EPS)).transpose(0, 2, 1, 3).reshape(B, L, H * dv)
    o = o * gn_g.astype(jnp.float32)
    return (o * jax.nn.silu(gate.astype(jnp.float32))).astype(gate.dtype)

def _dense_attention(q, k, v):
    s = jnp.einsum('bqkgd,bskd->bkgqs', q, k).astype(jnp.float32) * ATT_SCALE
    p = jax.nn.softmax(s, axis=-1).astype(v.dtype)
    return jnp.einsum('bkgqs,bskd->bqkgd', p, v)

def _latent_attention(q, k_lat, v_lat, k_ctx, v_ctx):
    B, L = q.shape[:2]
    k_all = jnp.concatenate([k_ctx, k_lat], axis=1)
    v_all = jnp.concatenate([v_ctx, v_lat], axis=1)
    qb = jnp.moveaxis(q.reshape(B, L // Q_BLOCK, Q_BLOCK, ATT_KV_HEADS, ATT_GROUP, ATT_HD), 1, 0)
    o = lax.map(lambda qblk: _dense_attention(qblk, k_all, v_all), qb)
    return jnp.moveaxis(o, 0, 1).reshape(B, L, ATT_W)

def _sqrelu_mlp(h, w1, w2):
    return jnp.square(jax.nn.relu(h @ w1)) @ w2

def _layer(x, xc, c_act, cc_act, w_mod, b_mod, norm1_g, norm2_g, w_in, w_out,
           ret_log_rate, ret_gn_g, q_norm_g, k_norm_g, w_ff1, w_ff2,
           ret_cs, att_cs, ctx_out):
    B, L, _ = x.shape
    Lc = xc.shape[1]
    mod = (c_act @ w_mod + b_mod)[:, None, :]
    mod_c = (cc_act @ w_mod + b_mod)[None, None, :]
    sh1, sc1, g1, sh2, sc2, g2 = jnp.split(mod, 6, axis=-1)
    csh1, csc1, cg1, csh2, csc2, cg2 = jnp.split(mod_c, 6, axis=-1)
    log_gamma = jnp.log1p(-jnp.exp(ret_log_rate.astype(jnp.float32)))

    h = _modulate(_rmsnorm(x, norm1_g), sh1, sc1)
    hc = _modulate(_rmsnorm(xc, norm1_g), csh1, csc1)
    rq, rk, rv, rg, aq, ak, av = jnp.split(h @ w_in, SPLIT_IDX, axis=-1)
    if ctx_out:
        crq, crk, crv, crg, caq, cak, cav = jnp.split(hc @ w_in, SPLIT_IDX, axis=-1)
    else:
        crk, crv = jnp.split(hc @ w_in[:, RK_OFF:RG_OFF], 2, axis=-1)
        cak, cav = jnp.split(hc @ w_in[:, AK_OFF:D_IN], 2, axis=-1)

    crk_h = _heads(crk, RET_HEADS) * RET_SCALE
    crv_h = _heads(crv, RET_HEADS)
    if ctx_out:
        zeros = jnp.zeros((B, RET_HEADS, RET_DK, RET_DV), jnp.float32)
        ret_c, s_f, s_b = _bidir_retention(_heads(crq, RET_HEADS), crk_h, crv_h, log_gamma, zeros, zeros)
    else:
        s_f = _retention_final_state(crk_h, crv_h, log_gamma[0])
        s_b = _retention_final_state(_flip(crk_h), _flip(crv_h), log_gamma[1])
    rq_h = _apply_rope(_heads(rq, RET_HEADS), *ret_cs)
    rk_h = _apply_rope(_heads(rk, RET_HEADS), *ret_cs) * RET_SCALE
    ret, _, _ = _bidir_retention(rq_h, rk_h, _heads(rv, RET_HEADS), log_gamma, s_f, s_b)
    ret = _ret_out(ret, rg, ret_gn_g)

    q = _apply_rope(_rmsnorm(aq.reshape(B, L, ATT_HEADS, ATT_HD), q_norm_g), *att_cs)
    k = _apply_rope(_rmsnorm(ak.reshape(B, L, ATT_KV_HEADS, ATT_HD), k_norm_g), *att_cs)
    v = av.reshape(B, L, ATT_KV_HEADS, ATT_HD)
    kc = _rmsnorm(cak.reshape(B, Lc, ATT_KV_HEADS, ATT_HD), k_norm_g)
    vc = cav.reshape(B, Lc, ATT_KV_HEADS, ATT_HD)
    att = _latent_attention(q.reshape(B, L, ATT_KV_HEADS, ATT_GROUP, ATT_HD), k, v, kc, vc)

    x = x + g1 * (jnp.concatenate([ret, att], axis=-1) @ w_out)

    h2 = _modulate(_rmsnorm(x, norm2_g), sh2, sc2)
    x = x + g2 * _sqrelu_mlp(h2, w_ff1, w_ff2)

    if ctx_out:
        ret_c = _ret_out(ret_c, crg, ret_gn_g)
        qc = _rmsnorm(caq.reshape(B, Lc, ATT_KV_HEADS, ATT_GROUP, ATT_HD), q_norm_g)
        att_c = _dense_attention(qc, kc, vc).reshape(B, Lc, ATT_W)
        xc = xc + cg1 * (jnp.concatenate([ret_c, att_c], axis=-1) @ w_out)
        hc2 = _modulate(_rmsnorm(xc, norm2_g), csh2, csc2)
        xc = xc + cg2 * _sqrelu_mlp(hc2, w_ff1, w_ff2)
    return x, xc

def second_inputs(seed: int = 0) -> dict:
    key = jax.random.key(seed)
    ks = jax.random.split(key, 17)
    f32 = jnp.float32
    nrm = lambda k, shape, s: jax.random.normal(k, shape, f32) * s
    base_rate = -(5.0 + jnp.arange(RET_HEADS, dtype=f32)) * np.float32(np.log(2.0))
    return {
        "x": nrm(ks[0], (BATCH, SEQ, D_MODEL), 1.0),
        "c": nrm(ks[1], (BATCH, D_MODEL), 1.0),
        "ctx": nrm(ks[2], (BATCH, CTX_LEN, D_MODEL), 1.0),
        "c_ctx": nrm(ks[3], (D_MODEL,), 1.0),
        "w_mod": nrm(ks[4], (DEPTH_2, D_MODEL, 6 * D_MODEL), 0.01),
        "b_mod": nrm(ks[5], (DEPTH_2, 6 * D_MODEL), 0.02),
        "norm1_g": 1.0 + nrm(ks[6], (DEPTH_2, D_MODEL), 0.02),
        "norm2_g": 1.0 + nrm(ks[7], (DEPTH_2, D_MODEL), 0.02),
        "w_in": nrm(ks[8], (DEPTH_2, D_MODEL, D_IN), D_MODEL ** -0.5),
        "w_out": nrm(ks[9], (DEPTH_2, MIX_W, D_MODEL), MIX_W ** -0.5),
        "ret_log_rate": base_rate[None, None, :] + nrm(ks[10], (DEPTH_2, 2, RET_HEADS), 0.05),
        "ret_gn_g": 1.0 + nrm(ks[11], (DEPTH_2, RET_W), 0.02),
        "q_norm_g": 1.0 + nrm(ks[12], (DEPTH_2, ATT_HD), 0.02),
        "k_norm_g": 1.0 + nrm(ks[13], (DEPTH_2, ATT_HD), 0.02),
        "w_ff1": nrm(ks[14], (DEPTH_2, D_MODEL, D_FF), D_MODEL ** -0.5),
        "w_ff2": nrm(ks[15], (DEPTH_2, D_FF, D_MODEL), D_FF ** -0.5),
        "final_norm_g": 1.0 + nrm(ks[16], (D_MODEL,), 0.02),
    }

def second_block(x, c, ctx, c_ctx, w_mod, b_mod, norm1_g, norm2_g, w_in, w_out,
              ret_log_rate, ret_gn_g, q_norm_g, k_norm_g, w_ff1, w_ff2, final_norm_g):
    L = x.shape[1]
    ROWS = L // GRID_W
    t = jnp.arange(L, dtype=jnp.float32)
    ret_ang = t[:, None] * _freqs(RET_DK // 2)
    ret_cs = (jnp.cos(ret_ang), jnp.sin(ret_ang))
    row = jnp.repeat(jnp.arange(ROWS, dtype=jnp.float32), GRID_W)
    col = jnp.tile(jnp.arange(GRID_W, dtype=jnp.float32), ROWS)
    af = _freqs(ATT_HD // 4)
    att_ang = jnp.concatenate([row[:, None] * af, col[:, None] * af], axis=-1)[:, None, :]
    att_cs = (jnp.cos(att_ang), jnp.sin(att_ang))

    c_act = jax.nn.silu(c)
    cc_act = jax.nn.silu(c_ctx)
    xc = ctx
    for l in range(DEPTH_2):
        x, xc = _layer(x, xc, c_act, cc_act, w_mod[l], b_mod[l], norm1_g[l], norm2_g[l],
                       w_in[l], w_out[l], ret_log_rate[l], ret_gn_g[l], q_norm_g[l], k_norm_g[l],
                       w_ff1[l], w_ff2[l], ret_cs, att_cs, l < DEPTH_2 - 1)
    return _rmsnorm(x, final_norm_g)


def setup_inputs(seed=0):
    out = dict(first_inputs(seed))
    for name, value in second_inputs(seed + 1).items():
        if name != "x":
            out[name + "_2"] = value
    return out


def reference(
    x, a_norm, a_w_in, a_conv, a_A_log, a_dt_bias, a_out_norm, a_w_out, kv_norm, w_kv, b_norm,
    b_w_q, b_rel_bias, b_w_out, f_norm, f_w_up, f_conv, f_conv_b, f_w_down, final_norm, c_2,
    ctx_2, c_ctx_2, w_mod_2, b_mod_2, norm1_g_2, norm2_g_2, w_in_2, w_out_2, ret_log_rate_2,
    ret_gn_g_2, q_norm_g_2, k_norm_g_2, w_ff1_2, w_ff2_2, final_norm_g_2,
):
    x = first_block(
        x, a_norm, a_w_in, a_conv, a_A_log, a_dt_bias, a_out_norm, a_w_out, kv_norm, w_kv,
        b_norm, b_w_q, b_rel_bias, b_w_out, f_norm, f_w_up, f_conv, f_conv_b, f_w_down,
        final_norm,
    )
    return second_block(
        x, c_2, ctx_2, c_ctx_2, w_mod_2, b_mod_2, norm1_g_2, norm2_g_2, w_in_2, w_out_2,
        ret_log_rate_2, ret_gn_g_2, q_norm_g_2, k_norm_g_2, w_ff1_2, w_ff2_2, final_norm_g_2,
    )


_drawn_inputs = setup_inputs


def setup_inputs(seed=0):
    import zlib

    import numpy as np

    out = dict(_drawn_inputs(seed))
    spreads = {}
    factors = {'a_out_norm': 4.377,
     'kv_norm': 8.0,
     'b_norm': 8.0,
     'b_rel_bias': 4.945,
     'f_norm': 2.922,
     'f_conv_b': 5.925,
     'final_norm': 2.784,
     'norm1_g_2': 8.0,
     'norm2_g_2': 8.0,
     'ret_gn_g_2': 8.0,
     'q_norm_g_2': 8.0,
     'k_norm_g_2': 8.0,
     'final_norm_g_2': 2.738}
    for name, (base, spread) in spreads.items():
        noise = np.random.default_rng([zlib.crc32(name.encode()), seed]).standard_normal(out[name].shape)
        drawn = base * np.exp(spread * noise) if base else spread * noise
        out[name] = jnp.asarray(drawn.astype(out[name].dtype))
    for name, factor in factors.items():
        out[name] = (out[name] * factor).astype(out[name].dtype)
    return out
```

```python
from contextlib import ExitStack, contextmanager

import numpy as np

import concourse.bass as bass
from concourse import mybir

F32 = mybir.dt.float32
F32R = mybir.dt.float32r
ALU = mybir.AluOpType
ACT = mybir.ActivationFunctionType
AX = mybir.AxisListType.X

P = 128
SEQ = 256
TT = SEQ // P
D = 1024
KD = D // P
EPS = 1e-6
NEG = -1e30

A_HEADS, HK = 8, 128
QKV_TILES = 3 * A_HEADS
A_TAPS = 4
B_HEADS, BH = 16, 64
FF = 2816
F_TILES = FF // P
F_TAPS = 3
RET_H = 4
ATT_H, ATT_KV, ATT_D = 8, 2, 64
FF2_TILES = 4 * D // P
CTX = 256
LEVELS = 6

RAW = 4
SPLIT = 4
BLOCKS = {}
_n = 0
for _name, _count in (("mod", 24), ("qkv", 12), ("z", 4), ("wo_a", 4), ("up0", 22), ("down0", 11),
                      ("k", 4), ("v", 4), ("q", 4), ("wo_b", 4), ("up1", 22), ("down1", 11),
                      ("win", 11), ("wo_c", 4), ("ff1", 16), ("ff2", 16)):
    BLOCKS[_name] = (_n, _count)
    _n += _count
UNITS = 2 * _n
CTX_BLOCKS = (2, 3, 4, 5, 10)
BANK = {}
_e = 0
for _name, (_b, _count) in BLOCKS.items():
    BANK[_name] = _e
    if _name in ("down0", "down1", "ff2"):
        continue
    _e += _count + (len(CTX_BLOCKS) if _name == "win" else 0)
MOD_COL = (0, 1, 2, 3, 4, 5, 6, 7, 12, 13, 14, 15, 16, 17, 18, 19)
for _name in BANK:
    BANK[_name] -= len(MOD_COL) if _name != "mod" else 0

COLS = {}
_c = 0
for _name, _count in (("a_norm", 8), ("kv_norm", 8), ("b_norm", 8), ("f_norm0", 8), ("f_norm1", 8),
                      ("norm1", 8), ("norm2", 8), ("a_conv", A_TAPS * 24), ("f_conv0", F_TAPS * 44),
                      ("f_conv1", F_TAPS * 44), ("f_bias0", 44), ("f_bias1", 44), ("b_mod", 48),
                      ("c", 8), ("c_ctx", 8)):
    COLS[_name] = (_c, _count)
    _c += _count
N_COLS = _c
CONSTS = {}
_c = 0
for _name, _count in (("ident", P), ("ones", P), ("tri", P), ("low", P), ("upT", P), ("join", 7 * P), ("join1T", P)):
    CONSTS[_name] = (_c, _count)
    _c += _count
N_CONSTS = _c
TABLES = {}
_c = 0
for _name, _count in (("fwd", 512), ("bwd", 512), ("ge", 512), ("le", 512), ("pos", 8),
                      ("rcos", 128), ("rsin", 128), ("acos", 64), ("asin", 64)):
    TABLES[_name] = (_c, _count)
    _c += _count
N_TABLES = _c
ROWS_A = (("out_norm", 128), ("A_log", 8), ("dt_bias", 8), ("rate", 8))
ROWS_C = (("final1", 1024), ("gn", 512), ("qn", 64), ("kn", 64), ("final2", 1024))



STAGED = {}
_s = 0
for _name in ("qkv", "wo_a", "up0", "wo_b", "up1", "wo_c", "ff1"):
    STAGED[_name] = _s
    _s += BLOCKS[_name][1]
STAT = {n: i for i, n in enumerate(("a", "f0", "kv", "f1", "x2", "ctx", "n1", "n2", "fin"))}
TURN = {n: i for i, n in enumerate(("a", "f0", "kv", "f1", "ctx", "n1", "n2"))}
SCALED = {n: i for i, n in enumerate(("a", "f0", "kv", "q", "f1", "ctx", "n1", "n2"))}
RES = {"down0": 4, "down1": 8, "x2": 10, "ff2": 14, "fin": 16}
PRODS = {"down0": 0, "down1": 22}
ACTS = {"down0": 0, "down1": 22, "ff2": 44}
AUX = 4


class Steps:

    def __init__(self, eng, sem):
        self.eng, self.sem, self.n, self.base = eng, sem, 0, 0

    def put(self, ins):
        ins.then_inc(self.sem, 1)
        self.n += 1
        return self.n

    def wait(self, n):
        self.eng.wait_ge(self.sem, self.base + n)

    def do(self, ins):
        self.wait(self.put(ins))

    @contextmanager
    def loop(self, i, turns, each):
        first = self.n
        self.base = i * each
        yield
        assert self.n - first == each, (self.n - first, each)
        self.base = 0
        self.n = first + turns * each


def turns(eng, count, body, steps=None, each=0):
    head = count % 4 or 4
    for j in range(head):
        body(0, j)
    n = (count - head) // 4
    if n == 0:
        return
    if n == 1:
        for j in range(4):
            body(0, head + j)
        return
    with eng.Fori(0, n) as i:
        if steps is None:
            for j in range(4):
                body(i, head + j)
        else:
            with steps.loop(i, n, 4 * each):
                for j in range(4):
                    body(i, head + j)


def one(m):
    return bass.ds(m, 1)


def build(nc, a, out, stop=None):
    with ExitStack() as ctx:
        def sb(name, shape, dt=F32, where=ctx):
            return where.enter_context(nc.sbuf_tensor(name, shape, dt))

        def sem(name):
            return ctx.enter_context(nc.semaphore(name))

        raw = sb("raw", [P, RAW, 1024])
        wH = sb("wH", [P, SPLIT, 1024], F32R)
        wL = sb("wL", [P, SPLIT, 1024], F32R)
        h = sb("h", [P, TT, D])
        xH = sb("xH", [P, KD, SEQ], F32R)
        xL = sb("xL", [P, KD, SEQ], F32R)
        cols = sb("cols", [P, N_COLS])
        cst = sb("cst", [P, N_CONSTS])
        rows_a = sb("rows_a", [P, 152])
        stage = sb("stage", [P, 2, 2, SEQ])
        cv = sb("cv", [P, 2, 2, SEQ])
        gate1 = sb("gate1", [P, D])
        gate2 = sb("gate2", [P, D])
        modc = sb("modc", [P, 32, 2])
        gs1 = sb("gs1", [P, KD, 2])
        gs2 = sb("gs2", [P, KD])
        ssq = sb("ssq", [P, TT])
        msq = sb("msq", [P, TT])
        rstd = sb("rstd", [P, TT])
        mhalf = sb("mhalf", [P, 32])
        lg = sb("lg", [P, 8])

        with ExitStack() as s:
            xn = sb("xn", [P, TT, D], where=s)
            xv = sb("xv", [P, KD, SEQ], where=s)
            ctx_in = sb("ctx_in", [P, TT, D], where=s)
            row_f1 = sb("row_f1", [P, D], where=s)
            xcH = sb("xcH", [P, KD, SEQ], F32R, where=s)
            xcL = sb("xcL", [P, KD, SEQ], F32R, where=s)
            qk_t = sb("qk_t", [P, TT, D], where=s)
            rv = sb("rv", [P, TT, 512], where=s)
            sg = sb("sg", [P, TT, 512], where=s)
            aqkv = sb("aqkv", [P, TT, 768], where=s)
            tb = sb("tb", [P, N_TABLES], where=s)
            rows_c = sb("rows_c", [P, 640], where=s)
        with ExitStack() as s:
            cakv = sb("cakv", [P, TT, 256], where=s)
            ckv = sb("ckv", [P, TT, D], where=s)
            rope = sb("rope", [P, TT, D], where=s)
            rqT = sb("rqT", [P, RET_H, SEQ], where=s)
            rkT = sb("rkT", [P, RET_H, SEQ], where=s)
            wt = sb("wt", [P, 2, 512], where=s)
            sT = sb("sT", [P, 2, 512], where=s)
            o_r = sb("o_r", [P, TT, RET_H, P], where=s)
            s_fb = sb("s_fb", [P, 2, RET_H, P], where=s)
            dec = sb("dec", [P, 4, TT, RET_H], where=s)
            st_r = sb("st_r", [P, 4, 8], where=s)
        with ExitStack() as s:
            sb("pad_att", [P, TT, 256], where=s)
            aqn = sb("aqn", [P, TT, 10, ATT_D], where=s)
            kcn = sb("kcn", [P, TT, 2, ATT_D], where=s)
            rt = sb("rt", [P, 4, 10, 32], where=s)
            asq = sb("asq", [P, 12, ATT_D], where=s)
            aqT = sb("aqT", [P, 4, SEQ], where=s)
            akT = sb("akT", [P, 512], where=s)
            ap_ = sb("ap_", [P, 2, TT, 512], where=s)
            apT = sb("apT", [P, 2, 4, SEQ], where=s)
            st_a = sb("st_a", [P, TT, 2, 12], where=s)
            st_p = sb("st_p", [P, 3, 4], where=s)
        with ExitStack() as s:
            sb("pad_m", [P, 2 * TT * D], where=s)
            bmrow = sb("bmrow", [P, 2048], where=s)
            cact = sb("cact", [P, 2, KD], where=s)
            cpH = sb("cpH", [P, KD, 2], F32R, where=s)
            cpL = sb("cpL", [P, KD, 2], F32R, where=s)
            crH = sb("crH", [P, KD, P], F32R, where=s)
            crL = sb("crL", [P, KD, P], F32R, where=s)
            baw = sb("baw", [P, KD, 16], where=s)
            baH = sb("baH", [P, KD, 16], F32R, where=s)
            baL = sb("baL", [P, KD, 16], F32R, where=s)
        with ExitStack() as s:
            tok = sb("tok", [P, TT, QKV_TILES, HK], where=s)
            feat = sb("feat", [P, QKV_TILES, SEQ], where=s)
            T_ = sb("T_", [P, 16, P], where=s)
            MT = sb("MT", [P, 16, P], where=s)
            U_ = sb("U_", [P, 16, P], where=s)
            AT = sb("AT", [P, 16, P], where=s)
            zs = sb("zs", [P, TT, D], where=s)
            sm = sb("sm", [P, 24, 24], where=s)
            r32 = sb("r32", [P, 3, 32], where=s)
        P_ = feat[:, 16:24, :].rearrange("p a (b c) -> p (a b) c", b=2)
        dG = stage[:, 0].rearrange("p a (b c) -> p (a b) c", b=2)
        dT = stage[:, 1].rearrange("p a (b c) -> p (a b) c", b=2)
        dS = cv[:, 0].rearrange("p a (b c) -> p (a b) c", b=2)
        dQ = cv[:, 1].rearrange("p a (b c) -> p (a b) c", b=2)
        with ExitStack() as s:
            act_a = sb("act_a", [P, FF2_TILES, SEQ], where=s)
            aH = sb("aH", [P, SPLIT, SEQ], F32R, where=s)
            aL = sb("aL", [P, SPLIT, SEQ], F32R, where=s)
            rows_f = sb("rows_f", [P, D], where=s)
        with ExitStack() as s:
            p_b = sb("p_b", [P, 2, 4, 384], where=s)
            pT_b = sb("pT_b", [P, 2, 4, 384], where=s)
            kT = sb("kT", [P, KD, SEQ], where=s)
            qT = sb("qT", [P, KD, SEQ], where=s)
            vt = sb("vt", [P, TT, D], where=s)
            x2H = sb("x2H", [P, KD, SEQ], F32R, where=s)
            x2L = sb("x2L", [P, KD, SEQ], F32R, where=s)
            slab = sb("slab", [P, B_HEADS, SEQ], where=s)
            st_b = sb("st_b", [P, 2, 3, 8], where=s)

        ps = [ctx.enter_context(nc.psum_tensor(f"ps{b}", [P, 512], F32)) for b in range(8)]

        x_in = sem("x_in")
        consts_in = sem("consts_in")
        slab_in = sem("slab_in")
        slab_masked = sem("slab_masked")
        early_in = sem("early_in")
        late_in = sem("late_in")
        final_in = sem("final_in")
        unit_in = [sem(f"unit_in{i}") for i in range(RAW)]
        hi_done = sem("hi_done")
        lo_done = sem("lo_done")
        unit_done = sem("unit_done")
        bank_free = sem("bank_free")
        unstaged = sem("unstaged")
        silu_done = sem("silu_done")
        prod_done = sem("prod_done")
        a_hi = sem("a_hi")
        a_lo = sem("a_lo")
        sq_done = sem("sq_done")
        ms_done = sem("ms_done")
        rstd_done = sem("rstd_done")
        xn_done = sem("xn_done")
        turned = sem("turned")
        val_dve = sem("val_dve")
        x_hi = sem("x_hi")
        x_ready = sem("x_ready")
        res_done = sem("res_done")
        act_s = sem("act_s")
        dve_s = sem("dve_s")
        pool_s = sem("pool_s")
        c_ready = sem("c_ready")
        mod_done = sem("mod_done")
        mod_ready = sem("mod_ready")
        out_done = sem("out_done")
        g_act = sem("g_act")
        g_dve = sem("g_dve")
        g_sum = sem("g_sum")
        tok_pe = sem("tok_pe")
        tok_act = sem("tok_act")
        tok_dve = sem("tok_dve")
        tok_sq = sem("tok_sq")
        unit_qk = sem("unit_qk")
        back_pe = sem("back_pe")
        back_act = sem("back_act")
        back_dve = sem("back_dve")
        dg_dve = sem("dg_dve")
        row_pe = sem("row_pe")
        arg_dve = sem("arg_dve")
        exp_act = sem("exp_act")
        kq_pe = sem("kq_pe")
        m_dve = sem("m_dve")
        at_dve = sem("at_dve")
        mt_pe = sem("mt_pe")
        mt_act = sem("mt_act")
        dbl_pe = sem("dbl_pe")
        dbl_dve = sem("dbl_dve")
        scan_pe = sem("scan_pe")
        scan_act = sem("scan_act")
        scan_dve = sem("scan_dve")
        pw_in = sem("pw_in")
        pw_out = sem("pw_out")
        y_rows = sem("y_rows")
        y_pe = sem("y_pe")
        y_hi = sem("y_hi")
        y_ready = sem("y_ready")
        b_score = sem("b_score")
        b_max = sem("b_max")
        b_exp = sem("b_exp")
        b_prob = sem("b_prob")
        b_turn = sem("b_turn")
        b_tact = sem("b_tact")
        b_tdve = sem("b_tdve")
        m_dec = sem("m_dec")
        m_ck = sem("m_ck")
        m_state = sem("m_state")
        m_sact = sem("m_sact")
        m_rope = sem("m_rope")
        m_turn = sem("m_turn")
        m_tact = sem("m_tact")
        m_tdve = sem("m_tdve")
        m_w = sem("m_w")
        m_wd = sem("m_wd")
        m_s = sem("m_s")
        m_sd = sem("m_sd")
        m_o = sem("m_o")
        m_od = sem("m_od")
        q_rope = sem("q_rope")
        q_turn = sem("q_turn")
        q_tact = sem("q_tact")
        s_pe = sem("s_pe")
        s_max = sem("s_max")
        s_exp = sem("s_exp")
        s_prob = sem("s_prob")
        s_turn = sem("s_turn")
        s_tact = sem("s_tact")
        s_tdve = sem("s_tdve")

        def U(name):
            return 2 * BLOCKS[name][0]

        block = ctx.enter_context(nc.Block())
        K_ = {n: cst[:, o:o + c] for n, (o, c) in CONSTS.items()}
        ident = K_["ident"]

        def col(name, k, n=1):
            return cols[:, COLS[name][0] + k:COLS[name][0] + k + n]

        @block.sync
        def _(sp):
            def unit(i, per, c, src, kk):
                if not (isinstance(i, int) and c < RAW):
                    sp.wait_ge(lo_done, i * per + (c - RAW + 1))
                dst = raw[:, c % RAW]
                if kk > 1:
                    dst = dst.rearrange("p (k n) -> p k n", k=kk)
                sp.dma_start(dst, src).then_inc(unit_in[c % RAW], 16)

            def feature_major(name, w, at):
                wk = w.rearrange("(k p) n -> p k n", p=P)

                def body(i, j):
                    for f in range(2):
                        unit(i, 8, U(name) + 2 * j + f, wk[:, :, bass.ds(at(i * 4 + j, f), P)], KD)
                turns(sp, BLOCKS[name][1], body)

            def token_major(name, w, c0):
                wk = w.rearrange("(k p) n -> p k n", p=P)

                def body(i, j):
                    for g in range(2):
                        unit(i, 8, U(name) + 2 * j + g,
                             wk[:, 4 * g:4 * g + 4, bass.ds((i * 4 + j) * 256 + c0, 256)], 4)
                turns(sp, BLOCKS[name][1], body)

            def rows_of(name, w):
                wk = w.rearrange("(k p) n -> k p n", p=P)

                def body(i, j):
                    unit(i, 4, U(name) + j,
                         wk[one(i * 4 + j)].rearrange("a p n -> p (a n)"), 1)
                turns(sp, 2 * BLOCKS[name][1], body)

            def dump(which, n):
                sp.wait_ge(which, n)
                sp.dma_start(out.rearrange("o (t p) d -> p (o t) d", p=P), h[:]).then_inc(out_done, 16)
                sp.wait_ge(out_done, 16)

            sp.dma_start(h[:], a["x"].rearrange("o (t p) d -> p (o t) d", p=P)).then_inc(x_in, 16)
            w_mod = a["w_mod_2"][0]
            wk = w_mod.rearrange("(k p) n -> p k n", p=P)
            for m in range(24):
                for f in range(2):
                    if m in MOD_COL:
                        unit(0, 0, 2 * m + f, wk[:, :, m * 256 + f * P:m * 256 + (f + 1) * P], KD)
                    else:
                        unit(0, 0, 2 * m + f, wk[:, 4 * f:4 * f + 4, m * 256:(m + 1) * 256], 4)
            feature_major("qkv", a["a_w_in"][0], lambda m, f: m * 256 + f * P)
            token_major("z", a["a_w_in"][0], 3 * D)
            token_major("wo_a", a["a_w_out"][0], 0)
            if stop == "wo_a":
                return dump(unstaged, STAGED["wo_a"] + 4)
            feature_major("up0", a["f_w_up"][0], lambda m, f: m * P + f * FF)
            rows_of("down0", a["f_w_down"][0])
            if stop == "down0":
                return dump(res_done, 4)
            feature_major("k", a["w_kv"], lambda m, f: m * 256 + f * P)
            token_major("v", a["w_kv"], D)
            feature_major("q", a["b_w_q"][0], lambda m, f: m * 256 + f * P)
            token_major("wo_b", a["b_w_out"][0], 0)
            if stop == "wo_b":
                return dump(unstaged, STAGED["wo_b"] + 4)
            feature_major("up1", a["f_w_up"][1], lambda m, f: m * P + f * FF)
            rows_of("down1", a["f_w_down"][1])
            if stop == "down1":
                return dump(res_done, 8)
            token_major("win", a["w_in_2"][0], 0)
            token_major("wo_c", a["w_out_2"][0], 0)
            if stop == "wo_c":
                return dump(unstaged, STAGED["wo_c"] + 4)
            feature_major("ff1", a["w_ff1_2"][0], lambda m, f: m * 256 + f * P)
            rows_of("ff2", a["w_ff2_2"][0])
            dump(res_done, RES["fin"])

        @block.tensor
        def _(pe):
            mm = nc.tensor.matmul

            def three(o, l, r, first, last, check=False):
                mm(o, l[0], r[0], start=first, stop=False, skip_group_check=check)
                mm(o, l[0], r[1], start=False, stop=False, skip_group_check=check)
                return mm(o, l[1], r[0], start=False, stop=last, skip_group_check=check)

            def bank(name, i, j):
                e = BANK[name] + j
                if not (isinstance(i, int) and e < 4):
                    pe.wait_ge(bank_free, i * 4 + (e - 3))
                return ps[e % 4]

            def w_unit(i, per, c):
                pe.wait_ge(lo_done, i * per + (c + 1))
                return [w[:, c % SPLIT] for w in (wH, wL)]

            def feature_major(name, x):
                def body(i, j):
                    b = bank(name, i, j)
                    for f in range(2):
                        w = [y.rearrange("p (k n) -> p k n", k=KD) for y in w_unit(i, 8, U(name) + 2 * j + f)]
                        for k in range(KD):
                            last = three(b[:, f * SEQ:(f + 1) * SEQ], [y[:, k] for y in w],
                                         [y[:, k] for y in x], k == 0, k == KD - 1)
                        last.then_inc(unit_done, 1)
                turns(pe, BLOCKS[name][1], body)

            def token_block(banks, i, c, xs):
                for g in range(2):
                    w = [y.rearrange("p (k n) -> p k n", k=4) for y in w_unit(i, 8, c + g)]
                    for b, x in zip(banks, xs):
                        for t in range(TT):
                            for k in range(4):
                                last = three(b[:, t * 256:(t + 1) * 256],
                                             [y[:, 4 * g + k, t * P:(t + 1) * P] for y in x],
                                             [y[:, k] for y in w], g == 0 and t == 0 and k == 0,
                                             g == 1 and k == 3, check=True)
                    last.then_inc(unit_done, 1)

            def token_major(name, x):
                turns(pe, BLOCKS[name][1],
                      lambda i, j: token_block([bank(name, i, j)], i, U(name) + 2 * j, [x]))

            def down(name, count):
                acc = [ps[AUX + 2 * t + c] for t in range(TT) for c in range(2)]

                def body(i, j):
                    w = w_unit(i, 4, U(name) + j)
                    pe.wait_ge(a_lo, i * 4 + (ACTS[name] + j + 1))
                    first, last = isinstance(i, int) and j == 0, isinstance(i, int) and j == count - 1
                    for t in range(TT):
                        for c in range(2):
                            done = three(acc[2 * t + c][:], [y[:, j % SPLIT, t * P:(t + 1) * P] for y in (aH, aL)],
                                         [y[:, c * 512:(c + 1) * 512] for y in w], first, last, check=True)
                    done.then_inc(unit_done, 1)
                turns(pe, count, body)

            def turn_rows(n):
                for t in range(TT):
                    pe.wait_ge(xn_done, 2 * TURN[n] + t + 1)
                    for k in range(KD):
                        o = (k % 2) * SEQ + t * P
                        tr = nc.tensor.transpose(ps[AUX + k // 2][:, o:o + P], xn[:, t, k * P:(k + 1) * P], ident)
                        if t == 1 and k % 2:
                            tr.then_inc(turned, 1)

            def ready(n):
                pe.wait_ge(x_ready, 2 * SCALED[n] + 2)


            def delta_pe():
                pe.wait_ge(g_dve, 4)
                for t in range(TT):
                    mm(ps[7][:, 8 * t:8 * t + 8], K_["tri"], sm[:, 10, 8 * t:8 * t + 8], start=True, stop=True)
                mm(ps[7][:, 16:24], K_["ones"], sm[:, 10, 0:8], start=True, stop=True).then_inc(g_sum, 1)
                pe.wait_ge(silu_done, 12)
                for q in range(12):
                    t, f0 = q // 6, 4 * (q % 6)
                    if q == 3:
                        pe.wait_ge(g_dve, 5)
                    if q >= 4:
                        pe.wait_ge((tok_act, tok_dve)[q % 2], q // 2 - 1)
                    for f in range(4):
                        tr = nc.tensor.transpose(ps[AUX + q % 4][:, f * P:(f + 1) * P],
                                                 feat[:, f0 + f, t * P:(t + 1) * P], ident)
                    tr.then_inc(tok_pe, 1)
                pe.wait_ge(tok_act, 6)
                pe.wait_ge(tok_dve, 6)
                pe.wait_ge(unit_qk, 2)
                for q in range(8):
                    if q >= 4:
                        pe.wait_ge((back_act, back_dve)[q % 2], q // 2 - 1)
                    for f in range(2):
                        for t in range(TT):
                            tr = nc.tensor.transpose(ps[AUX + q % 4][:, f * SEQ + t * P:f * SEQ + (t + 1) * P],
                                                     tok[:, t, 2 * q + f], ident)
                    tr.then_inc(back_pe, 1)
                pe.wait_ge(back_act, 4)
                pe.wait_ge(back_dve, 4)
                for g in range(4):
                    t, h0 = g // 2, 4 * (g % 2)
                    pe.wait_ge(dg_dve, g + 1)
                    mm(ps[4][:], K_["ones"], dG.rearrange("p a b -> p (a b)"), start=True, stop=True).then_inc(row_pe, 1)
                    if g:
                        pe.wait_ge(m_dve, g)
                        pe.wait_ge(at_dve, g)
                    for x in range(4):
                        k = feat[:, 8 + h0 + x, t * P:(t + 1) * P]
                        mm(ps[5][:, x * P:(x + 1) * P], k, k, start=True, stop=True)
                        last = mm(ps[6][:, x * P:(x + 1) * P], k, feat[:, h0 + x, t * P:(t + 1) * P], start=True, stop=True)
                    last.then_inc(kq_pe, 1)
                    pe.wait_ge(m_dve, g + 1)
                    if g:
                        pe.wait_ge(mt_act, g)
                    for x in range(4):
                        tr = nc.tensor.transpose(ps[7][:, x * P:(x + 1) * P], T_[:, 4 * g + x], ident)
                    tr.then_inc(mt_pe, 1)

                def join(i, l):
                    for step in range(3):
                        for g in range(4):
                            k = l * 12 + step * 4 + g
                            pe.wait_ge(dbl_dve, i * 12 + (k - 2 if k > 3 else 1))
                            for x in range(4 * g, 4 * g + 4):
                                lhs, rhs = ((MT, T_), (U_, P_), (P_, U_))[step]
                                last = mm(ps[AUX + g][:, (x % 4) * P:(x % 4 + 1) * P], lhs[:, x], rhs[:, x],
                                          start=True, stop=True)
                            last.then_inc(dbl_pe, 1)
                join(0, 0)
                with pe.Fori(0, LEVELS - 1) as i:
                    join(i, 1)

                def heads(bank, lhs, rhs):
                    for hb in range(2):
                        for x in range(4):
                            n = 4 * hb + x
                            last = mm(ps[bank + hb][:, x * P:(x + 1) * P], lhs(n), rhs(n), start=True, stop=True)
                        last.then_inc(scan_pe, 1)
                pe.wait_ge(dbl_dve, 1 + 12 * LEVELS)
                pe.wait_ge(scan_dve, 1)
                heads(4, lambda n: U_[:, n], lambda n: tok[:, 0, 16 + n])
                pe.wait_ge(scan_act, 2)
                pe.wait_ge(scan_dve, 2)
                heads(6, lambda n: tok[:, 0, 8 + n], lambda n: P_[:, n])
                pe.wait_ge(scan_act, 4)
                heads(4, lambda n: feat[:, 8 + n, P:2 * P], lambda n: T_[:, n])
                heads(6, lambda n: feat[:, n, P:2 * P], lambda n: T_[:, n])
                pe.wait_ge(scan_dve, 4)
                heads(4, lambda n: AT[:, n], lambda n: P_[:, n])
                pe.wait_ge(scan_dve, 7)
                heads(6, lambda n: U_[:, 8 + n], lambda n: T_[:, 8 + n])
                pe.wait_ge(scan_act, 8)
                heads(4, lambda n: AT[:, 8 + n], lambda n: P_[:, 8 + n])
                pe.wait_ge(scan_act, 8)
                pe.wait_ge(y_rows, 1)
                for b in range(4):
                    for k in range(2 * b, 2 * b + 2):
                        for t in range(TT):
                            o = (k % 2) * SEQ + t * P
                            tr = nc.tensor.transpose(ps[AUX + b][:, o:o + P], tok[:, t, k], ident)
                    tr.then_inc(y_pe, 1)

            def band_pe():
                pe.wait_ge(bank_free, BANK["q"] + 4)
                pe.wait_ge(slab_masked, 1)

                def scores(g):
                    if g:
                        pe.wait_ge(b_max, g)
                    for x in range(4):
                        n, r, o = 4 * g + x, 64 * (x % 2), x // 2
                        q, k = qT[r:r + 64, n // 2], kT[r:r + 64, n // 2]
                        mm(ps[4 + x % 2][:, o * 256:(o + 1) * 256], q[:, P:], k, start=True, stop=True)
                        last = mm(ps[6 + x % 2][:, o * P:(o + 1) * P], q[:, 0:P], k[:, 0:P], start=True, stop=True)
                    last.then_inc(b_score, 1)
                scores(0)
                for g in range(4):
                    if g < 3:
                        scores(g + 1)
                    pe.wait_ge(b_prob, g + 1)
                    if g:
                        pe.wait_ge(y_ready, 4 + g)
                    for x in range(4):
                        for o, c in ((0, 256), (P, 0), (2 * P, P)):
                            tr = nc.tensor.transpose(ps[x][:, o:o + P], p_b[:, g % 2, x, c:c + P], ident)
                        tr.then_inc(b_turn, 1)
                    pe.wait_ge(b_tact, 2 * g + 2)
                    pe.wait_ge(b_tdve, 2 * g + 2)
                    for x in range(4):
                        n, r, o = 4 * g + x, 64 * (x % 2), (x // 2) * SEQ
                        mm(ps[0][r:r + 64, o:o + SEQ], vt[:, 0, n * BH:(n + 1) * BH], pT_b[:, g % 2, x, 0:256],
                           start=True, stop=False)
                        last = mm(ps[0][r:r + 64, o + P:o + SEQ], vt[:, 1, n * BH:(n + 1) * BH],
                                  pT_b[:, g % 2, x, 256:384], start=False, stop=True)
                    last.then_inc(y_pe, 1)

            def mix_pe():
                pe.wait_ge(m_ck, 4)
                pe.wait_ge(bank_free, BANK["wo_c"])
                for d in range(2):
                    for n in range(RET_H):
                        for t in range(TT):
                            last = mm(ps[4 + d][:, n * P:(n + 1) * P], rope[:, t, d * 512 + n * P:d * 512 + (n + 1) * P],
                                      ckv[:, t, 512 + n * P:512 + (n + 1) * P], start=t == 0, stop=t == 1)
                    last.then_inc(m_state, 1)
                pe.wait_ge(m_sact, 2)
                pe.wait_ge(m_rope, 2)
                for b in range(4):
                    for f in range(2):
                        for t in range(TT):
                            o = f * SEQ + t * P
                            tr = nc.tensor.transpose(ps[AUX + b][:, o:o + P],
                                                     rope[:, t, (2 * b + f) * P:(2 * b + f + 1) * P], ident)
                    tr.then_inc(m_turn, 1)
                pe.wait_ge(m_tact, 2)
                pe.wait_ge(m_tdve, 2)
                for n in range(RET_H):
                    for j in range(TT):
                        last = mm(ps[4][:, j * SEQ:(j + 1) * SEQ], rkT[:, n, j * P:(j + 1) * P], rqT[:, n],
                                  start=True, stop=True)
                    last.then_inc(m_s, 1)
                    pe.wait_ge(m_sd, n + 1)
                    if n:
                        pe.wait_ge(m_od, n)
                    for t in range(TT):
                        for j in range(TT):
                            mm(ps[6][:, t * P:(t + 1) * P], sT[:, n % 2, j * SEQ + t * P:j * SEQ + (t + 1) * P],
                               rv[:, j, n * P:(n + 1) * P], start=j == 0, stop=j == 1)
                    for d in range(2):
                        for t in range(TT):
                            o = ps[6 + d][:, 256 * (1 - d) + t * P:256 * (1 - d) + (t + 1) * P]
                            last = mm(o, rqT[:, n, t * P:(t + 1) * P], s_fb[:, d, n], start=True, stop=True)
                    last.then_inc(m_o, 1)
                pe.wait_ge(y_rows, 2)
                for b in range(2):
                    for f in range(2):
                        for t in range(TT):
                            o = f * SEQ + t * P
                            tr = nc.tensor.transpose(ps[4 + b][:, o:o + P], o_r[:, t, 2 * b + f], ident)
                    tr.then_inc(y_pe, 1)
                pe.wait_ge(q_rope, 2)
                pe.wait_ge(y_ready, 10)
                for b in range(2):
                    for f in range(2):
                        for t in range(TT):
                            o = f * SEQ + t * P
                            w = 2 * (2 * b + f)
                            tr = nc.tensor.transpose(ps[4 + b][:, o:o + P], aqn[:, t, w:w + 2].rearrange("p a b -> p (a b)"), ident)
                    tr.then_inc(q_turn, 1)
                for t in range(TT):
                    nc.tensor.transpose(ps[6][:, t * P:(t + 1) * P], kcn[:, t].rearrange("p a b -> p (a b)"), ident)
                    tr = nc.tensor.transpose(ps[6][:, SEQ + t * P:SEQ + (t + 1) * P],
                                             aqn[:, t, 8:10].rearrange("p a b -> p (a b)"), ident)
                tr.then_inc(q_turn, 1)
                pe.wait_ge(q_tact, 3)

                def scores(j):
                    if j:
                        pe.wait_ge(s_exp, 4 * j)
                    for s in range(2):
                        for t in range(TT):
                            mm(ps[4 + 2 * s + t][:], aqT[64 * s:64 * s + 64, j, t * P:(t + 1) * P],
                               akT[64 * s:64 * s + 64], start=True, stop=True).then_inc(s_pe, 1)
                scores(0)
                for j in range(4):
                    pe.wait_ge(s_prob, 4 * j + 4)
                    if j < 3:
                        scores(j + 1)
                    if j:
                        pe.wait_ge(y_ready, 10 + j)
                    for s in range(2):
                        for kp in range(2):
                            for k in range(2):
                                for t in range(TT):
                                    o, c = k * SEQ + t * P, (2 * kp + k) * P
                                    tr = nc.tensor.transpose(ps[2 * s + kp][:, o:o + P], ap_[:, s, t, c:c + P], ident)
                            tr.then_inc(s_turn, 1)
                    pe.wait_ge(s_tact, 2 * j + 2)
                    pe.wait_ge(s_tdve, 2 * j + 2)
                    r = 64 * (j % 2)
                    for s in range(2):
                        for k in range(4):
                            v = (cakv[:, k, P + 64 * s:P + 64 * s + 64] if k < 2
                                 else aqkv[:, k - 2, 640 + 64 * s:704 + 64 * s])
                            last = mm(ps[0][r:r + 64, s * SEQ:(s + 1) * SEQ], v, apT[:, s, k], start=k == 0, stop=k == 3)
                    last.then_inc(y_pe, 1)

            X = [xH, xL]
            pe.wait_ge(consts_in, 48)
            turn_rows("a")
            ready("a")
            pe.wait_ge(c_ready, 1)
            tiles = 0
            for m in range(24):
                if m in MOD_COL:
                    for f in range(2):
                        w = [y.rearrange("p (k n) -> p k n", k=KD) for y in w_unit(0, 0, 2 * m + f)]
                        for k in range(KD):
                            last = three(ps[AUX][:, 2 * tiles:2 * tiles + 2], [y[:, k] for y in w],
                                         [cpH[:, k], cpL[:, k]], k == 0, k == KD - 1)
                        last.then_inc(unit_done, 1)
                        tiles += 1
                else:
                    e = m - 8 if m < 12 else m - 16
                    if e >= 4:
                        pe.wait_ge(bank_free, e - 3)
                    for g in range(2):
                        w = [y.rearrange("p (k n) -> p k n", k=4) for y in w_unit(0, 0, 2 * m + g)]
                        for k in range(4):
                            last = three(ps[e % 4][:, 0:256], [crH[:, 4 * g + k], crL[:, 4 * g + k]],
                                         [y[:, k] for y in w], g == 0 and k == 0, g == 1 and k == 3)
                        last.then_inc(unit_done, 1)
            for t in range(TT):
                for k in range(KD):
                    last = three(ps[AUX + 1][:, 16 * t:16 * t + 16], [y[:, k, t * P:(t + 1) * P] for y in X],
                                 [baH[:, k], baL[:, k]], k == 0, k == KD - 1)
            last.then_inc(mod_done, 1)
            if stop == "mod":
                return
            feature_major("qkv", X)
            token_major("z", X)
            delta_pe()
            pe.wait_ge(y_ready, 4)
            token_major("wo_a", X)
            if stop == "wo_a":
                return
            turn_rows("f0")
            ready("f0")
            feature_major("up0", X)
            down("down0", F_TILES)
            if stop == "down0":
                return
            turn_rows("kv")
            ready("kv")
            feature_major("k", X)
            token_major("v", X)
            ready("q")
            feature_major("q", [x2H, x2L])
            band_pe()
            pe.wait_ge(y_ready, 8)
            token_major("wo_b", X)
            if stop == "wo_b":
                return
            turn_rows("f1")
            ready("f1")
            feature_major("up1", X)
            down("down1", F_TILES)
            if stop == "down1":
                return
            turn_rows("ctx")
            ready("ctx")
            turn_rows("n1")
            ready("n1")
            e = BANK["win"]
            for m in range(11):
                xs = [X, [xcH, xcL]] if m in CTX_BLOCKS else [X]
                pe.wait_ge(bank_free, e + len(xs) - 4)
                token_block([ps[(e + y) % 4] for y in range(len(xs))], 0, U("win") + 2 * m, xs)
                e += len(xs)
            mix_pe()
            pe.wait_ge(y_ready, 8 + 2 + 4)
            token_major("wo_c", X)
            if stop == "wo_c":
                return
            turn_rows("n2")
            ready("n2")
            feature_major("ff1", X)
            down("ff2", FF2_TILES)

        @block.scalar
        def _(act):
            st = Steps(act, act_s)
            fn = nc.scalar.activation

            def hi(i, per, c):
                if isinstance(i, int) and c >= UNITS:
                    return
                act.wait_ge(unit_in[c % RAW], i * (16 * per // RAW) + 16 * (c // RAW + 1))
                if not (isinstance(i, int) and c < SPLIT):
                    act.wait_ge(unit_done, i * per + (c - SPLIT + 1))
                fn(wH[:, c % SPLIT], raw[:, c % RAW], ACT.Copy).then_inc(hi_done, 1)

            def ahead(i, c):
                hi(i, 8, c + SPLIT)
                hi(i, 8, c + SPLIT + 1)

            def blocks(name, evacuate, after=None):
                def body(i, j):
                    act.wait_ge(unit_done, i * 8 + (U(name) + 2 * j + 2))
                    evacuate(i, j, ps[(BANK[name] + j) % 4]).then_inc(bank_free, 1)
                    ahead(i, U(name) + 2 * j)
                    if after:
                        after(i, j)
                turns(act, BLOCKS[name][1], body)

            def staging(name, func=ACT.Copy, after=None):
                def body(i, j):
                    n = STAGED[name] + j
                    act.wait_ge(unit_done, i * 8 + (U(name) + 2 * j + 2))
                    if not (isinstance(i, int) and n < 2):
                        act.wait_ge(unstaged, i * 4 + (n - 1))
                    b = ps[(BANK[name] + j) % 4]
                    fn(stage[:, n % 2].rearrange("p a b -> p (a b)"), b[:], func).then_inc(bank_free, 1)
                    ahead(i, U(name) + 2 * j)
                    if after:
                        after(i, j)
                turns(act, BLOCKS[name][1], body)

            def down(name, count):
                def part(i, j):
                    m = j + SPLIT
                    act.wait_ge(unit_done, i * 4 + (U(name) + j + 1))
                    fn(aH[:, m % SPLIT], act_a[:, one(i * 4 + m)].rearrange("p a n -> p (a n)"),
                       ACT.Copy).then_inc(a_hi, 1)

                def body(i, j):
                    hi(i, 4, U(name) + j + SPLIT)
                    part(i, j)
                def made(m):
                    if name == "ff2":
                        act.wait_ge(unstaged, STAGED["ff1"] + m // 2 + 1)
                    else:
                        act.wait_ge(prod_done, PRODS[name] + m + 1)
                for m in range(SPLIT):
                    made(m)
                    fn(aH[:, m], act_a[:, m], ACT.Copy).then_inc(a_hi, 1)
                made(count - 1)
                turns(act, count - SPLIT, body)
                for j in range(count - SPLIT, count):
                    hi(0, 4, U(name) + j + SPLIT)

            def squares(n, src):
                for t in range(TT):
                    fn(xn[:, t], src[:, t], ACT.Square, accum_out=ssq[:, t:t + 1]).then_inc(sq_done, 1)

            def scaled(n, turn, gain, bias, oH):
                e = SCALED[n]
                act.wait_ge(turned, 4 * TURN[turn] + 2)
                if e:
                    act.wait_ge(x_ready, 2 * e)
                for k in range(4):
                    s = st.put(fn(xv[:, k], ps[AUX + k // 2][:, (k % 2) * SEQ:(k % 2 + 1) * SEQ],
                                  ACT.Identity, scale=gain(k), bias=bias(k)))
                st.wait(s)
                fn(oH[:, 0:4], xv[:, 0:4], ACT.Copy).then_inc(x_hi, 1)
                act.wait_ge(val_dve, 4 * (e + 1))
                fn(oH[:, 4:8], xv[:, 4:8], ACT.Copy).then_inc(x_hi, 1)

            def no(k):
                return 0.0

            def cp(o, i, **kw):
                return fn(o, i, ACT.Copy, **kw)

            def gates_act():
                act.wait_ge(g_dve, 1)
                ba = sm[:, 12:14, 0:16]
                fn(sm[:, 2, 0:16].rearrange("p (t n) -> p t n", t=TT), ba[:, :, 0:8], ACT.Exp, scale=-1.0)
                fn(sm[:, 14, 0:8], rows_a[:, 128:136], ACT.Exp)
                fn(sm[:, 15, 0:8], rows_a[:, 144:152], ACT.Exp).then_inc(g_act, 1)
                act.wait_ge(g_dve, 2)
                fn(sm[:, 4, 0:16], sm[:, 3, 0:16], ACT.Exp).then_inc(g_act, 1)
                act.wait_ge(g_dve, 3)
                fn(sm[:, 6], sm[:, 5], ACT.Ln).then_inc(g_act, 1)

            def delta_act():
                act.wait_ge(g_dve, 5)
                fn(sm[:, 17, 0:16], sm[:, 16, 0:16], ACT.Exp)
                fn(sm[:, 19, 0:8], sm[:, 18, 0:8], ACT.Exp).then_inc(g_act, 1)
                for q in range(0, 12, 2):
                    t, f0 = q // 6, 4 * (q % 6)
                    act.wait_ge(tok_pe, q + 1)
                    cp(tok[:, t, f0:f0 + 4].rearrange("p a b -> p (a b)"), ps[AUX + q % 4][:]).then_inc(tok_act, 1)
                for q in range(0, 8, 2):
                    act.wait_ge(back_pe, q + 1)
                    cp(feat[:, 2 * q:2 * q + 2].rearrange("p a b -> p (a b)"), ps[AUX + q % 4][:]).then_inc(back_act, 1)
                for g in range(4):
                    act.wait_ge(arg_dve, g + 1)
                    fn(dS, dS, ACT.Exp)
                    fn(dT, dT, ACT.Exp).then_inc(exp_act, 1)
                    act.wait_ge(mt_pe, g + 1)
                    cp(MT[:, 4 * g:4 * g + 4].rearrange("p a b -> p (a b)"), ps[7][:]).then_inc(mt_act, 1)

                def banks(first, bank, o):
                    for hb in range(2):
                        act.wait_ge(scan_pe, first + hb)
                        cp(o(4 * hb), ps[bank + hb][:].rearrange("p (a b) -> p a b", a=4)).then_inc(scan_act, 1)
                banks(1, 4, lambda n: P_[:, n:n + 4])
                banks(3, 6, lambda n: T_[:, n:n + 4])
                banks(9, 4, lambda n: tok[:, 0, n:n + 4])
                banks(11, 6, lambda n: P_[:, 8 + n:12 + n])
                for b in range(4):
                    act.wait_ge(y_pe, b + 1)
                    cp(xH[:, 2 * b:2 * b + 2].rearrange("p a b -> p (a b)"), ps[AUX + b][:]).then_inc(y_hi, 1)

            def band_act():
                for g in range(4):
                    b = g % 2
                    act.wait_ge(b_max, g + 1)
                    for x in range(4):
                        for t in range(TT):
                            c = slice(0, 256) if t else slice(256, 384)
                            e = fn(p_b[:, b, x, c], p_b[:, b, x, c], ACT.Exp, bias=st_b[:, b, 1, 2 * x + t:2 * x + t + 1],
                                   accum_out=st_b[:, b, 2, 2 * x + t:2 * x + t + 1])
                            e.then_inc(b_exp, 1)
                    for x in (0, 2):
                        act.wait_ge(b_turn, 4 * g + x + 1)
                        cp(pT_b[:, b, x], ps[x][:, 0:384]).then_inc(b_tact, 1)
                    act.wait_ge(y_pe, 4 + g + 1)
                    cp(xH[:, 2 * g:2 * g + 2].rearrange("p a b -> p (a b)"), ps[0][:]).then_inc(y_hi, 1)

            def mix_act():
                for k in range(4):
                    for t in range(TT):
                        o = TABLES["pos"][0] + 2 * k + t
                        e = fn(dec[:, k, t], lg[:, 4 * (k % 2):4 * (k % 2) + 4], ACT.Exp, scale=tb[:, o:o + 1])
                e.then_inc(m_dec, 1)
                for d in range(2):
                    act.wait_ge(m_state, d + 1)
                    cp(s_fb[:, d].rearrange("p a b -> p (a b)"), ps[4 + d][:], scale=HK ** -0.5).then_inc(m_sact, 1)
                for b in (0, 2):
                    act.wait_ge(m_turn, b + 1)
                    o = rkT if b else rqT
                    cp(o[:, 0:2].rearrange("p a b -> p (a b)"), ps[AUX + b][:]).then_inc(m_tact, 1)
                act.wait_ge(m_rope, 2)
                for n in range(RET_H):
                    if n:
                        act.wait_ge(m_sd, n)
                    for d, name in enumerate(("fwd", "bwd")):
                        o = TABLES[name][0]
                        e = fn(wt[:, d], tb[:, o:o + 512], ACT.Exp, scale=lg[:, 4 * d + n:4 * d + n + 1])
                    e.then_inc(m_w, 1)
                for b in range(2):
                    act.wait_ge(y_pe, 8 + b + 1)
                    cp(xH[:, 2 * b:2 * b + 2].rearrange("p a b -> p (a b)"), ps[4 + b][:]).then_inc(y_hi, 1)
                for b in range(2):
                    act.wait_ge(q_turn, b + 1)
                    cp(aqT[:, 2 * b:2 * b + 2].rearrange("p a b -> p (a b)"), ps[4 + b][:]).then_inc(q_tact, 1)
                act.wait_ge(q_turn, 3)
                cp(akT[:], ps[6][:]).then_inc(q_tact, 1)
                for j in range(4):
                    for s in range(2):
                        for t in range(TT):
                            n = 2 * s + t
                            act.wait_ge(s_max, 4 * j + n + 1)
                            if j:
                                act.wait_ge(s_turn, 4 * j)
                            fn(ap_[:, s, t], ps[4 + n][:], ACT.Exp, bias=st_p[:, 1, n:n + 1], scale=ATT_D ** -0.5,
                               accum_out=st_p[:, 2, n:n + 1]).then_inc(s_exp, 1)
                    for b in (0, 2):
                        act.wait_ge(s_turn, 4 * j + b + 1)
                        cp(apT[:, b // 2, 0:2].rearrange("p a b -> p (a b)"), ps[b][:]).then_inc(s_tact, 1)
                    act.wait_ge(y_pe, 10 + j + 1)
                    r = 64 * (j % 2)
                    cp(xH[r:r + 64, 4 + j // 2:8:2], ps[0][r:r + 64].rearrange("p (a b) -> p a b", a=2)).then_inc(y_hi, 1)

            act.dma_start(cols[:], a["cols"]).then_inc(consts_in, 16)
            act.dma_start(cst[:], a["consts"]).then_inc(consts_in, 16)
            act.dma_start(rows_a[:], a["rows_a"].partition_broadcast(P).rearrange("p a n -> p (a n)")).then_inc(consts_in, 16)
            act.dma_start(bmrow[:], a["rows_m"].partition_broadcast(P).rearrange("p a n -> p (a n)")).then_inc(early_in, 16)
            act.dma_start(baw[:], a["a_w_in"][0].rearrange("(k p) n -> p k n", p=P)[:, :, 4 * D:4 * D + 16]).then_inc(early_in, 16)
            act.wait_ge(x_in, 16)
            squares("a", h)
            act.wait_ge(consts_in, 48)
            st.do(fn(cact[:].rearrange("p a k -> p (a k)"), col("c", 0, 16), ACT.Silu))
            st.put(fn(cpH[:], cact[:].rearrange("p a k -> p k a"), ACT.Copy))
            st.put(fn(crH[:], cact[:, 0].unsqueeze(2).broadcast_to([P, KD, P]), ACT.Copy))
            act.wait_ge(early_in, 32)
            st.do(fn(baH[:], baw[:], ACT.Copy))
            act_cond = st.n
            for c in range(SPLIT):
                hi(0, 0, c)
            scaled("a", "a", lambda k: col("a_norm", k), no, xH)
            for m in range(24):
                act.wait_ge(unit_done, 2 * m + 2)
                if m not in MOD_COL:
                    e = m - 8 if m < 12 else m - 16
                    g = gate1 if e < 4 else gate2
                    fn(g[:, (e % 4) * 256:(e % 4 + 1) * 256], ps[e % 4][:, 0:256], ACT.Copy).then_inc(bank_free, 1)
                ahead(0, 2 * m)
            if stop == "mod":
                return

            gates_act()

            def silu_a(i, j):
                n = STAGED["qkv"] + j
                act.wait_ge(unstaged, i * 4 + (n + 1))
                fn(feat[:, bass.ds((i * 4 + j) * 2, 2)], cv[:, n % 2], ACT.Silu).then_inc(silu_done, 1)
            staging("qkv", after=silu_a)
            blocks("z", lambda i, j, b: fn(zs[:, :, bass.ds((i * 4 + j) * 256, 256)],
                                           b[:].rearrange("p (t n) -> p t n", t=TT), ACT.Silu))
            delta_act()
            staging("wo_a")
            if stop == "wo_a":
                return

            def silu_f(which):
                def after(i, j):
                    n = STAGED[which] + j
                    act.wait_ge(unstaged, i * 4 + (n + 1))
                    fn(cv[:, n % 2, 0], cv[:, n % 2, 0], ACT.Silu).then_inc(silu_done, 1)
                return after

            def ffn(l):
                n = f"f{l}"
                squares(n, h)
                scaled(n, n, lambda k: col(f"f_norm{l}", k), no, xH)
                staging(f"up{l}", after=silu_f(f"up{l}"))
                down(f"down{l}", F_TILES)
            act.wait_ge(unstaged, STAGED["wo_a"] + 4)
            ffn(0)
            if stop == "down0":
                return
            act.wait_ge(res_done, RES["down0"])
            squares("kv", h)
            scaled("kv", "kv", lambda k: col("kv_norm", k), no, xH)
            scaled("q", "kv", lambda k: col("b_norm", k), no, x2H)

            def two(buf, scale=1.0):
                return lambda i, j, b: fn(buf[:, bass.ds((i * 4 + j) * 2, 2)], b[:].rearrange("p (f n) -> p f n", f=2),
                                          ACT.Copy, scale=scale)
            blocks("k", two(kT))
            blocks("v", lambda i, j, b: fn(vt[:, :, bass.ds((i * 4 + j) * 256, 256)],
                                           b[:].rearrange("p (t n) -> p t n", t=TT), ACT.Copy))
            blocks("q", two(qT, BH ** -0.5))
            band_act()
            staging("wo_b")
            if stop == "wo_b":
                return
            act.wait_ge(unstaged, STAGED["wo_b"] + 4)
            ffn(1)
            if stop == "down1":
                return
            act.wait_ge(res_done, RES["down1"])
            squares("x2", h)
            act.wait_ge(late_in, 64)
            act.wait_ge(res_done, RES["x2"])
            squares("ctx", ctx_in)
            scaled("ctx", "ctx", lambda k: gs1[:, k, 1:2], lambda k: modc[:, k, 1:2], xcH)
            squares("n1", h)
            scaled("n1", "n1", lambda k: gs1[:, k, 0:1], lambda k: modc[:, k, 0:1], xH)
            e = BANK["win"]
            for m in range(11):
                act.wait_ge(unit_done, U("win") + 2 * m + 2)
                b = ps[e % 4][:].rearrange("p (t n) -> p t n", t=TT)
                if m < 4:
                    o, f = qk_t[:, :, m * 256:(m + 1) * 256], ACT.Copy
                elif m < 6:
                    o, f = rv[:, :, (m - 4) * 256:(m - 3) * 256], ACT.Copy
                elif m < 8:
                    o, f = sg[:, :, (m - 6) * 256:(m - 5) * 256], ACT.Silu
                else:
                    o, f = aqkv[:, :, (m - 8) * 256:(m - 7) * 256], ACT.Copy
                fn(o, b, f).then_inc(bank_free, 1)
                e += 1
                if m in CTX_BLOCKS:
                    b = ps[e % 4][:].rearrange("p (t n) -> p t n", t=TT)
                    o = cakv[:] if m == 10 else ckv[:, :, (m - 2) * 256:(m - 1) * 256]
                    fn(o, b, ACT.Copy).then_inc(bank_free, 1)
                    e += 1
                ahead(0, U("win") + 2 * m)
            mix_act()
            staging("wo_c")
            if stop == "wo_c":
                return
            act.wait_ge(unstaged, STAGED["wo_c"] + 4)
            squares("n2", h)
            scaled("n2", "n2", lambda k: gs2[:, k:k + 1], lambda k: modc[:, 16 + k, 0:1], xH)
            staging("ff1", func=ACT.Relu)
            down("ff2", FF2_TILES)
            act.wait_ge(res_done, RES["ff2"])
            squares("fin", h)

        @block.gpsimd
        def _(pool):
            def inverse_root(o, i):
                return nc.gpsimd.tensor_tensor(o, i, mhalf[:, 0:i.shape[1]], ALU.pow)

            nc.gpsimd.memset(mhalf[:], -0.5).then_inc(pool_s, 1)
            pool.wait_ge(pool_s, 1)

            def norm(n):
                pool.wait_ge(ms_done, STAT[n] + 1)
                inverse_root(rstd[:], msq[:]).then_inc(rstd_done, 1)

            norm("a")
            if stop == "mod":
                return
            for t in range(TT):
                pool.wait_ge(tok_act, 3 * t + 2)
                pool.wait_ge(tok_dve, 3 * t + 2)
                nc.gpsimd.tensor_tensor((T_, MT)[t][:], tok[:, t, 0:16], tok[:, t, 0:16], ALU.mult).then_inc(tok_sq, 1)
            pool.wait_ge(pw_in, 1)
            inverse_root(r32[:, 1], r32[:, 0]).then_inc(pw_out, 1)
            pool.wait_ge(pw_in, 2)
            inverse_root(r32[:, 1, 0:16], r32[:, 0, 0:16]).then_inc(pw_out, 1)
            if stop == "wo_a":
                return
            pool.wait_ge(unstaged, STAGED["wo_a"] + 4)
            rb = a["b_rel_bias"]
            pool.dma_start(slab[:], bass.AP(tensor=rb.tensor, offset=P + 1, ap=[[1, P], [513, B_HEADS], [1, SEQ]])).then_inc(slab_in, 16)
            pool.wait_ge(slab_in, 16)
            nc.gpsimd.memset(slab[0:64, :, 0:64], NEG).then_inc(slab_masked, 1)
            norm("f0")
            if stop == "down0":
                return
            norm("kv")
            if stop == "wo_b":
                return
            norm("f1")
            if stop == "down1":
                return
            pool.wait_ge(res_done, RES["down1"])
            pool.dma_start(row_f1[:], a["rows_c"][:, 0:1024].partition_broadcast(P).rearrange("p a n -> p (a n)")).then_inc(late_in, 16)
            pool.dma_start(ctx_in[:], a["ctx_2"].rearrange("o (t p) d -> p (o t) d", p=P)).then_inc(late_in, 16)
            pool.dma_start(tb[:], a["tables"]).then_inc(late_in, 16)
            pool.dma_start(rows_c[:], a["rows_c"][:, 1024:1664].partition_broadcast(P).rearrange("p a n -> p (a n)")).then_inc(late_in, 16)
            norm("x2")
            norm("ctx")
            norm("n1")
            pool.wait_ge(pw_in, 3)
            inverse_root(st_r[:, 3], st_r[:, 2]).then_inc(pw_out, 1)
            pool.wait_ge(pw_in, 4)
            for t in range(TT):
                last = inverse_root(st_a[:, t, 1], st_a[:, t, 0])
            last.then_inc(pw_out, 1)
            if stop == "wo_c":
                return
            pool.wait_ge(unstaged, STAGED["wo_c"] + 4)
            pool.dma_start(rows_f[:], a["rows_c"][:, 1664:2688].partition_broadcast(P).rearrange("p a n -> p (a n)")).then_inc(final_in, 16)
            norm("n2")
            norm("fin")

        @block.vector
        def _(dve):
            st = Steps(dve, dve_s)
            tt = nc.vector.tensor_tensor
            ts = nc.vector.tensor_scalar
            stt = nc.vector.scalar_tensor_tensor

            def bc(x, n):
                return x.unsqueeze(2).broadcast_to([x.shape[0], x.shape[1], n])

            def rep(x, n):
                return x.unsqueeze(1).broadcast_to([x.shape[0], n, x.shape[1]])

            def four(x):
                return x.rearrange("p (a b) -> p a b", a=4)

            def rest(o, x, hi):
                return tt(o, x, hi.bitcast(F32), ALU.subtract)

            def lo(i, per, c):
                if isinstance(i, int) and c >= UNITS:
                    return
                dve.wait_ge(hi_done, i * per + (c + 1))
                rest(wL[:, c % SPLIT], raw[:, c % RAW], wH[:, c % SPLIT]).then_inc(lo_done, 1)

            def ahead(i, c):
                lo(i, 8, c + SPLIT)
                lo(i, 8, c + SPLIT + 1)

            def blocks(name, before=None, each=0):
                def body(i, j):
                    if before:
                        before(i, j)
                    ahead(i, U(name) + 2 * j)
                turns(dve, BLOCKS[name][1], body, st, each)

            def free(name, i, j):
                dve.wait_ge(bank_free, i * 4 + (BANK[name] + j + 1))

            def normed(n, src, o=None):
                dve.wait_ge(sq_done, 2 * STAT[n] + 2)
                ts(msq[:], ssq[:], 1.0 / D, EPS, ALU.mult, ALU.add).then_inc(ms_done, 1)
                dve.wait_ge(rstd_done, STAT[n] + 1)
                for t in range(TT):
                    if o is None:
                        ts(xn[:, t], src[:, t], rstd[:, t:t + 1], None, ALU.mult).then_inc(xn_done, 1)
                    else:
                        o(t)

            def scaled(n, turn, gain, bias, oH, oL):
                e = SCALED[n]
                dve.wait_ge(turned, 4 * TURN[turn] + 4)
                if e:
                    dve.wait_ge(x_ready, 2 * e)
                for k in range(4, 8):
                    src = ps[AUX + k // 2][:, (k % 2) * SEQ:(k % 2 + 1) * SEQ]
                    if bias:
                        v = ts(xv[:, k], src, gain(k), bias(k), ALU.mult, ALU.add)
                    else:
                        v = ts(xv[:, k], src, gain(k), None, ALU.mult)
                    v.then_inc(val_dve, 1)
                for f in range(2):
                    dve.wait_ge(x_hi, 2 * e + f + 1)
                    rest(oL[:, 4 * f:4 * f + 4], xv[:, 4 * f:4 * f + 4], oH[:, 4 * f:4 * f + 4]).then_inc(x_ready, 1)

            def down(name, count, gate=None):
                for m in range(SPLIT):
                    dve.wait_ge(a_hi, ACTS[name] + m + 1)
                    rest(aL[:, m], act_a[:, m], aH[:, m]).then_inc(a_lo, 1)

                def body(i, j):
                    lo(i, 4, U(name) + j + SPLIT)
                    m = j + SPLIT
                    dve.wait_ge(a_hi, i * 4 + (ACTS[name] + m + 1))
                    rest(aL[:, m % SPLIT], act_a[:, one(i * 4 + m)].rearrange("p a n -> p (a n)"),
                         aH[:, m % SPLIT]).then_inc(a_lo, 1)
                turns(dve, count - SPLIT, body)
                for j in range(count - SPLIT, count):
                    lo(0, 4, U(name) + j + SPLIT)
                dve.wait_ge(unit_done, U(name) + count)
                for t in range(TT):
                    for c in range(2):
                        hc = h[:, t, c * 512:(c + 1) * 512]
                        b = ps[AUX + 2 * t + c][:]
                        if gate is not None:
                            tmp = stage[:, c].rearrange("p a b -> p (a b)")
                            st.do(tt(tmp, b, gate[:, c * 512:(c + 1) * 512], ALU.mult))
                            b = tmp
                        tt(hc, hc, b, ALU.add).then_inc(res_done, 1)

            def residual(name, gate=None):
                def body(i, j):
                    free(name, i, j)
                    n = STAGED[name] + j
                    s = stage[:, n % 2]
                    hc = h[:, :, bass.ds((i * 4 + j) * 256, 256)]
                    if gate is not None:
                        st.do(tt(s, s, rep(gate[:, bass.ds((i * 4 + j) * 256, 256)], TT), ALU.mult))
                    tt(hc, hc, s, ALU.add).then_inc(unstaged, 1)
                blocks(name, body, 1 if gate is not None else 0)

            def gates():
                ba = sm[:, 12:14, 0:16]
                v = lambda k: sm[:, k, 0:16].rearrange("p (t n) -> p t n", t=TT)
                nc.vector.tensor_copy(ba, ps[AUX + 1][:, 0:32].rearrange("p (t n) -> p t n", t=TT)).then_inc(g_dve, 1)
                dve.wait_ge(g_dve, 1)
                st.do(tt(v(1), ba[:, :, 8:16], rep(rows_a[:, 136:144], TT), ALU.add))
                st.do(ts(sm[:, 3, 0:16], sm[:, 1, 0:16], -1.0, None, ALU.mult))
                tt(sm[:, 3, 0:16], sm[:, 3, 0:16], sm[:, 1, 0:16], ALU.min).then_inc(g_dve, 1)
                dve.wait_ge(g_act, 1)
                st.do(ts(sm[:, 2, 0:16], sm[:, 2, 0:16], 1.0, None, ALU.add))
                st.do(nc.vector.reciprocal(sm[:, 0, 0:16], sm[:, 2, 0:16]))
                st.do(ts(sm[:, 4, 16:24], sm[:, 15, 0:8], -1.0, None, ALU.mult))
                dve.wait_ge(g_act, 2)
                ts(sm[:, 5], sm[:, 4], 1.0, None, ALU.add).then_inc(g_dve, 1)
                dve.wait_ge(g_dve, 3)
                st.do(ts(sm[:, 7], sm[:, 5], 1.0, None, ALU.is_equal))
                st.do(stt(sm[:, 9], sm[:, 5], -1.0, sm[:, 7], ALU.add, ALU.add))
                st.do(nc.vector.reciprocal(sm[:, 9], sm[:, 9]))
                dve.wait_ge(g_act, 3)
                st.do(tt(sm[:, 8], sm[:, 6], sm[:, 7], ALU.add))
                st.do(tt(sm[:, 8], sm[:, 8], sm[:, 4], ALU.mult))
                st.do(tt(sm[:, 8], sm[:, 8], sm[:, 9], ALU.mult))
                st.put(nc.vector.tensor_copy(lg[:], sm[:, 8, 16:24]))
                st.do(stt(sm[:, 1, 0:16], sm[:, 1, 0:16], 0.0, sm[:, 8, 0:16], ALU.max, ALU.add))
                stt(v(10), v(1), -1.0, rep(sm[:, 14, 0:8], TT), ALU.mult, ALU.mult).then_inc(g_dve, 1)

            def delta():
                dve.wait_ge(g_sum, 1)
                st.do(nc.vector.tensor_copy(sm[:, 16, 0:16], ps[7][:, 0:16]))
                tt(sm[:, 18, 0:8], ps[7][:, 16:24], sm[:, 16, 0:8], ALU.subtract).then_inc(g_dve, 1)
                gc, beta, g_, eg, ke = (sm[:, k, 0:16] for k in (16, 0, 10, 17, 19))
                for q in range(1, 12, 2):
                    t, f0 = q // 6, 4 * (q % 6)
                    dve.wait_ge(tok_pe, q + 1)
                    nc.vector.tensor_copy(tok[:, t, f0:f0 + 4], four(ps[AUX + q % 4][:])).then_inc(tok_dve, 1)
                for t in range(TT):
                    dve.wait_ge(tok_sq, t + 1)
                    st.do(nc.vector.tensor_reduce(r32[:, 0, 16 * t:16 * t + 16], (T_, MT)[t][:], AX, ALU.add))
                ts(r32[:, 0], r32[:, 0], EPS, None, ALU.add).then_inc(pw_in, 1)
                dve.wait_ge(pw_out, 1)
                r = r32[:, 1].rearrange("p (t n) -> p t n", t=TT)
                st.do(ts(r[:, :, 0:8], r[:, :, 0:8], HK ** -0.5, None, ALU.mult))
                for t in range(TT):
                    tt(tok[:, t, 0:16], tok[:, t, 0:16], bc(r32[:, 1, 16 * t:16 * t + 16], HK), ALU.mult).then_inc(unit_qk, 1)
                for q in range(1, 8, 2):
                    dve.wait_ge(back_pe, q + 1)
                    nc.vector.tensor_copy(feat[:, 2 * q:2 * q + 2].rearrange("p a b -> p (a b)"),
                                          ps[AUX + q % 4][:]).then_inc(back_dve, 1)
                for g in range(4):
                    q4 = slice(4 * g, 4 * g + 4)
                    tt(dG, rep(K_["tri"], 4), bc(g_[:, q4], P), ALU.mult).then_inc(dg_dve, 1)
                    dve.wait_ge(row_pe, g + 1)
                    st.do(tt(dT, four(ps[4][:]), bc(gc[:, q4], P), ALU.subtract))
                    st.do(tt(dS, rep(K_["low"], 4), dT, ALU.subtract))
                    tt(dT, dT, rep(K_["upT"], 4), ALU.add).then_inc(arg_dve, 1)
                    dve.wait_ge(exp_act, g + 1)
                    dve.wait_ge(kq_pe, g + 1)
                    st.do(tt(dS, four(ps[5][:]), dS, ALU.mult))
                    tt(T_[:, q4], dS, bc(beta[:, q4], P), ALU.mult).then_inc(m_dve, 1)
                    tt(AT[:, q4], four(ps[6][:]), dT, ALU.mult).then_inc(at_dve, 1)
                    dve.wait_ge(at_dve, g + 1)
                dve.wait_ge(mt_act, 4)
                join = K_["join"].rearrange("p (l n) -> p l n", l=7)
                st.do(tt(T_[:], T_[:], rep(join[:, 0], 16), ALU.mult))
                st.do(tt(U_[:], MT[:], rep(K_["join1T"], 16), ALU.mult))
                st.do(tt(T_[:], T_[:], rep(ident, 16), ALU.add))
                tt(U_[:], U_[:], rep(ident, 16), ALU.add).then_inc(dbl_dve, 1)

                def level(i, l):
                    mask = join[:, one(i + (l + 1))].broadcast_to([P, 4, P])
                    for step in range(3):
                        for g in range(4):
                            q4 = slice(4 * g, 4 * g + 4)
                            dve.wait_ge(dbl_pe, i * 12 + (l * 12 + step * 4 + g + 1))
                            b = four(ps[AUX + g][:])
                            if step == 0:
                                tt(P_[:, q4], b, mask, ALU.mult).then_inc(dbl_dve, 1)
                            else:
                                o = (T_, U_)[step - 1][:, q4]
                                tt(o, o, b, ALU.add).then_inc(dbl_dve, 1)
                level(0, 0)
                with dve.Fori(0, LEVELS - 1) as i:
                    level(i, 1)
                tt(tok[:, 0, 16:24], tok[:, 0, 16:24], bc(beta[:, 0:8], HK), ALU.mult).then_inc(scan_dve, 1)
                dve.wait_ge(g_act, 4)
                tt(tok[:, 0, 8:16], tok[:, 0, 8:16], bc(ke[:, 0:8], HK), ALU.mult).then_inc(scan_dve, 1)
                for hb in range(2):
                    dve.wait_ge(scan_pe, 5 + hb)
                    tt(MT[:, 8 + 4 * hb:12 + 4 * hb], four(ps[4 + hb][:]), bc(eg[:, 8 + 4 * hb:12 + 4 * hb], P),
                       ALU.mult).then_inc(scan_dve, 1)
                dve.wait_ge(scan_dve, 4)
                st.do(tt(MT[:, 8:16], tok[:, 1, 16:24], MT[:, 8:16], ALU.subtract))
                tt(T_[:, 8:16], MT[:, 8:16], bc(beta[:, 8:16], P), ALU.mult).then_inc(scan_dve, 1)
                for hb in range(2):
                    dve.wait_ge(scan_pe, 7 + hb)
                    tt(MT[:, 4 * hb:4 + 4 * hb], four(ps[6 + hb][:]), bc(eg[:, 8 + 4 * hb:12 + 4 * hb], P),
                       ALU.mult).then_inc(scan_dve, 1)
                dve.wait_ge(scan_dve, 7)
                for hb in range(2):
                    dve.wait_ge(scan_pe, 13 + hb)
                    tt(tok[:, 1, 4 * hb:4 * hb + 4], four(ps[4 + hb][:]), MT[:, 4 * hb:4 * hb + 4],
                       ALU.add).then_inc(scan_dve, 1)
                dve.wait_ge(scan_dve, 9)
                dve.wait_ge(scan_act, 6)
                for t in range(TT):
                    st.put(tt(MT[:, 8 * t:8 * t + 8], tok[:, t, 0:8], tok[:, t, 0:8], ALU.mult))
                st.wait(st.n)
                st.do(nc.vector.tensor_reduce(r32[:, 0, 0:16], MT[:], AX, ALU.add))
                ts(r32[:, 0, 0:16], r32[:, 0, 0:16], 1.0 / HK, EPS, ALU.mult, ALU.add).then_inc(pw_in, 1)
                dve.wait_ge(pw_out, 2)
                dve.wait_ge(bank_free, BANK["z"] + 4)
                for t in range(TT):
                    o = tok[:, t, 0:8]
                    st.do(tt(o, o, bc(r32[:, 1, 8 * t:8 * t + 8], HK), ALU.mult))
                    st.do(tt(o, o, rep(rows_a[:, 0:128], 8), ALU.mult))
                    last = tt(o, o, zs[:, t].rearrange("p (a b) -> p a b", a=8), ALU.mult)
                last.then_inc(y_rows, 1)
                for b in range(4):
                    dve.wait_ge(y_hi, b + 1)
                    rest(xL[:, 2 * b:2 * b + 2].rearrange("p a b -> p (a b)"), ps[AUX + b][:],
                         xH[:, 2 * b:2 * b + 2].rearrange("p a b -> p (a b)")).then_inc(y_ready, 1)

            def band():
                for g in range(4):
                    b = g % 2
                    dve.wait_ge(b_score, g + 1)
                    if g == 0:
                        dve.wait_ge(slab_masked, 1)
                    for x in range(4):
                        n, o = 4 * g + x, x // 2
                        for t in range(TT):
                            c = slice(0, 256) if t else slice(256, 384)
                            w = ps[4 + x % 2][:, o * 256:(o + 1) * 256] if t else ps[6 + x % 2][:, o * P:(o + 1) * P]
                            s = slab[:, n, ::-1] if t else slab[:, n, P - 1::-1]
                            st.put(nc.vector.tensor_tensor_reduce(p_b[:, b, x, c], w, s, 1.0, -3e38, ALU.add, ALU.max,
                                                                  st_b[:, b, 0, 2 * x + t:2 * x + t + 1]))
                    st.wait(st.n)
                    ts(st_b[:, b, 1], st_b[:, b, 0], -1.0, None, ALU.mult).then_inc(b_max, 1)
                    dve.wait_ge(b_exp, 8 * g + 8)
                    st.do(nc.vector.reciprocal(st_b[:, b, 0], st_b[:, b, 2]))
                    r = st_b[:, b, 0].rearrange("p (x t) -> p x t", t=TT)
                    tt(p_b[:, b, :, 0:256], p_b[:, b, :, 0:256], bc(r[:, :, 1], 256), ALU.mult)
                    tt(p_b[:, b, :, 256:384], p_b[:, b, :, 256:384], bc(r[:, :, 0], P), ALU.mult).then_inc(b_prob, 1)
                    for x in (1, 3):
                        dve.wait_ge(b_turn, 4 * g + x + 1)
                        nc.vector.tensor_copy(pT_b[:, b, x], ps[x][:, 0:384]).then_inc(b_tdve, 1)
                    dve.wait_ge(y_hi, 4 + g + 1)
                    rest(xL[:, 2 * g:2 * g + 2].rearrange("p a b -> p (a b)"), ps[0][:],
                         xH[:, 2 * g:2 * g + 2].rearrange("p a b -> p (a b)")).then_inc(y_ready, 1)

            def table(name, t=None):
                o, n = TABLES[name]
                return tb[:, o:o + n] if t is None else tb[:, o + t * n // 2:o + (t + 1) * n // 2]

            def mix():
                dve.wait_ge(m_dec, 1)
                dve.wait_ge(bank_free, BANK["wo_c"])
                for d in range(2):
                    for t in range(TT):
                        tt(rope[:, t, d * 512:(d + 1) * 512].rearrange("p (a b) -> p a b", a=4),
                           ckv[:, t, 0:512].rearrange("p (a b) -> p a b", a=4), bc(dec[:, 2 + d, t], P),
                           ALU.mult).then_inc(m_ck, 1)
                dve.wait_ge(m_state, 2)
                for t in range(TT):
                    x = qk_t[:, t].rearrange("p (n c) -> p n c", n=8)
                    o = rope[:, t].rearrange("p (n c) -> p n c", n=8)
                    cos, sin = rep(table("rcos", t), 8), rep(table("rsin", t), 8)
                    u, w = (wt[:, y].rearrange("p (n c) -> p n c", n=8) for y in range(2))
                    st.put(tt(o[:, :, 0:64], x[:, :, 0:64], cos, ALU.mult))
                    st.put(tt(o[:, :, 64:], x[:, :, 0:64], sin, ALU.mult))
                    st.put(tt(u, x[:, :, 64:], sin, ALU.mult))
                    st.do(tt(w, x[:, :, 64:], cos, ALU.mult))
                    st.put(tt(o[:, :, 0:64], o[:, :, 0:64], u, ALU.subtract))
                    tt(o[:, :, 64:], o[:, :, 64:], w, ALU.add).then_inc(m_rope, 1)
                    dve.wait_ge(m_rope, t + 1)
                for b in (1, 3):
                    dve.wait_ge(m_turn, b + 1)
                    o = rkT if b == 3 else rqT
                    nc.vector.tensor_copy(o[:, 2:4].rearrange("p a b -> p (a b)"), ps[AUX + b][:]).then_inc(m_tdve, 1)
                for n in range(RET_H):
                    dve.wait_ge(m_w, n + 1)
                    st.put(tt(wt[:, 0], wt[:, 0], table("ge"), ALU.mult))
                    st.do(tt(wt[:, 1], wt[:, 1], table("le"), ALU.mult))
                    st.do(tt(wt[:, 0], wt[:, 0], wt[:, 1], ALU.add))
                    dve.wait_ge(m_s, n + 1)
                    stt(sT[:, n % 2], ps[4][:], HK ** -0.5, wt[:, 0], ALU.mult, ALU.mult).then_inc(m_sd, 1)
                    dve.wait_ge(m_o, n + 1)
                    st.do(nc.vector.tensor_copy(o_r[:, :, n], ps[6][:, 0:256].rearrange("p (t c) -> p t c", t=TT)))
                    for t in range(TT):
                        st.do(stt(o_r[:, t, n], ps[6][:, 256 + t * P:256 + (t + 1) * P], dec[:, 0, t, n:n + 1],
                                  o_r[:, t, n], ALU.mult, ALU.add))
                    for t in range(TT):
                        last = stt(o_r[:, t, n], ps[7][:, t * P:(t + 1) * P], dec[:, 1, t, n:n + 1],
                                   o_r[:, t, n], ALU.mult, ALU.add)
                    last.then_inc(m_od, 1)
                dve.wait_ge(m_od, RET_H)
                o = o_r[:].rearrange("p t n c -> p (t n) c")
                sq = rope[:, 0].rearrange("p (a b) -> p a b", a=8)
                st.do(nc.vector.tensor_reduce(st_r[:, 0], o, AX, ALU.add))
                st.do(ts(st_r[:, 0], st_r[:, 0], 1.0 / HK, None, ALU.mult))
                st.do(tt(o, o, bc(st_r[:, 0], HK), ALU.subtract))
                st.do(tt(sq, o, o, ALU.mult))
                st.do(nc.vector.tensor_reduce(st_r[:, 1], sq, AX, ALU.add))
                ts(st_r[:, 2], st_r[:, 1], 1.0 / HK, EPS, ALU.mult, ALU.add).then_inc(pw_in, 1)
                dve.wait_ge(pw_out, 3)
                st.do(tt(o, o, bc(st_r[:, 3], HK), ALU.mult))
                o2 = o_r[:].rearrange("p t n c -> p t (n c)")
                st.do(tt(o2, o2, rep(rows_c[:, 0:512], TT), ALU.mult))
                tt(o2, o2, sg[:], ALU.mult).then_inc(y_rows, 1)
                for b in range(2):
                    dve.wait_ge(y_hi, 8 + b + 1)
                    rest(xL[:, 2 * b:2 * b + 2].rearrange("p a b -> p (a b)"), ps[4 + b][:],
                         xH[:, 2 * b:2 * b + 2].rearrange("p a b -> p (a b)")).then_inc(y_ready, 1)
                for t in range(TT):
                    x = aqkv[:, t, 0:640].rearrange("p (n c) -> p n c", c=ATT_D)
                    xc = cakv[:, t, 0:128].rearrange("p (n c) -> p n c", c=ATT_D)
                    st.put(tt(asq[:, 0:10], x, x, ALU.mult))
                    st.do(tt(asq[:, 10:12], xc, xc, ALU.mult))
                    st.do(nc.vector.tensor_reduce(st_a[:, t, 0], asq[:], AX, ALU.add))
                    last = ts(st_a[:, t, 0], st_a[:, t, 0], 1.0 / ATT_D, EPS, ALU.mult, ALU.add)
                    st.put(last) if t == 0 else last.then_inc(pw_in, 1)
                dve.wait_ge(pw_out, 4)
                qn, kn = rows_c[:, 512:576], rows_c[:, 576:640]
                for t in range(TT):
                    x = aqkv[:, t, 0:640].rearrange("p (n c) -> p n c", c=ATT_D)
                    xc = cakv[:, t, 0:128].rearrange("p (n c) -> p n c", c=ATT_D)
                    st.put(tt(x, x, bc(st_a[:, t, 1, 0:10], ATT_D), ALU.mult))
                    st.do(tt(kcn[:, t], xc, bc(st_a[:, t, 1, 10:12], ATT_D), ALU.mult))
                    st.put(tt(x[:, 0:8], x[:, 0:8], rep(qn, 8), ALU.mult))
                    st.put(tt(x[:, 8:10], x[:, 8:10], rep(kn, 2), ALU.mult))
                    st.do(tt(kcn[:, t], kcn[:, t], rep(kn, 2), ALU.mult))
                    cos, sin = rep(table("acos", t), 10), rep(table("asin", t), 10)
                    st.put(tt(rt[:, 0], x[:, :, 0:32], cos, ALU.mult))
                    st.put(tt(rt[:, 1], x[:, :, 32:], sin, ALU.mult))
                    st.put(tt(rt[:, 2], x[:, :, 0:32], sin, ALU.mult))
                    st.do(tt(rt[:, 3], x[:, :, 32:], cos, ALU.mult))
                    for c, y, op in ((0, 0, ALU.subtract), (32, 2, ALU.add)):
                        for s in range(2):
                            st.put(tt(aqn[:, t, s:8:2, c:c + 32], rt[:, y, 4 * s:4 * s + 4], rt[:, y + 1, 4 * s:4 * s + 4], op))
                        last = tt(aqn[:, t, 8:10, c:c + 32], rt[:, y, 8:10], rt[:, y + 1, 8:10], op)
                        st.put(last) if c == 0 else last.then_inc(q_rope, 1)
                    dve.wait_ge(q_rope, t + 1)
                for j in range(4):
                    for n in range(4):
                        dve.wait_ge(s_pe, 4 * j + n + 1)
                        st.do(nc.vector.tensor_reduce(st_p[:, 0, n:n + 1], ps[4 + n][:], AX, ALU.max))
                        ts(st_p[:, 1, n:n + 1], st_p[:, 0, n:n + 1], -ATT_D ** -0.5, None, ALU.mult).then_inc(s_max, 1)
                    for n in range(4):
                        dve.wait_ge(s_exp, 4 * j + n + 1)
                        st.do(nc.vector.reciprocal(st_p[:, 0, n:n + 1], st_p[:, 2, n:n + 1]))
                        w = ap_[:, n // 2, n % 2]
                        ts(w, w, st_p[:, 0, n:n + 1], None, ALU.mult).then_inc(s_prob, 1)
                    for b in (1, 3):
                        dve.wait_ge(s_turn, 4 * j + b + 1)
                        nc.vector.tensor_copy(apT[:, b // 2, 2:4].rearrange("p a b -> p (a b)"), ps[b][:]).then_inc(s_tdve, 1)
                    dve.wait_ge(y_hi, 10 + j + 1)
                    r = 64 * (j % 2)
                    rest(xL[r:r + 64, 4 + j // 2:8:2], ps[0][r:r + 64].rearrange("p (a b) -> p a b", a=2),
                         xH[r:r + 64, 4 + j // 2:8:2]).then_inc(y_ready, 1)

            dve.wait_ge(x_in, 16)
            normed("a", h)
            dve.wait_ge(act_s, 4)
            rest(cpL[:], cact[:].rearrange("p a k -> p k a"), cpH[:])
            rest(crL[:], bc(cact[:, 0], P), crH[:])
            rest(baL[:], baw[:], baH[:]).then_inc(c_ready, 1)
            for c in range(SPLIT):
                lo(0, 0, c)
            scaled("a", "a", lambda k: col("a_norm", k), None, xH, xL)
            for m in range(24):
                ahead(0, 2 * m)
            dve.wait_ge(mod_done, 1)
            gates()
            mp = ps[AUX][:, 0:64].rearrange("p (f c) -> p f c", c=2)
            st.put(tt(modc[:, 0:16], mp[:, 0:16], bc(col("b_mod", 0, 16), 2), ALU.add))
            st.do(tt(modc[:, 16:32], mp[:, 16:32], bc(col("b_mod", 24, 16), 2), ALU.add))
            st.put(stt(gs1[:], modc[:, 8:16], 1.0, bc(col("norm1", 0, 8), 2), ALU.add, ALU.mult))
            st.put(stt(gs2[:], modc[:, 24:32, 0], 1.0, col("norm2", 0, 8), ALU.add, ALU.mult))
            dve.wait_ge(bank_free, 8)
            st.put(tt(gate1[:], gate1[:], bmrow[:, 0:D], ALU.add))
            st.do(tt(gate2[:], gate2[:], bmrow[:, D:], ALU.add))
            if stop == "mod":
                return

            def conv(name, taps, tiles, bias, nextto):
                wname = {"qkv": "a_conv", "up0": "f_conv0", "up1": "f_conv1"}[name]

                def body(i, j):
                    free(name, i, j)
                    n = STAGED[name] + j
                    if name == "qkv" and not (isinstance(i, int) and j < 2):
                        dve.wait_ge(silu_done, i * 4 + (j - 1))
                    m = i * 4 + j
                    marks = [0, 0]
                    for d in range(taps):
                        for f in range(2):
                            o, x = cv[:, n % 2, f], stage[:, n % 2, f]
                            w = cols[:, one(COLS[wname][0] + (taps - 1 - d) * tiles + nextto(m, f))]
                            if d == 0:
                                if bias:
                                    c = ts(o, x, w, cols[:, one(COLS[bias][0] + nextto(m, f))], ALU.mult, ALU.add)
                                else:
                                    c = ts(o, x, w, None, ALU.mult)
                                marks[f] = st.put(c)
                                continue
                            st.wait(marks[f])
                            c = stt(o[:, d:], x[:, 0:SEQ - d], w, o[:, d:], ALU.mult, ALU.add)
                            if d == taps - 1 and f == 1:
                                c.then_inc(unstaged, 1)
                            else:
                                marks[f] = st.put(c)
                return body, 2 * taps - 1

            body, each = conv("qkv", A_TAPS, QKV_TILES, None, lambda m, f: m * 2 + f)
            blocks("qkv", body, each)
            blocks("z")
            delta()
            residual("wo_a")
            if stop == "wo_a":
                return

            def ffn(l, before):
                dve.wait_ge(unstaged, before)
                normed(f"f{l}", h)
                scaled(f"f{l}", f"f{l}", lambda k: col(f"f_norm{l}", k), None, xH, xL)
                up = f"up{l}"
                conv_, steps = conv(up, F_TAPS, 2 * F_TILES, f"f_bias{l}", lambda m, f: m + f * F_TILES)
                si = 12 + 22 * l

                def body(i, j):
                    conv_(i, j)
                    ahead(i, U(up) + 2 * j)
                    n = STAGED[up] + j
                    dve.wait_ge(silu_done, i * 4 + (si + j + 1))
                    tt(act_a[:, one(i * 4 + j)].rearrange("p a n -> p (a n)"), cv[:, n % 2, 0], cv[:, n % 2, 1],
                       ALU.mult).then_inc(prod_done, 1)
                turns(dve, BLOCKS[up][1], body, st, steps)
                down(f"down{l}", F_TILES)
            ffn(0, STAGED["wo_a"] + 4)
            if stop == "down0":
                return
            dve.wait_ge(res_done, RES["down0"])
            normed("kv", h)
            scaled("kv", "kv", lambda k: col("kv_norm", k), None, xH, xL)
            scaled("q", "kv", lambda k: col("b_norm", k), None, x2H, x2L)
            blocks("k")
            blocks("v")
            blocks("q")
            band()
            residual("wo_b")
            if stop == "wo_b":
                return
            ffn(1, STAGED["wo_b"] + 4)
            if stop == "down1":
                return
            dve.wait_ge(res_done, RES["down1"])

            def final(row):
                def o(t):
                    st.do(ts(h[:, t], h[:, t], rstd[:, t:t + 1], None, ALU.mult))
                    tt(h[:, t], h[:, t], row[:], ALU.mult).then_inc(res_done, 1)
                return o
            dve.wait_ge(late_in, 64)
            normed("x2", h, final(row_f1))
            dve.wait_ge(res_done, RES["x2"])
            normed("ctx", ctx_in)
            scaled("ctx", "ctx", lambda k: gs1[:, k, 1:2], lambda k: modc[:, k, 1:2], xcH, xcL)
            normed("n1", h)
            scaled("n1", "n1", lambda k: gs1[:, k, 0:1], lambda k: modc[:, k, 0:1], xH, xL)
            for m in range(11):
                ahead(0, U("win") + 2 * m)
            mix()
            residual("wo_c", gate1)
            if stop == "wo_c":
                return
            dve.wait_ge(unstaged, STAGED["wo_c"] + 4)
            normed("n2", h)
            scaled("n2", "n2", lambda k: gs2[:, k:k + 1], lambda k: modc[:, 16 + k, 0:1], xH, xL)

            def square(i, j):
                free("ff1", i, j)
                s = stage[:, (STAGED["ff1"] + j) % 2]
                tt(act_a[:, bass.ds((i * 4 + j) * 2, 2)], s, s, ALU.mult).then_inc(unstaged, 1)
            blocks("ff1", square)
            down("ff2", FF2_TILES, gate2)
            dve.wait_ge(res_done, RES["ff2"])
            dve.wait_ge(final_in, 16)
            normed("fin", h, final(rows_f))


def columns(x):
    x = np.asarray(x)
    return x.reshape(-1, P).T


def constants():
    i, j = np.arange(P)[:, None], np.arange(P)[None, :]
    joins = []
    for l in range(7):
        s = 1 << l
        joins.append(-((i // (2 * s) == j // (2 * s)) & (i % (2 * s) >= s) & (j % (2 * s) < s)).astype(np.float32))
    parts = [np.eye(P), np.ones((P, P)), i <= j, np.where(j < i, 0.0, NEG), np.where(j >= i, 0.0, NEG), *joins, joins[0].T]
    return np.concatenate([np.asarray(x, np.float32) for x in parts], axis=1)


def tables():
    p, i = np.arange(P)[:, None], np.arange(SEQ)[None, :]
    rel = np.concatenate([i - (p + P * t) for t in range(TT)], axis=1).astype(np.float32)
    pos = np.concatenate([p, p + P], axis=1).astype(np.float32)
    t = np.arange(SEQ, dtype=np.float32)

    def freqs(n):
        return (np.float32(10000.0) ** (-np.arange(n, dtype=np.float32) / np.float32(n))).astype(np.float32)

    def rows(x):
        return np.concatenate([x[k * P:(k + 1) * P] for k in range(TT)], axis=1)
    ra = (t[:, None] * freqs(64)).astype(np.float64)
    aa = np.concatenate([np.floor(t / 64)[:, None] * freqs(16), (t % 64)[:, None] * freqs(16)], axis=1).astype(np.float64)
    parts = [np.maximum(rel, 0), np.maximum(-rel, 0), rel >= 0, rel <= 0, pos + 1, SEQ - pos, CTX - 1 - pos, pos,
             rows(np.cos(ra)), rows(np.sin(ra)), rows(np.cos(aa)), rows(np.sin(aa))]
    return np.concatenate([np.asarray(x, np.float32) for x in parts], axis=1)


BIG = ("x", "b_rel_bias", "a_w_in", "a_w_out", "w_kv", "b_w_q", "b_w_out", "f_w_up", "f_w_down", "ctx_2", "w_mod_2", "w_in_2",
       "w_out_2", "w_ff1_2", "w_ff2_2")


def lay_out(v):
    g = {n: np.ascontiguousarray(v[n]) for n in BIG}
    order = [v["a_norm"], v["kv_norm"], v["b_norm"], v["f_norm"][0], v["f_norm"][1], v["norm1_g_2"], v["norm2_g_2"],
             v["a_conv"], v["f_conv"][0], v["f_conv"][1], v["f_conv_b"][0], v["f_conv_b"][1], v["b_mod_2"],
             v["c_2"], v["c_ctx_2"]]
    g["cols"] = np.ascontiguousarray(np.concatenate([columns(x) for x in order], axis=1))
    flat = lambda xs: np.ascontiguousarray(np.concatenate([np.asarray(x).reshape(1, -1) for x in xs], axis=1))
    g["rows_a"] = flat([v["a_out_norm"], v["a_A_log"], v["a_dt_bias"], v["ret_log_rate_2"]])
    bm = np.asarray(v["b_mod_2"]).reshape(6, D)
    g["rows_m"] = flat([bm[2], bm[5]])
    g["rows_c"] = flat([v["final_norm"], v["ret_gn_g_2"], v["q_norm_g_2"], v["k_norm_g_2"], v["final_norm_g_2"]])
    g["consts"] = constants()
    g["tables"] = tables()
    return g


def program(nc, arrays, stop=None):
    aps = {n: nc.dram_tensor(f"in_{n}", x.shape, mybir.dt.from_np(x.dtype), kind="ExternalInput").ap()
           for n, x in arrays.items()}
    out = nc.dram_tensor("out", (1, SEQ, D), F32, kind="ExternalOutput").ap()
    build(nc, aps, out, stop)


def kernel(**inputs):
    import concourse.bacc as bacc
    from concourse.bass_utils import run_bass_kernel_spmd

    arrays = lay_out(inputs)
    nc = bacc.Bacc("TRN2", target_bir_lowering=False, num_devices=1)
    program(nc, arrays)
    r = run_bass_kernel_spmd(nc, [{f"in_{n}": x for n, x in arrays.items()}], core_ids=[0])
    return r.results[0]["out"]
```

```python
from contextlib import ExitStack, contextmanager

import numpy as np

import concourse.bass as bass
from concourse import mybir

F32 = mybir.dt.float32
F32R = mybir.dt.float32r
ALU = mybir.AluOpType
ACT = mybir.ActivationFunctionType
AX = mybir.AxisListType.X

P = 128
SEQ = 256
TT = SEQ // P
D = 1024
KD = D // P
EPS = 1e-6
NEG = -1e30

A_HEADS, HK = 8, 128
QKV_TILES = 3 * A_HEADS
A_TAPS = 4
B_HEADS, BH = 16, 64
FF = 2816
F_TILES = FF // P
F_TAPS = 3
RET_H = 4
ATT_H, ATT_KV, ATT_D = 8, 2, 64
FF2_TILES = 4 * D // P
CTX = 256
LEVELS = 6

RAW = 4
SPLIT = 4
BLOCKS = {}
_n = 0
for _name, _count in (("qkv", 12), ("z", 4), ("wo_a", 4), ("up0", 22), ("down0", 11),
                      ("k", 4), ("v", 4), ("q", 4), ("wo_b", 4), ("up1", 22), ("down1", 11),
                      ("win", 11), ("wo_c", 4), ("ff1", 16), ("ff2", 16)):
    BLOCKS[_name] = (_n, _count)
    _n += _count
UNITS = 2 * _n
CTX_BLOCKS = (2, 3, 4, 5, 10)
BANK = {}
_e = 0
for _name, (_b, _count) in BLOCKS.items():
    BANK[_name] = _e
    if _name in ("down0", "down1", "ff2"):
        continue
    _e += _count + (len(CTX_BLOCKS) if _name == "win" else 0)
MOD_GROUPS = 6
MOD_EARLY = 3

COLS = {}
_c = 0
for _name, _count in (("a_norm", 8), ("kv_norm", 8), ("b_norm", 8), ("f_norm0", 8), ("f_norm1", 8),
                      ("norm1", 8), ("norm2", 8), ("a_conv", A_TAPS * 24), ("f_conv0", F_TAPS * 44),
                      ("f_conv1", F_TAPS * 44), ("f_bias0", 44), ("f_bias1", 44), ("b_mod", 48),
                      ("c", 8), ("c_ctx", 8)):
    COLS[_name] = (_c, _count)
    _c += _count
N_COLS = _c
CONSTS = {}
_c = 0
for _name, _count in (("ident", P), ("ones", P), ("tri", P), ("low", P), ("upT", P), ("join", 7 * P), ("join1T", P)):
    CONSTS[_name] = (_c, _count)
    _c += _count
N_CONSTS = _c
TABLES = {}
_c = 0
for _name, _count in (("fwd", 512), ("bwd", 512), ("ge", 512), ("le", 512), ("pos", 8),
                      ("rcos", 128), ("rsin", 128), ("acos", 64), ("asin", 64)):
    TABLES[_name] = (_c, _count)
    _c += _count
N_TABLES = _c
ROWS_A = (("out_norm", 128), ("A_log", 8), ("dt_bias", 8), ("rate", 8))
ROWS_C = (("final1", 1024), ("gn", 512), ("qn", 64), ("kn", 64), ("final2", 1024))



STAGED = {}
_s = 0
for _name in ("qkv", "wo_a", "up0", "wo_b", "up1", "wo_c", "ff1"):
    STAGED[_name] = _s
    _s += BLOCKS[_name][1]
STAT = {n: i for i, n in enumerate(("a", "f0", "kv", "f1", "x2", "ctx", "n1", "n2", "fin"))}
TURN = {n: i for i, n in enumerate(("a", "f0", "kv", "f1", "ctx", "n1", "n2"))}
SCALED = {n: i for i, n in enumerate(("a", "f0", "kv", "q", "f1", "ctx", "n1", "n2"))}
RES = {"down0": 4, "down1": 8, "x2": 10, "ff2": 14, "fin": 16}
PRODS = {"down0": 0, "down1": 22}
ACTS = {"down0": 0, "down1": 22, "ff2": 44}
AUX = 4


TOK_HEAD = [(f, t) for f0 in (16, 8, 0) for f in (f0, f0 + 4) for t in range(TT)]
TOK_BANK = [(6, ()), (7, (("pw", 1),)), (6, (("act", 1),)), (7, (("act", 2),)),
            (4, (("arg", 3),)), (5, (("arg", 4),)), (6, (("act", 3),)), (7, (("act", 4),)),
            (4, (("dve", 1),)), (5, (("dve", 2),)), (6, (("dve", 3),)), (7, (("dve", 4),))]
BACK_HEAD = (8, 10, 12, 14, 0, 2, 4, 6)


ATT_BANKS = (1, 3, 2, 0)


class Steps:

    def __init__(self, eng, sem):
        self.eng, self.sem, self.n, self.base = eng, sem, 0, 0

    def put(self, ins):
        ins.then_inc(self.sem, 1)
        self.n += 1
        return self.n

    def wait(self, n):
        self.eng.wait_ge(self.sem, self.base + n)

    def do(self, ins):
        self.wait(self.put(ins))

    @contextmanager
    def loop(self, i, turns, each):
        first = self.n
        self.base = i * each
        yield
        assert self.n - first == each, (self.n - first, each)
        self.base = 0
        self.n = first + turns * each


def turns(eng, count, body, steps=None, each=0):
    head = count % 4 or 4
    for j in range(head):
        body(0, j)
    n = (count - head) // 4
    if n == 0:
        return
    if n == 1:
        for j in range(4):
            body(0, head + j)
        return
    with eng.Fori(0, n) as i:
        if steps is None:
            for j in range(4):
                body(i, head + j)
        else:
            with steps.loop(i, n, 4 * each):
                for j in range(4):
                    body(i, head + j)


def one(m):
    return bass.ds(m, 1)


def build(nc, a, out):
    with ExitStack() as ctx:
        def sb(name, shape, dt=F32, where=ctx):
            return where.enter_context(nc.sbuf_tensor(name, shape, dt))

        def sem(name):
            return ctx.enter_context(nc.semaphore(name))

        raw = sb("raw", [P, RAW, 1024])
        wH = sb("wH", [P, SPLIT, 1024], F32R)
        wL = sb("wL", [P, SPLIT, 1024], F32R)
        h = sb("h", [P, TT, D])
        xH = sb("xH", [P, KD, SEQ], F32R)
        xL = sb("xL", [P, KD, SEQ], F32R)
        cols = sb("cols", [P, N_COLS])
        cst = sb("cst", [P, N_CONSTS])
        rows_a = sb("rows_a", [P, 152])
        stage = sb("stage", [P, 2, 2, SEQ])
        cv = sb("cv", [P, 2, 2, SEQ])
        gate1 = sb("gate1", [P, D])
        gate2 = sb("gate2", [P, D])
        modc = sb("modc", [P, 32, 2])
        gs1 = sb("gs1", [P, KD, 2])
        gs2 = sb("gs2", [P, KD])
        ssq = sb("ssq", [P, TT])
        msq = sb("msq", [P, TT])
        rstd = sb("rstd", [P, TT])
        mhalf = sb("mhalf", [P, 32])
        lg = sb("lg", [P, 8])
        cact = sb("cact", [P, KD, 2])
        mrow = sb("mrow", [2, D])

        with ExitStack() as s:
            xn = sb("xn", [P, TT, D], where=s)
            xv = sb("xv", [P, KD, SEQ], where=s)
            ctx_in = sb("ctx_in", [P, TT, D], where=s)
            row_f1 = sb("row_f1", [P, D], where=s)
            xcH = sb("xcH", [P, KD, SEQ], F32R, where=s)
            xcL = sb("xcL", [P, KD, SEQ], F32R, where=s)
            qk_t = sb("qk_t", [P, TT, D], where=s)
            rv = sb("rv", [P, TT, 512], where=s)
            sg = sb("sg", [P, TT, 512], where=s)
            aqkv = sb("aqkv", [P, TT, 768], where=s)
            tb = sb("tb", [P, N_TABLES], where=s)
            rows_c = sb("rows_c", [P, 640], where=s)
            bmrow = sb("bmrow", [P, 2048], where=s)
        with ExitStack() as s:
            cakv = sb("cakv", [P, TT, 256], where=s)
            ckv = sb("ckv", [P, TT, D], where=s)
            rope = sb("rope", [P, TT, D], where=s)
            rqT = sb("rqT", [P, RET_H, SEQ], where=s)
            rkT = sb("rkT", [P, RET_H, SEQ], where=s)
            wt = sb("wt", [P, 2, 512], where=s)
            sT = sb("sT", [P, 2, 512], where=s)
            o_r = sb("o_r", [P, TT, RET_H, P], where=s)
            s_fb = sb("s_fb", [P, 2, RET_H, P], where=s)
            dec = sb("dec", [P, 4, TT, RET_H], where=s)
            st_r = sb("st_r", [P, 4, 8], where=s)
        with ExitStack() as s:
            sb("pad_att", [P, TT, 256], where=s)
            aqn = sb("aqn", [P, TT, 10, ATT_D], where=s)
            kcn = sb("kcn", [P, TT, 2, ATT_D], where=s)
            rt = sb("rt", [P, 4, 10, 32], where=s)
            asq = sb("asq", [P, 12, ATT_D], where=s)
            aqT = sb("aqT", [P, 4, SEQ], where=s)
            akT = sb("akT", [P, 512], where=s)
            ap_ = sb("ap_", [P, 2, TT, 512], where=s)
            apT = sb("apT", [P, 2, 4, SEQ], where=s)
            st_a = sb("st_a", [P, TT, 2, 12], where=s)
            st_p = sb("st_p", [P, 3, 4], where=s)
        with ExitStack() as s:
            sb("pad_m", [P, 2 * TT * D], where=s)
            baw = sb("baw", [P, KD, 16], where=s)
            baH = sb("baH", [P, KD, 16], F32R, where=s)
            baL = sb("baL", [P, KD, 16], F32R, where=s)
        with ExitStack() as s:
            tok = sb("tok", [P, TT, QKV_TILES, HK], where=s)
            feat = sb("feat", [P, QKV_TILES, SEQ], where=s)
            T_ = sb("T_", [P, 16, P], where=s)
            MT = sb("MT", [P, 16, P], where=s)
            U_ = sb("U_", [P, 16, P], where=s)
            AT = sb("AT", [P, 16, P], where=s)
            zs = sb("zs", [P, TT, D], where=s)
            sm = sb("sm", [P, 24, 24], where=s)
            r32 = sb("r32", [P, 3, 32], where=s)
        P_ = feat[:, 16:24, :].rearrange("p a (b c) -> p (a b) c", b=2)
        dG = [stage[:, x].rearrange("p a (b c) -> p (a b) c", b=2) for x in range(2)]
        with ExitStack() as s:
            act_a = sb("act_a", [P, FF2_TILES, SEQ], where=s)
            aH = sb("aH", [P, SPLIT, SEQ], F32R, where=s)
            aL = sb("aL", [P, SPLIT, SEQ], F32R, where=s)
            rows_f = sb("rows_f", [P, D], where=s)
        with ExitStack() as s:
            p_b = sb("p_b", [P, 2, 4, 384], where=s)
            pT_b = sb("pT_b", [P, 2, 4, 384], where=s)
            kT = sb("kT", [P, KD, SEQ], where=s)
            qT = sb("qT", [P, KD, SEQ], where=s)
            vt = sb("vt", [P, TT, D], where=s)
            x2H = sb("x2H", [P, KD, SEQ], F32R, where=s)
            x2L = sb("x2L", [P, KD, SEQ], F32R, where=s)
            slab = sb("slab", [P, B_HEADS, SEQ], where=s)
            st_b = sb("st_b", [P, 2, 3, 8], where=s)

        ps = [ctx.enter_context(nc.psum_tensor(f"ps{b}", [P, 512], F32)) for b in range(8)]

        x_in = sem("x_in")
        consts_in = sem("consts_in")
        slab_in = sem("slab_in")
        slab_masked = sem("slab_masked")
        early_in = sem("early_in")
        late_in = sem("late_in")
        final_in = sem("final_in")
        unit_in = [sem(f"unit_in{i}") for i in range(RAW)]
        hi_done = sem("hi_done")
        lo_done = sem("lo_done")
        unit_done = sem("unit_done")
        bank_free = sem("bank_free")
        unstaged = sem("unstaged")
        silu_done = sem("silu_done")
        prod_done = sem("prod_done")
        a_hi = sem("a_hi")
        a_lo = sem("a_lo")
        sq_done = sem("sq_done")
        ms_done = sem("ms_done")
        rstd_done = sem("rstd_done")
        xn_done = sem("xn_done")
        turned = sem("turned")
        val_dve = sem("val_dve")
        x_hi = sem("x_hi")
        x_ready = sem("x_ready")
        res_done = sem("res_done")
        act_s = sem("act_s")
        dve_s = sem("dve_s")
        pool_s = sem("pool_s")
        c_ready = sem("c_ready")
        ba_done = sem("ba_done")
        cond_ready = sem("cond_ready")
        mod_in = [sem(f"mod_in{i}") for i in range(RAW)]
        mod_used = sem("mod_used")
        mod_kept = sem("mod_kept")
        mod_out = sem("mod_out")
        mod_act = sem("mod_act")
        out_done = sem("out_done")
        g_act = sem("g_act")
        g_dve = sem("g_dve")
        g_sum = sem("g_sum")
        tok_pe = sem("tok_pe")
        tok_act = sem("tok_act")
        tok_dve = sem("tok_dve")
        tok_sq = sem("tok_sq")
        tok_ss = sem("tok_ss")
        back_pe = sem("back_pe")
        back_act = sem("back_act")
        back_dve = sem("back_dve")
        dg_dve = sem("dg_dve")
        row_pe = sem("row_pe")
        arg_dve = sem("arg_dve")
        exp_act = sem("exp_act")
        kq_pe = sem("kq_pe")
        m_dve = sem("m_dve")
        at_dve = sem("at_dve")
        mt_pe = sem("mt_pe")
        mt_act = sem("mt_act")
        dbl_pe = sem("dbl_pe")
        dbl_dve = sem("dbl_dve")
        scan_pe = sem("scan_pe")
        scan_act = sem("scan_act")
        scan_dve = sem("scan_dve")
        pw_in = sem("pw_in")
        pw_out = sem("pw_out")
        y_rows = sem("y_rows")
        y_pe = sem("y_pe")
        y_hi = sem("y_hi")
        y_ready = sem("y_ready")
        b_score = sem("b_score")
        b_max = sem("b_max")
        b_exp = sem("b_exp")
        b_prob = sem("b_prob")
        b_turn = sem("b_turn")
        b_tact = sem("b_tact")
        b_tdve = sem("b_tdve")
        m_dec = sem("m_dec")
        m_ck = sem("m_ck")
        m_state = sem("m_state")
        m_sact = sem("m_sact")
        m_rope = sem("m_rope")
        m_turn = sem("m_turn")
        m_tact = sem("m_tact")
        m_tdve = sem("m_tdve")
        m_w = sem("m_w")
        m_wd = sem("m_wd")
        m_s = sem("m_s")
        m_sd = sem("m_sd")
        m_o = sem("m_o")
        m_od = sem("m_od")
        q_rope = sem("q_rope")
        q_turn = sem("q_turn")
        q_tact = sem("q_tact")
        s_pe = sem("s_pe")
        s_max = sem("s_max")
        s_exp = sem("s_exp")
        s_prob = sem("s_prob")
        s_turn = sem("s_turn")
        s_tact = sem("s_tact")
        s_tdve = sem("s_tdve")

        def U(name):
            return 2 * BLOCKS[name][0]

        def halves(x, l, odd):
            s = 1 << l
            if odd is None:
                return x.rearrange("p (n s) -> p n s", s=s)
            return x.rearrange("p (n h s) -> p n h s", h=2, s=s)[:, :, odd]

        class ModulationSteps:

            def __init__(self, pe):
                self.pe, self.m = pe, 0

            def units(self, n):
                for _ in range(n):
                    m = self.m
                    g, k = m // KD, m % KD
                    if k == 0:
                        if g == 0:
                            self.pe.wait_ge(cond_ready, 1)
                        else:
                            self.pe.wait_ge(mod_act, g)
                    slot = (U("wo_a" if g < MOD_EARLY else "wo_c") + 4 + m) % RAW
                    self.pe.wait_ge(mod_in[m % RAW], 16 * (m // RAW + 1))
                    for c in range(2):
                        last = nc.tensor.matmul(ps[c][0:2, :], cact[:, k], raw[:, slot, c * 512:(c + 1) * 512],
                                                start=k == 0, stop=k == KD - 1)
                    last.then_inc(mod_used, 1)
                    self.m += 1

            def finish(self):
                g = self.m // KD - 1
                self.pe.wait_ge(mod_kept, g + 1)
                if g % 3 < 2:
                    for k in range(KD):
                        last = nc.tensor.matmul(ps[0][:, 2 * k:2 * k + 2], mrow[:, k * P:(k + 1) * P],
                                                ident[0:2, 0:2], start=True, stop=True)
                else:
                    for c in range(2):
                        last = nc.tensor.matmul(ps[c][:], K_["ones"][0:1, :], mrow[0:1, c * 512:(c + 1) * 512],
                                                start=True, stop=True)
                last.then_inc(mod_out, 1)

        block = ctx.enter_context(nc.Block())
        K_ = {n: cst[:, o:o + c] for n, (o, c) in CONSTS.items()}
        ident = K_["ident"]

        def col(name, k, n=1):
            return cols[:, COLS[name][0] + k:COLS[name][0] + k + n]

        @block.sync
        def _(sp):
            def unit(i, per, c, src, kk):
                if not (isinstance(i, int) and c < RAW):
                    sp.wait_ge(lo_done, i * per + (c - RAW + 1))
                dst = raw[:, c % RAW]
                if kk > 1:
                    dst = dst.rearrange("p (k n) -> p k n", k=kk)
                sp.dma_start(dst, src).then_inc(unit_in[c % RAW], 16)

            def feature_major(name, w, at):
                wk = w.rearrange("(k p) n -> p k n", p=P)

                def body(i, j):
                    for f in range(2):
                        unit(i, 8, U(name) + 2 * j + f, wk[:, :, bass.ds(at(i * 4 + j, f), P)], KD)
                turns(sp, BLOCKS[name][1], body)

            def modulation(first, last, c):
                for m in range(KD * first, KD * last):
                    n = m - KD * first
                    if n < RAW:
                        sp.wait_ge(lo_done, c + n - RAW + 1)
                    else:
                        sp.wait_ge(mod_used, m - RAW + 1)
                    g, k = m // KD, m % KD
                    sp.dma_start(raw[:, (c + n) % RAW],
                                 a["w_mod_2"][0][k * P:(k + 1) * P, g * D:(g + 1) * D]).then_inc(mod_in[m % RAW], 16)

            def token_major(name, w, c0, groups=None):
                wk = w.rearrange("(k p) n -> p k n", p=P)

                def body(i, j):
                    if groups and j == 2:
                        modulation(*groups, U(name) + 4)
                    for g in range(2):
                        if groups and j >= 2:
                            sp.wait_ge(mod_used, KD * groups[1] - RAW + 2 * (j - 2) + g + 1)
                        unit(i, 8, U(name) + 2 * j + g,
                             wk[:, 4 * g:4 * g + 4, bass.ds((i * 4 + j) * 256 + c0, 256)], 4)
                turns(sp, BLOCKS[name][1], body)

            def rows_of(name, w):
                wk = w.rearrange("(k p) n -> k p n", p=P)

                def body(i, j):
                    unit(i, 4, U(name) + j,
                         wk[one(i * 4 + j)].rearrange("a p n -> p (a n)"), 1)
                turns(sp, 2 * BLOCKS[name][1], body)

            def dump(which, n):
                sp.wait_ge(which, n)
                sp.dma_start(out.rearrange("o (t p) d -> p (o t) d", p=P), h[:]).then_inc(out_done, 16)
                sp.wait_ge(out_done, 16)

            sp.dma_start(h[:], a["x"].rearrange("o (t p) d -> p (o t) d", p=P)).then_inc(x_in, 16)
            feature_major("qkv", a["a_w_in"][0], lambda m, f: m * 256 + f * P)
            token_major("z", a["a_w_in"][0], 3 * D)
            token_major("wo_a", a["a_w_out"][0], 0, (0, MOD_EARLY))
            feature_major("up0", a["f_w_up"][0], lambda m, f: m * P + f * FF)
            rows_of("down0", a["f_w_down"][0])
            feature_major("k", a["w_kv"], lambda m, f: m * 256 + f * P)
            token_major("v", a["w_kv"], D)
            feature_major("q", a["b_w_q"][0], lambda m, f: m * 256 + f * P)
            token_major("wo_b", a["b_w_out"][0], 0)
            feature_major("up1", a["f_w_up"][1], lambda m, f: m * P + f * FF)
            rows_of("down1", a["f_w_down"][1])
            token_major("win", a["w_in_2"][0], 0)
            token_major("wo_c", a["w_out_2"][0], 0, (MOD_EARLY, MOD_GROUPS))
            feature_major("ff1", a["w_ff1_2"][0], lambda m, f: m * 256 + f * P)
            rows_of("ff2", a["w_ff2_2"][0])
            dump(res_done, RES["fin"])

        @block.tensor
        def _(pe):
            mm = nc.tensor.matmul

            def three(o, l, r, first, last, check=False):
                mm(o, l[0], r[0], start=first, stop=False, skip_group_check=check)
                mm(o, l[0], r[1], start=False, stop=False, skip_group_check=check)
                return mm(o, l[1], r[0], start=False, stop=last, skip_group_check=check)

            def bank(name, i, j):
                e = BANK[name] + j
                if not (isinstance(i, int) and e < 4):
                    pe.wait_ge(bank_free, i * 4 + (e - 3))
                return ps[e % 4]

            def w_unit(i, per, c):
                pe.wait_ge(lo_done, i * per + (c + 1))
                return [w[:, c % SPLIT] for w in (wH, wL)]

            def feature_major(name, x):
                def body(i, j):
                    b = bank(name, i, j)
                    for f in range(2):
                        w = [y.rearrange("p (k n) -> p k n", k=KD) for y in w_unit(i, 8, U(name) + 2 * j + f)]
                        for k in range(KD):
                            last = three(b[:, f * SEQ:(f + 1) * SEQ], [y[:, k] for y in w],
                                         [y[:, k] for y in x], k == 0, k == KD - 1)
                        last.then_inc(unit_done, 1)
                turns(pe, BLOCKS[name][1], body)

            def token_block(banks, i, c, xs):
                for g in range(2):
                    w = [y.rearrange("p (k n) -> p k n", k=4) for y in w_unit(i, 8, c + g)]
                    for b, x in zip(banks, xs):
                        for t in range(TT):
                            for k in range(4):
                                last = three(b[:, t * 256:(t + 1) * 256],
                                             [y[:, 4 * g + k, t * P:(t + 1) * P] for y in x],
                                             [y[:, k] for y in w], g == 0 and t == 0 and k == 0,
                                             g == 1 and k == 3, check=True)
                    last.then_inc(unit_done, 1)

            def token_major(name, x):
                turns(pe, BLOCKS[name][1],
                      lambda i, j: token_block([bank(name, i, j)], i, U(name) + 2 * j, [x]))

            def down(name, count):
                acc = [ps[AUX + 2 * t + c] for t in range(TT) for c in range(2)]

                def body(i, j):
                    w = w_unit(i, 4, U(name) + j)
                    pe.wait_ge(a_lo, i * 4 + (ACTS[name] + j + 1))
                    first, last = isinstance(i, int) and j == 0, isinstance(i, int) and j == count - 1
                    for t in range(TT):
                        for c in range(2):
                            done = three(acc[2 * t + c][:], [y[:, j % SPLIT, t * P:(t + 1) * P] for y in (aH, aL)],
                                         [y[:, c * 512:(c + 1) * 512] for y in w], first, last, check=True)
                    done.then_inc(unit_done, 1)
                turns(pe, count, body)

            def turn_rows(n):
                for t in range(TT):
                    pe.wait_ge(xn_done, 2 * TURN[n] + t + 1)
                    for k in range(KD):
                        o = (k % 2) * SEQ + t * P
                        tr = nc.tensor.transpose(ps[AUX + k // 2][:, o:o + P], xn[:, t, k * P:(k + 1) * P], ident)
                        if t == 1 and k % 2:
                            tr.then_inc(turned, 1)

            def ready(n):
                pe.wait_ge(x_ready, 2 * SCALED[n] + 2)


            mod = ModulationSteps(pe)

            def delta_front_pe():
                def sums():
                    pe.wait_ge(g_dve, 4)
                    for t in range(TT):
                        mm(ps[7][:, 8 * t:8 * t + 8], K_["tri"], sm[:, 10, 8 * t:8 * t + 8], start=True, stop=True)
                    mm(ps[7][:, 16:24], K_["ones"], sm[:, 10, 0:8], start=True, stop=True).then_inc(g_sum, 1)

                def square_sums():
                    pe.wait_ge(tok_sq, 2)
                    pe.wait_ge(g_dve, 5)
                    for t in range(TT):
                        for n in range(16):
                            sq = (T_, MT)[n // 8].rearrange("p (h t) n -> p h (t n)", t=TT)
                            last = mm(ps[7][:, 32 + 16 * t + n:33 + 16 * t + n], sq[:, n % 8, t * P:(t + 1) * P],
                                      K_["ones"][:, 0:1], start=True, stop=True)
                    last.then_inc(tok_ss, 1)

                def row(g):
                    pe.wait_ge(dg_dve, g + 1)
                    if g >= 2:
                        pe.wait_ge(arg_dve, g - 1)
                    mm(ps[AUX + g % 2][:], K_["ones"], dG[g % 2].rearrange("p a b -> p (a b)"),
                       start=True, stop=True).then_inc(row_pe, 1)

                def to_tok(q):
                    bank, free = TOK_BANK[q]
                    for which, n in free:
                        pe.wait_ge({"act": tok_act, "dve": tok_dve, "arg": arg_dve, "pw": pw_in}[which], n)
                    f0, t = TOK_HEAD[q]
                    for f in range(4):
                        tr = nc.tensor.transpose(ps[bank][:, f * P:(f + 1) * P],
                                                 feat[:, f0 + f, t * P:(t + 1) * P], ident)
                    tr.then_inc(tok_pe, 1)

                def to_feat(q):
                    h0 = BACK_HEAD[q]
                    pe.wait_ge(tok_dve, 4 if h0 >= 8 else 8)
                    if q < 4:
                        pe.wait_ge(tok_dve, 5 + q)
                    else:
                        pe.wait_ge((back_act, back_dve)[q % 2], q // 2 - 1)
                    for f in range(2):
                        for t in range(TT):
                            tr = nc.tensor.transpose(ps[AUX + q % 4][:, f * SEQ + t * P:f * SEQ + (t + 1) * P],
                                                     tok[:, t, h0 + f], ident)
                    tr.then_inc(back_pe, 1)

                def z(j):
                    token_block([bank("z", 0, j)], 0, U("z") + 2 * j, [X])
                sums()
                z(0)
                square_sums()
                row(0)
                row(1)
                to_tok(0)
                to_tok(1)
                z(1)
                row(2)
                row(3)
                for q in range(2, 6):
                    to_tok(q)
                z(2)
                for q in range(6, 10):
                    to_tok(q)
                z(3)
                to_tok(10)
                to_tok(11)
                for q in range(8):
                    to_feat(q)

            def delta_pe():
                pe.wait_ge(bank_free, BANK["z"] + 4)
                mod.units(4)
                pe.wait_ge(back_act, 4)
                pe.wait_ge(back_dve, 4)

                def products(g):
                    t, h0 = g // 2, 4 * (g % 2)
                    if g >= 2:
                        pe.wait_ge(at_dve, g - 1)
                    for x in range(4):
                        k = feat[:, 8 + h0 + x, t * P:(t + 1) * P]
                        mm(ps[4 + g % 2][:, x * P:(x + 1) * P], k, k, start=True, stop=True)
                        last = mm(ps[6 + g % 2][:, x * P:(x + 1) * P], k, feat[:, h0 + x, t * P:(t + 1) * P],
                                  start=True, stop=True)
                    last.then_inc(kq_pe, 1)

                def turn_m(g):
                    pe.wait_ge(m_dve, g + 1)
                    if g >= 2:
                        pe.wait_ge(mt_act, g - 1)
                    for x in range(4):
                        tr = nc.tensor.transpose(ps[2 + g % 2][:, x * P:(x + 1) * P], T_[:, 4 * g + x], ident)
                    tr.then_inc(mt_pe, 1)
                products(0)
                for g in range(1, 4):
                    products(g)
                    turn_m(g - 1)
                turn_m(3)
                mod.units(4)

                for l in range(LEVELS):
                    for step in range(3):
                        if l == LEVELS - 1 and step == 1:
                            continue
                        for g in range(4):
                            k = l * 12 + step * 4 + g
                            pe.wait_ge(dbl_dve, max(k + 1 - (4 if l == LEVELS - 1 and step == 2 else 0), 4))
                            for x in range(4 * g, 4 * g + 4):
                                lhs, rhs = ((MT, T_), (U_, P_), (P_, U_))[step]
                                o = ps[AUX + g][:, (x % 4) * P:(x % 4 + 1) * P]
                                if step == 0:
                                    last = mm(o, lhs[:, x], rhs[:, x], start=True, stop=True)
                                else:
                                    last = mm(halves(o[:, 0:64], l + 1, None), lhs[:, x], halves(rhs[:, x], l + 1, step - 1),
                                              start=True, stop=True)
                            last.then_inc(dbl_pe, 1)

                def heads(bank, lhs, rhs):
                    for hb in range(2):
                        for x in range(4):
                            n = 4 * hb + x
                            last = mm(ps[bank + hb][:, x * P:(x + 1) * P], lhs(n), rhs(n), start=True, stop=True)
                        last.then_inc(scan_pe, 1)
                pe.wait_ge(dbl_dve, 12 * LEVELS)
                pe.wait_ge(scan_dve, 1)
                heads(4, lambda n: U_[:, n], lambda n: tok[:, 0, 16 + n])
                mod.finish()
                pe.wait_ge(scan_act, 2)
                pe.wait_ge(scan_dve, 2)
                heads(6, lambda n: tok[:, 0, 8 + n], lambda n: P_[:, n])
                mod.units(1)
                pe.wait_ge(scan_act, 4)
                heads(4, lambda n: feat[:, 8 + n, P:2 * P], lambda n: T_[:, n])
                heads(6, lambda n: feat[:, n, P:2 * P], lambda n: T_[:, n])
                mod.units(1)
                pe.wait_ge(scan_dve, 4)
                heads(4, lambda n: AT[:, n], lambda n: P_[:, n])
                pe.wait_ge(scan_dve, 7)
                mod.units(1)
                heads(6, lambda n: U_[:, 8 + n], lambda n: T_[:, 8 + n])
                mod.units(1)
                pe.wait_ge(scan_act, 8)
                heads(4, lambda n: AT[:, 8 + n], lambda n: P_[:, 8 + n])
                mod.units(4)
                mod.finish()
                mod.units(8)
                pe.wait_ge(y_rows, 1)
                for b in range(4):
                    for k in range(2 * b, 2 * b + 2):
                        for t in range(TT):
                            o = (k % 2) * SEQ + t * P
                            tr = nc.tensor.transpose(ps[AUX + b][:, o:o + P], tok[:, t, k], ident)
                    tr.then_inc(y_pe, 1)
                mod.finish()

            def band_pe():
                pe.wait_ge(bank_free, BANK["q"] + 4)
                pe.wait_ge(slab_masked, 1)

                def scores(g):
                    if g:
                        pe.wait_ge(b_max, g)
                    for x in range(4):
                        n, r, o = 4 * g + x, 64 * (x % 2), x // 2
                        q, k = qT[r:r + 64, n // 2], kT[r:r + 64, n // 2]
                        mm(ps[4 + x % 2][:, o * 256:(o + 1) * 256], q[:, P:], k, start=True, stop=True)
                        last = mm(ps[6 + x % 2][:, o * P:(o + 1) * P], q[:, 0:P], k[:, 0:P], start=True, stop=True)
                    last.then_inc(b_score, 1)
                scores(0)
                scores(1)
                for g in range(4):
                    pe.wait_ge(b_prob, g + 1)
                    for d in range(3):
                        if g:
                            pe.wait_ge((b_tact, b_tdve)[d % 2], (2 * g, g)[d % 2])
                        for x in (range(2 * d, 2 * d + 2) if d < 2 else range(4)):
                            for o, c in (((0, 256), (P, 0)) if d < 2 else ((2 * P, P),)):
                                at = (x % 2) * 256 + o if d < 2 else x * P
                                tr = nc.tensor.transpose(ps[d][:, at:at + P], p_b[:, g % 2, x, c:c + P], ident)
                        tr.then_inc(b_turn, 1)
                    if g < 2:
                        scores(g + 2)
                    pe.wait_ge(b_tact, 2 * g + 2)
                    pe.wait_ge(b_tdve, g + 1)
                    if g:
                        pe.wait_ge(y_ready, 4 + g)
                    for x in range(4):
                        n, r, o = 4 * g + x, 64 * (x % 2), (x // 2) * SEQ
                        mm(ps[3][r:r + 64, o:o + SEQ], vt[:, 0, n * BH:(n + 1) * BH], pT_b[:, g % 2, x, 0:256],
                           start=True, stop=False)
                        last = mm(ps[3][r:r + 64, o + P:o + SEQ], vt[:, 1, n * BH:(n + 1) * BH],
                                  pT_b[:, g % 2, x, 256:384], start=False, stop=True)
                    last.then_inc(y_pe, 1)

            def mix_pe():
                pe.wait_ge(m_ck, 4)
                pe.wait_ge(bank_free, BANK["wo_c"])
                mod.units(5)
                for d in range(2):
                    for n in range(RET_H):
                        for t in range(TT):
                            last = mm(ps[4 + d][:, n * P:(n + 1) * P], rope[:, t, d * 512 + n * P:d * 512 + (n + 1) * P],
                                      ckv[:, t, 512 + n * P:512 + (n + 1) * P], start=t == 0, stop=t == 1)
                    last.then_inc(m_state, 1)
                mod.units(3)
                pe.wait_ge(m_sact, 2)
                pe.wait_ge(m_rope, 2)
                for b in range(4):
                    for f in range(2):
                        for t in range(TT):
                            o = f * SEQ + t * P
                            tr = nc.tensor.transpose(ps[AUX + b][:, o:o + P],
                                                     rope[:, t, (2 * b + f) * P:(2 * b + f + 1) * P], ident)
                    tr.then_inc(m_turn, 1)
                mod.finish()
                pe.wait_ge(m_tact, 2)
                pe.wait_ge(m_tdve, 2)
                for n in range(RET_H):
                    for j in range(TT):
                        last = mm(ps[4][:, j * SEQ:(j + 1) * SEQ], rkT[:, n, j * P:(j + 1) * P], rqT[:, n],
                                  start=True, stop=True)
                    last.then_inc(m_s, 1)
                    mod.units(2)
                    pe.wait_ge(m_sd, n + 1)
                    if n:
                        pe.wait_ge(m_od, n)
                    for t in range(TT):
                        for j in range(TT):
                            mm(ps[6][:, t * P:(t + 1) * P], sT[:, n % 2, j * SEQ + t * P:j * SEQ + (t + 1) * P],
                               rv[:, j, n * P:(n + 1) * P], start=j == 0, stop=j == 1)
                    for d in range(2):
                        for t in range(TT):
                            o = ps[6 + d][:, 256 * (1 - d) + t * P:256 * (1 - d) + (t + 1) * P]
                            last = mm(o, rqT[:, n, t * P:(t + 1) * P], s_fb[:, d, n], start=True, stop=True)
                    last.then_inc(m_o, 1)
                mod.finish()
                mod.units(8)
                pe.wait_ge(y_rows, 2)
                for b in range(2):
                    for f in range(2):
                        for t in range(TT):
                            o = f * SEQ + t * P
                            tr = nc.tensor.transpose(ps[4 + b][:, o:o + P], o_r[:, t, 2 * b + f], ident)
                    tr.then_inc(y_pe, 1)
                mod.finish()
                pe.wait_ge(q_rope, 2)
                pe.wait_ge(y_ready, 10)
                for b in range(2):
                    for f in range(2):
                        for t in range(TT):
                            o = f * SEQ + t * P
                            w = 2 * (2 * b + f)
                            tr = nc.tensor.transpose(ps[4 + b][:, o:o + P], aqn[:, t, w:w + 2].rearrange("p a b -> p (a b)"), ident)
                    tr.then_inc(q_turn, 1)
                for t in range(TT):
                    nc.tensor.transpose(ps[6][:, t * P:(t + 1) * P], kcn[:, t].rearrange("p a b -> p (a b)"), ident)
                    tr = nc.tensor.transpose(ps[6][:, SEQ + t * P:SEQ + (t + 1) * P],
                                             aqn[:, t, 8:10].rearrange("p a b -> p (a b)"), ident)
                tr.then_inc(q_turn, 1)
                pe.wait_ge(q_tact, 3)

                pe.wait_ge(mod_act, MOD_GROUPS)

                def scores(j):
                    if j:
                        pe.wait_ge(s_exp, 4 * j)
                    for s in range(2):
                        for t in range(TT):
                            mm(ps[4 + 2 * s + t][:], aqT[64 * s:64 * s + 64, j, t * P:(t + 1) * P],
                               akT[64 * s:64 * s + 64], start=True, stop=True).then_inc(s_pe, 1)
                scores(0)
                for j in range(4):
                    for n in ATT_BANKS:
                        s, kp = n // 2, n % 2
                        pe.wait_ge(s_prob, 4 * j + 2 * s + 2)
                        if j and n == 0:
                            pe.wait_ge(y_ready, 10 + j)
                        for k in range(2):
                            for t in range(TT):
                                o, c = k * SEQ + t * P, (2 * kp + k) * P
                                tr = nc.tensor.transpose(ps[n][:, o:o + P], ap_[:, s, t, c:c + P], ident)
                        tr.then_inc(s_turn, 1)
                    if j < 3:
                        scores(j + 1)
                    pe.wait_ge(s_tact, 2 * j + 2)
                    pe.wait_ge(s_tdve, 2 * j + 2)
                    r = 64 * (j % 2)
                    for s in range(2):
                        for k in range(4):
                            v = (cakv[:, k, P + 64 * s:P + 64 * s + 64] if k < 2
                                 else aqkv[:, k - 2, 640 + 64 * s:704 + 64 * s])
                            last = mm(ps[0][r:r + 64, s * SEQ:(s + 1) * SEQ], v, apT[:, s, k], start=k == 0, stop=k == 3)
                    last.then_inc(y_pe, 1)

            X = [xH, xL]
            pe.wait_ge(consts_in, 48)
            turn_rows("a")
            ready("a")
            pe.wait_ge(c_ready, 1)
            for t in range(TT):
                for k in range(KD):
                    last = three(ps[AUX + 1][:, 16 * t:16 * t + 16], [y[:, k, t * P:(t + 1) * P] for y in X],
                                 [baH[:, k], baL[:, k]], k == 0, k == KD - 1)
            last.then_inc(ba_done, 1)
            feature_major("qkv", X)
            delta_front_pe()
            delta_pe()
            pe.wait_ge(y_ready, 4)
            pe.wait_ge(mod_act, MOD_EARLY)
            token_major("wo_a", X)
            turn_rows("f0")
            ready("f0")
            feature_major("up0", X)
            down("down0", F_TILES)
            turn_rows("kv")
            ready("kv")
            feature_major("k", X)
            token_major("v", X)
            ready("q")
            feature_major("q", [x2H, x2L])
            band_pe()
            pe.wait_ge(y_ready, 8)
            token_major("wo_b", X)
            turn_rows("f1")
            ready("f1")
            feature_major("up1", X)
            down("down1", F_TILES)
            turn_rows("ctx")
            ready("ctx")
            turn_rows("n1")
            ready("n1")
            e = BANK["win"]
            for m in range(11):
                xs = [X, [xcH, xcL]] if m in CTX_BLOCKS else [X]
                pe.wait_ge(bank_free, e + len(xs) - 4)
                token_block([ps[(e + y) % 4] for y in range(len(xs))], 0, U("win") + 2 * m, xs)
                e += len(xs)
            mix_pe()
            pe.wait_ge(y_ready, 8 + 2 + 4)
            token_major("wo_c", X)
            turn_rows("n2")
            ready("n2")
            feature_major("ff1", X)
            down("ff2", FF2_TILES)

        @block.scalar
        def _(act):
            st = Steps(act, act_s)
            fn = nc.scalar.activation

            def hi(i, per, c):
                if isinstance(i, int) and c >= UNITS:
                    return
                act.wait_ge(unit_in[c % RAW], i * (16 * per // RAW) + 16 * (c // RAW + 1))
                if not (isinstance(i, int) and c < SPLIT):
                    act.wait_ge(unit_done, i * per + (c - SPLIT + 1))
                fn(wH[:, c % SPLIT], raw[:, c % RAW], ACT.Copy).then_inc(hi_done, 1)

            def ahead(i, c):
                hi(i, 8, c + SPLIT)
                hi(i, 8, c + SPLIT + 1)

            def blocks(name, evacuate, after=None):
                def body(i, j):
                    act.wait_ge(unit_done, i * 8 + (U(name) + 2 * j + 2))
                    evacuate(i, j, ps[(BANK[name] + j) % 4]).then_inc(bank_free, 1)
                    ahead(i, U(name) + 2 * j)
                    if after:
                        after(i, j)
                turns(act, BLOCKS[name][1], body)

            def staging(name, func=ACT.Copy, after=None):
                def body(i, j):
                    n = STAGED[name] + j
                    act.wait_ge(unit_done, i * 8 + (U(name) + 2 * j + 2))
                    if not (isinstance(i, int) and n < 2):
                        act.wait_ge(unstaged, i * 4 + (n - 1))
                    b = ps[(BANK[name] + j) % 4]
                    fn(stage[:, n % 2].rearrange("p a b -> p (a b)"), b[:], func).then_inc(bank_free, 1)
                    ahead(i, U(name) + 2 * j)
                    if after:
                        after(i, j)
                turns(act, BLOCKS[name][1], body)

            def down(name, count):
                def part(i, j):
                    m = j + SPLIT
                    act.wait_ge(unit_done, i * 4 + (U(name) + j + 1))
                    fn(aH[:, m % SPLIT], act_a[:, one(i * 4 + m)].rearrange("p a n -> p (a n)"),
                       ACT.Copy).then_inc(a_hi, 1)

                def body(i, j):
                    hi(i, 4, U(name) + j + SPLIT)
                    part(i, j)
                def made(m):
                    if name == "ff2":
                        act.wait_ge(unstaged, STAGED["ff1"] + m // 2 + 1)
                    else:
                        act.wait_ge(prod_done, PRODS[name] + m + 1)
                for m in range(SPLIT):
                    made(m)
                    fn(aH[:, m], act_a[:, m], ACT.Copy).then_inc(a_hi, 1)
                made(count - 1)
                turns(act, count - SPLIT, body)
                for j in range(count - SPLIT, count):
                    hi(0, 4, U(name) + j + SPLIT)

            def squares(n, src):
                for t in range(TT):
                    fn(xn[:, t], src[:, t], ACT.Square, accum_out=ssq[:, t:t + 1]).then_inc(sq_done, 1)

            def scaled(n, turn, gain, bias, oH):
                e = SCALED[n]
                act.wait_ge(turned, 4 * TURN[turn] + 2)
                if e:
                    act.wait_ge(x_ready, 2 * e)
                for k in range(4):
                    s = st.put(fn(xv[:, k], ps[AUX + k // 2][:, (k % 2) * SEQ:(k % 2 + 1) * SEQ],
                                  ACT.Identity, scale=gain(k), bias=bias(k)))
                st.wait(s)
                fn(oH[:, 0:4], xv[:, 0:4], ACT.Copy).then_inc(x_hi, 1)
                act.wait_ge(val_dve, 4 * (e + 1))
                fn(oH[:, 4:8], xv[:, 4:8], ACT.Copy).then_inc(x_hi, 1)

            def no(k):
                return 0.0

            def cp(o, i, **kw):
                return fn(o, i, ACT.Copy, **kw)

            def gates_act():
                act.wait_ge(g_dve, 1)
                ba = sm[:, 12:14, 0:16]
                fn(sm[:, 2, 0:16].rearrange("p (t n) -> p t n", t=TT), ba[:, :, 0:8], ACT.Exp, scale=-1.0)
                fn(sm[:, 14, 0:8], rows_a[:, 128:136], ACT.Exp)
                fn(sm[:, 15, 0:8], rows_a[:, 144:152], ACT.Exp).then_inc(g_act, 1)
                act.wait_ge(g_dve, 2)
                fn(sm[:, 4, 0:16], sm[:, 3, 0:16], ACT.Exp).then_inc(g_act, 1)
                act.wait_ge(g_dve, 3)
                fn(sm[:, 6], sm[:, 5], ACT.Ln).then_inc(g_act, 1)

            def mod_keep():
                g = mods[0]
                act.wait_ge(mod_used, KD * (g + 1))
                if g:
                    act.wait_ge(mod_out, g)
                fn(mrow[:, 0:512], ps[0][0:2, :], ACT.Copy)
                fn(mrow[:, 512:], ps[1][0:2, :], ACT.Copy).then_inc(mod_kept, 1)

            def mod_place():
                g = mods[0]
                act.wait_ge(mod_out, g + 1)
                if g % 3 < 2:
                    o = 8 * (g if g < 3 else g - 1)
                    last = fn(modc[:, o:o + 8], ps[0][:, 0:16].rearrange("p (k c) -> p k c", c=2), ACT.Copy)
                else:
                    gate = gate1 if g < 3 else gate2
                    fn(gate[:, 0:512], ps[0][:], ACT.Copy)
                    last = fn(gate[:, 512:], ps[1][:], ACT.Copy)
                last.then_inc(mod_act, 1)
                mods[0] += 1
            mods = [0]

            def delta_front_act():
                act.wait_ge(silu_done, 12)
                fq = feat[:].rearrange("p h n -> p (h n)")
                for x, o in enumerate((T_, MT)):
                    fn(o[:].rearrange("p h n -> p (h n)"), fq[:, x * 2048:(x + 1) * 2048], ACT.Square).then_inc(tok_sq, 1)

                def z(j):
                    act.wait_ge(unit_done, U("z") + 2 * j + 2)
                    fn(zs[:, :, j * 256:(j + 1) * 256], ps[(BANK["z"] + j) % 4][:].rearrange("p (t n) -> p t n", t=TT),
                       ACT.Silu).then_inc(bank_free, 1)
                    ahead(0, U("z") + 2 * j)

                def decays(g):
                    act.wait_ge(arg_dve, g + 1)
                    fn(U_[:, 4 * g:4 * g + 4], U_[:, 4 * g:4 * g + 4], ACT.Exp)
                    fn(AT[:, 4 * g:4 * g + 4], AT[:, 4 * g:4 * g + 4], ACT.Exp).then_inc(exp_act, 1)

                def v_tok(q):
                    f0, t = TOK_HEAD[q]
                    act.wait_ge(tok_pe, q + 1)
                    cp(tok[:, t, f0:f0 + 4].rearrange("p a b -> p (a b)"), ps[TOK_BANK[q][0]][:]).then_inc(tok_act, 1)
                z(0)
                act.wait_ge(g_dve, 5)
                fn(sm[:, 17, 0:16], sm[:, 16, 0:16], ACT.Exp)
                fn(sm[:, 19, 0:8], sm[:, 18, 0:8], ACT.Exp).then_inc(g_act, 1)
                decays(0)
                decays(1)
                v_tok(0)
                v_tok(1)
                z(1)
                decays(2)
                decays(3)
                v_tok(2)
                v_tok(3)
                z(2)
                z(3)
                for q in range(0, 8, 2):
                    act.wait_ge(back_pe, q + 1)
                    cp(feat[:, BACK_HEAD[q]:BACK_HEAD[q] + 2].rearrange("p a b -> p (a b)"),
                       ps[AUX + q % 4][:]).then_inc(back_act, 1)

            def delta_act():
                for g in range(4):
                    act.wait_ge(mt_pe, g + 1)
                    cp(MT[:, 4 * g:4 * g + 4].rearrange("p a b -> p (a b)"), ps[2 + g % 2][:]).then_inc(mt_act, 1)
                mod_keep()

                def banks(first, bank, o):
                    for hb in range(2):
                        act.wait_ge(scan_pe, first + hb)
                        cp(o(4 * hb), ps[bank + hb][:].rearrange("p (a b) -> p a b", a=4)).then_inc(scan_act, 1)
                banks(1, 4, lambda n: P_[:, n:n + 4])
                mod_place()
                banks(3, 6, lambda n: T_[:, n:n + 4])
                banks(9, 4, lambda n: tok[:, 0, n:n + 4])
                banks(11, 6, lambda n: P_[:, 8 + n:12 + n])
                mod_keep()
                mod_place()
                mod_keep()
                for b in range(4):
                    act.wait_ge(y_pe, b + 1)
                    cp(xH[:, 2 * b:2 * b + 2].rearrange("p a b -> p (a b)"), ps[AUX + b][:]).then_inc(y_hi, 1)
                mod_place()

            def band_act():
                def exps(g):
                    b = g % 2
                    act.wait_ge(b_max, g + 1)
                    for x in range(4):
                        for t in range(TT):
                            c = slice(0, 256) if t else slice(256, 384)
                            e = fn(p_b[:, b, x, c], p_b[:, b, x, c], ACT.Exp, bias=st_b[:, b, 1, 2 * x + t:2 * x + t + 1],
                                   accum_out=st_b[:, b, 2, 2 * x + t:2 * x + t + 1])
                            e.then_inc(b_exp, 1)
                exps(0)
                for g in range(4):
                    if g < 3:
                        exps(g + 1)
                    act.wait_ge(b_turn, 3 * g + 1)
                    cp(pT_b[:, g % 2, 0:2, 0:256], ps[0][:].rearrange("p (x n) -> p x n", x=2)).then_inc(b_tact, 1)
                    act.wait_ge(b_turn, 3 * g + 3)
                    cp(pT_b[:, g % 2, :, 256:384], ps[2][:].rearrange("p (x n) -> p x n", x=4)).then_inc(b_tact, 1)
                    act.wait_ge(y_pe, 4 + g + 1)
                    cp(xH[:, 2 * g:2 * g + 2].rearrange("p a b -> p (a b)"), ps[3][:]).then_inc(y_hi, 1)

            def mix_act():
                for k in range(4):
                    for t in range(TT):
                        o = TABLES["pos"][0] + 2 * k + t
                        e = fn(dec[:, k, t], lg[:, 4 * (k % 2):4 * (k % 2) + 4], ACT.Exp, scale=tb[:, o:o + 1])
                e.then_inc(m_dec, 1)
                for d in range(2):
                    act.wait_ge(m_state, d + 1)
                    cp(s_fb[:, d].rearrange("p a b -> p (a b)"), ps[4 + d][:], scale=HK ** -0.5).then_inc(m_sact, 1)
                mod_keep()
                for b in (0, 2):
                    act.wait_ge(m_turn, b + 1)
                    o = rkT if b else rqT
                    cp(o[:, 0:2].rearrange("p a b -> p (a b)"), ps[AUX + b][:]).then_inc(m_tact, 1)
                mod_place()
                act.wait_ge(m_rope, 2)
                for n in range(RET_H):
                    if n:
                        act.wait_ge(m_sd, n)
                    for d, name in enumerate(("fwd", "bwd")):
                        o = TABLES[name][0]
                        e = fn(wt[:, d], tb[:, o:o + 512], ACT.Exp, scale=lg[:, 4 * d + n:4 * d + n + 1])
                    e.then_inc(m_w, 1)
                mod_keep()
                mod_place()
                mod_keep()
                for b in range(2):
                    act.wait_ge(y_pe, 8 + b + 1)
                    cp(xH[:, 2 * b:2 * b + 2].rearrange("p a b -> p (a b)"), ps[4 + b][:]).then_inc(y_hi, 1)
                mod_place()
                for b in range(2):
                    act.wait_ge(q_turn, b + 1)
                    cp(aqT[:, 2 * b:2 * b + 2].rearrange("p a b -> p (a b)"), ps[4 + b][:]).then_inc(q_tact, 1)
                act.wait_ge(q_turn, 3)
                cp(akT[:], ps[6][:]).then_inc(q_tact, 1)
                def exps(j):
                    for s in range(2):
                        for t in range(TT):
                            n = 2 * s + t
                            act.wait_ge(s_max, 4 * j + n + 1)
                            if j:
                                act.wait_ge(s_turn, 4 * j)
                            fn(ap_[:, s, t], ps[4 + n][:], ACT.Exp, bias=st_p[:, 1, n:n + 1], scale=ATT_D ** -0.5,
                               accum_out=st_p[:, 2, n:n + 1]).then_inc(s_exp, 1)
                exps(0)
                for j in range(4):
                    for x in (1, 3):
                        n = ATT_BANKS[x]
                        act.wait_ge(s_turn, 4 * j + x + 1)
                        cp(apT[:, n // 2, 2 * (n % 2):2 * (n % 2) + 2].rearrange("p a b -> p (a b)"),
                           ps[n][:]).then_inc(s_tact, 1)
                    if j < 3:
                        exps(j + 1)
                    act.wait_ge(y_pe, 10 + j + 1)
                    r = 64 * (j % 2)
                    cp(xH[r:r + 64, 4 + j // 2:8:2], ps[0][r:r + 64].rearrange("p (a b) -> p a b", a=2)).then_inc(y_hi, 1)

            act.dma_start(cols[:], a["cols"]).then_inc(consts_in, 16)
            act.dma_start(cst[:], a["consts"]).then_inc(consts_in, 16)
            act.dma_start(rows_a[:], a["rows_a"].partition_broadcast(P).rearrange("p a n -> p (a n)")).then_inc(consts_in, 16)
            act.dma_start(baw[:], a["a_w_in"][0].rearrange("(k p) n -> p k n", p=P)[:, :, 4 * D:4 * D + 16]).then_inc(early_in, 16)
            act.wait_ge(x_in, 16)
            squares("a", h)
            act.wait_ge(consts_in, 48)
            fn(cact[:].rearrange("p k a -> p a k"), col("c", 0, 16).rearrange("p (a k) -> p a k", a=2),
               ACT.Silu).then_inc(cond_ready, 1)
            act.wait_ge(early_in, 16)
            ba_steps = st.put(fn(baH[:], baw[:], ACT.Copy))
            assert ba_steps == 1
            for c in range(SPLIT):
                hi(0, 0, c)
            scaled("a", "a", lambda k: col("a_norm", k), no, xH)
            gates_act()

            def silu_a(i, j):
                n = STAGED["qkv"] + j
                act.wait_ge(unstaged, i * 4 + (n + 1))
                fn(feat[:, bass.ds((i * 4 + j) * 2, 2)], cv[:, n % 2], ACT.Silu).then_inc(silu_done, 1)
            staging("qkv", after=silu_a)
            delta_front_act()
            delta_act()
            staging("wo_a")

            def silu_f(which):
                def after(i, j):
                    n = STAGED[which] + j
                    act.wait_ge(unstaged, i * 4 + (n + 1))
                    fn(cv[:, n % 2, 0], cv[:, n % 2, 0], ACT.Silu).then_inc(silu_done, 1)
                return after

            def ffn(l):
                n = f"f{l}"
                squares(n, h)
                scaled(n, n, lambda k: col(f"f_norm{l}", k), no, xH)
                staging(f"up{l}", after=silu_f(f"up{l}"))
                down(f"down{l}", F_TILES)
            act.wait_ge(unstaged, STAGED["wo_a"] + 4)
            ffn(0)
            act.wait_ge(res_done, RES["down0"])
            squares("kv", h)
            scaled("kv", "kv", lambda k: col("kv_norm", k), no, xH)
            scaled("q", "kv", lambda k: col("b_norm", k), no, x2H)

            def two(buf, scale=1.0):
                return lambda i, j, b: fn(buf[:, bass.ds((i * 4 + j) * 2, 2)], b[:].rearrange("p (f n) -> p f n", f=2),
                                          ACT.Copy, scale=scale)
            blocks("k", two(kT))
            blocks("v", lambda i, j, b: fn(vt[:, :, bass.ds((i * 4 + j) * 256, 256)],
                                           b[:].rearrange("p (t n) -> p t n", t=TT), ACT.Copy))
            blocks("q", two(qT, BH ** -0.5))
            band_act()
            staging("wo_b")
            act.wait_ge(unstaged, STAGED["wo_b"] + 4)
            ffn(1)
            act.wait_ge(res_done, RES["down1"])
            squares("x2", h)
            act.wait_ge(late_in, 80)
            act.wait_ge(res_done, RES["x2"])
            squares("ctx", ctx_in)
            scaled("ctx", "ctx", lambda k: gs1[:, k, 1:2], lambda k: modc[:, k, 1:2], xcH)
            squares("n1", h)
            scaled("n1", "n1", lambda k: gs1[:, k, 0:1], lambda k: modc[:, k, 0:1], xH)
            e = BANK["win"]
            for m in range(11):
                act.wait_ge(unit_done, U("win") + 2 * m + 2)
                b = ps[e % 4][:].rearrange("p (t n) -> p t n", t=TT)
                if m < 4:
                    o, f = qk_t[:, :, m * 256:(m + 1) * 256], ACT.Copy
                elif m < 6:
                    o, f = rv[:, :, (m - 4) * 256:(m - 3) * 256], ACT.Copy
                elif m < 8:
                    o, f = sg[:, :, (m - 6) * 256:(m - 5) * 256], ACT.Silu
                else:
                    o, f = aqkv[:, :, (m - 8) * 256:(m - 7) * 256], ACT.Copy
                fn(o, b, f).then_inc(bank_free, 1)
                e += 1
                if m in CTX_BLOCKS:
                    b = ps[e % 4][:].rearrange("p (t n) -> p t n", t=TT)
                    o = cakv[:] if m == 10 else ckv[:, :, (m - 2) * 256:(m - 1) * 256]
                    fn(o, b, ACT.Copy).then_inc(bank_free, 1)
                    e += 1
                ahead(0, U("win") + 2 * m)
            mix_act()
            staging("wo_c")
            act.wait_ge(unstaged, STAGED["wo_c"] + 4)
            squares("n2", h)
            scaled("n2", "n2", lambda k: gs2[:, k:k + 1], lambda k: modc[:, 16 + k, 0:1], xH)
            staging("ff1", func=ACT.Relu)
            down("ff2", FF2_TILES)
            act.wait_ge(res_done, RES["ff2"])
            squares("fin", h)

        @block.gpsimd
        def _(pool):
            def inverse_root(o, i):
                return nc.gpsimd.tensor_tensor(o, i, mhalf[:, 0:i.shape[1]], ALU.pow)

            nc.gpsimd.memset(mhalf[:], -0.5).then_inc(pool_s, 1)
            pool.wait_ge(pool_s, 1)

            def norm(n):
                pool.wait_ge(ms_done, STAT[n] + 1)
                inverse_root(rstd[:], msq[:]).then_inc(rstd_done, 1)

            norm("a")
            pool.wait_ge(pw_in, 1)
            inverse_root(r32[:, 1], r32[:, 0]).then_inc(pw_out, 1)
            pool.wait_ge(pw_in, 2)
            inverse_root(r32[:, 1, 0:16], r32[:, 0, 0:16]).then_inc(pw_out, 1)
            pool.wait_ge(unstaged, STAGED["wo_a"] + 4)
            rb = a["b_rel_bias"]
            pool.dma_start(slab[:], bass.AP(tensor=rb.tensor, offset=P + 1, ap=[[1, P], [513, B_HEADS], [1, SEQ]])).then_inc(slab_in, 16)
            pool.wait_ge(slab_in, 16)
            nc.gpsimd.memset(slab[0:64, :, 0:64], NEG).then_inc(slab_masked, 1)
            norm("f0")
            norm("kv")
            norm("f1")
            pool.wait_ge(res_done, RES["down1"])
            pool.dma_start(row_f1[:], a["rows_c"][:, 0:1024].partition_broadcast(P).rearrange("p a n -> p (a n)")).then_inc(late_in, 16)
            pool.dma_start(ctx_in[:], a["ctx_2"].rearrange("o (t p) d -> p (o t) d", p=P)).then_inc(late_in, 16)
            pool.dma_start(tb[:], a["tables"]).then_inc(late_in, 16)
            pool.dma_start(rows_c[:], a["rows_c"][:, 1024:1664].partition_broadcast(P).rearrange("p a n -> p (a n)")).then_inc(late_in, 16)
            pool.dma_start(bmrow[:], a["rows_m"].partition_broadcast(P).rearrange("p a n -> p (a n)")).then_inc(late_in, 16)
            norm("x2")
            norm("ctx")
            norm("n1")
            pool.wait_ge(pw_in, 3)
            inverse_root(st_r[:, 3], st_r[:, 2]).then_inc(pw_out, 1)
            pool.wait_ge(pw_in, 4)
            for t in range(TT):
                last = inverse_root(st_a[:, t, 1], st_a[:, t, 0])
            last.then_inc(pw_out, 1)
            pool.wait_ge(unstaged, STAGED["wo_c"] + 4)
            pool.dma_start(rows_f[:], a["rows_c"][:, 1664:2688].partition_broadcast(P).rearrange("p a n -> p (a n)")).then_inc(final_in, 16)
            norm("n2")
            norm("fin")

        @block.vector
        def _(dve):
            st = Steps(dve, dve_s)
            tt = nc.vector.tensor_tensor
            ts = nc.vector.tensor_scalar
            stt = nc.vector.scalar_tensor_tensor

            def bc(x, n):
                return x.unsqueeze(2).broadcast_to([x.shape[0], x.shape[1], n])

            def rep(x, n):
                return x.unsqueeze(1).broadcast_to([x.shape[0], n, x.shape[1]])

            def four(x):
                return x.rearrange("p (a b) -> p a b", a=4)

            def rest(o, x, hi):
                return tt(o, x, hi.bitcast(F32), ALU.subtract)

            def lo(i, per, c):
                if isinstance(i, int) and c >= UNITS:
                    return
                dve.wait_ge(hi_done, i * per + (c + 1))
                rest(wL[:, c % SPLIT], raw[:, c % RAW], wH[:, c % SPLIT]).then_inc(lo_done, 1)

            def ahead(i, c):
                lo(i, 8, c + SPLIT)
                lo(i, 8, c + SPLIT + 1)

            def blocks(name, before=None, each=0):
                def body(i, j):
                    if before:
                        before(i, j)
                    ahead(i, U(name) + 2 * j)
                turns(dve, BLOCKS[name][1], body, st, each)

            def free(name, i, j):
                dve.wait_ge(bank_free, i * 4 + (BANK[name] + j + 1))

            def normed(n, src, o=None):
                dve.wait_ge(sq_done, 2 * STAT[n] + 2)
                ts(msq[:], ssq[:], 1.0 / D, EPS, ALU.mult, ALU.add).then_inc(ms_done, 1)
                dve.wait_ge(rstd_done, STAT[n] + 1)
                for t in range(TT):
                    if o is None:
                        ts(xn[:, t], src[:, t], rstd[:, t:t + 1], None, ALU.mult).then_inc(xn_done, 1)
                    else:
                        o(t)

            def scaled(n, turn, gain, bias, oH, oL):
                e = SCALED[n]
                dve.wait_ge(turned, 4 * TURN[turn] + 4)
                if e:
                    dve.wait_ge(x_ready, 2 * e)
                for k in range(4, 8):
                    src = ps[AUX + k // 2][:, (k % 2) * SEQ:(k % 2 + 1) * SEQ]
                    if bias:
                        v = ts(xv[:, k], src, gain(k), bias(k), ALU.mult, ALU.add)
                    else:
                        v = ts(xv[:, k], src, gain(k), None, ALU.mult)
                    v.then_inc(val_dve, 1)
                for f in range(2):
                    dve.wait_ge(x_hi, 2 * e + f + 1)
                    rest(oL[:, 4 * f:4 * f + 4], xv[:, 4 * f:4 * f + 4], oH[:, 4 * f:4 * f + 4]).then_inc(x_ready, 1)

            def down(name, count, gate=None):
                for m in range(SPLIT):
                    dve.wait_ge(a_hi, ACTS[name] + m + 1)
                    rest(aL[:, m], act_a[:, m], aH[:, m]).then_inc(a_lo, 1)

                def body(i, j):
                    lo(i, 4, U(name) + j + SPLIT)
                    m = j + SPLIT
                    dve.wait_ge(a_hi, i * 4 + (ACTS[name] + m + 1))
                    rest(aL[:, m % SPLIT], act_a[:, one(i * 4 + m)].rearrange("p a n -> p (a n)"),
                         aH[:, m % SPLIT]).then_inc(a_lo, 1)
                turns(dve, count - SPLIT, body)
                for j in range(count - SPLIT, count):
                    lo(0, 4, U(name) + j + SPLIT)
                dve.wait_ge(unit_done, U(name) + count)
                for t in range(TT):
                    for c in range(2):
                        hc = h[:, t, c * 512:(c + 1) * 512]
                        b = ps[AUX + 2 * t + c][:]
                        if gate is not None:
                            tmp = stage[:, c].rearrange("p a b -> p (a b)")
                            st.do(tt(tmp, b, gate[:, c * 512:(c + 1) * 512], ALU.mult))
                            b = tmp
                        tt(hc, hc, b, ALU.add).then_inc(res_done, 1)

            def residual(name, gate=None):
                def body(i, j):
                    free(name, i, j)
                    n = STAGED[name] + j
                    s = stage[:, n % 2]
                    hc = h[:, :, bass.ds((i * 4 + j) * 256, 256)]
                    if gate is not None:
                        st.do(tt(s, s, rep(gate[:, bass.ds((i * 4 + j) * 256, 256)], TT), ALU.mult))
                    tt(hc, hc, s, ALU.add).then_inc(unstaged, 1)
                blocks(name, body, 1 if gate is not None else 0)

            def gates():
                ba = sm[:, 12:14, 0:16]
                v = lambda k: sm[:, k, 0:16].rearrange("p (t n) -> p t n", t=TT)
                nc.vector.tensor_copy(ba, ps[AUX + 1][:, 0:32].rearrange("p (t n) -> p t n", t=TT)).then_inc(g_dve, 1)
                dve.wait_ge(g_dve, 1)
                st.do(tt(v(1), ba[:, :, 8:16], rep(rows_a[:, 136:144], TT), ALU.add))
                st.do(ts(sm[:, 3, 0:16], sm[:, 1, 0:16], -1.0, None, ALU.mult))
                tt(sm[:, 3, 0:16], sm[:, 3, 0:16], sm[:, 1, 0:16], ALU.min).then_inc(g_dve, 1)
                dve.wait_ge(g_act, 1)
                st.do(ts(sm[:, 2, 0:16], sm[:, 2, 0:16], 1.0, None, ALU.add))
                st.do(nc.vector.reciprocal(sm[:, 0, 0:16], sm[:, 2, 0:16]))
                st.do(ts(sm[:, 4, 16:24], sm[:, 15, 0:8], -1.0, None, ALU.mult))
                dve.wait_ge(g_act, 2)
                ts(sm[:, 5], sm[:, 4], 1.0, None, ALU.add).then_inc(g_dve, 1)
                dve.wait_ge(g_dve, 3)
                st.do(ts(sm[:, 7], sm[:, 5], 1.0, None, ALU.is_equal))
                st.do(stt(sm[:, 9], sm[:, 5], -1.0, sm[:, 7], ALU.add, ALU.add))
                st.do(nc.vector.reciprocal(sm[:, 9], sm[:, 9]))
                dve.wait_ge(g_act, 3)
                st.do(tt(sm[:, 8], sm[:, 6], sm[:, 7], ALU.add))
                st.do(tt(sm[:, 8], sm[:, 8], sm[:, 4], ALU.mult))
                st.do(tt(sm[:, 8], sm[:, 8], sm[:, 9], ALU.mult))
                st.put(nc.vector.tensor_copy(lg[:], sm[:, 8, 16:24]))
                st.do(stt(sm[:, 1, 0:16], sm[:, 1, 0:16], 0.0, sm[:, 8, 0:16], ALU.max, ALU.add))
                stt(v(10), v(1), -1.0, rep(sm[:, 14, 0:8], TT), ALU.mult, ALU.mult).then_inc(g_dve, 1)

            gc, beta, g_, eg, ke = (sm[:, k, 0:16] for k in (16, 0, 10, 17, 19))

            def delta_front():
                def spread(g):
                    if g >= 2:
                        dve.wait_ge(row_pe, g - 1)
                    tt(dG[g % 2], rep(K_["tri"], 4), bc(g_[:, 4 * g:4 * g + 4], P), ALU.mult).then_inc(dg_dve, 1)

                def exponents(g):
                    q4 = slice(4 * g, 4 * g + 4)
                    dve.wait_ge(row_pe, g + 1)
                    st.do(tt(AT[:, q4], four(ps[AUX + g % 2][:]), bc(gc[:, q4], P), ALU.subtract))
                    st.do(tt(U_[:, q4], rep(K_["low"], 4), AT[:, q4], ALU.subtract))
                    tt(AT[:, q4], AT[:, q4], rep(K_["upT"], 4), ALU.add).then_inc(arg_dve, 1)

                def qk_tok(q):
                    f0, t = TOK_HEAD[q]
                    dve.wait_ge(tok_pe, q + 1)
                    tt(tok[:, t, f0:f0 + 4], four(ps[TOK_BANK[q][0]][:]), bc(r32[:, 1, 16 * t + f0:16 * t + f0 + 4], HK),
                       ALU.mult).then_inc(tok_dve, 1)
                dve.wait_ge(g_sum, 1)
                st.do(nc.vector.tensor_copy(sm[:, 16, 0:16], ps[7][:, 0:16]))
                tt(sm[:, 18, 0:8], ps[7][:, 16:24], sm[:, 16, 0:8], ALU.subtract).then_inc(g_dve, 1)
                spread(0)
                spread(1)
                ahead(0, U("z"))
                dve.wait_ge(tok_ss, 1)
                ts(r32[:, 0], ps[7][:, 32:64], EPS, None, ALU.add).then_inc(pw_in, 1)
                exponents(0)
                spread(2)
                exponents(1)
                spread(3)
                ahead(0, U("z") + 2)
                exponents(2)
                exponents(3)
                dve.wait_ge(pw_out, 1)
                r = r32[:, 1].rearrange("p (t n) -> p t n", t=TT)
                st.do(ts(r[:, :, 0:8], r[:, :, 0:8], HK ** -0.5, None, ALU.mult))
                qk_tok(4)
                qk_tok(5)
                ahead(0, U("z") + 4)
                for q in range(6, 10):
                    qk_tok(q)
                ahead(0, U("z") + 6)
                qk_tok(10)
                qk_tok(11)
                for q in range(1, 8, 2):
                    dve.wait_ge(back_pe, q + 1)
                    nc.vector.tensor_copy(feat[:, BACK_HEAD[q]:BACK_HEAD[q] + 2].rearrange("p a b -> p (a b)"),
                                          ps[AUX + q % 4][:]).then_inc(back_dve, 1)

            def delta():
                join = K_["join"].rearrange("p (l n) -> p l n", l=7)
                dve.wait_ge(exp_act, 4)
                st.do(tt(U_[:], U_[:], bc(beta, P), ALU.mult))

                def set_up(g):
                    q4 = slice(4 * g, 4 * g + 4)
                    dve.wait_ge(mt_act, g + 1)
                    st.put(tt(T_[:, q4], T_[:, q4], rep(join[:, 0], 4), ALU.mult))
                    st.do(tt(U_[:, q4], MT[:, q4], rep(K_["join1T"], 4), ALU.mult))
                    st.put(tt(T_[:, q4], T_[:, q4], rep(ident, 4), ALU.add))
                    tt(U_[:, q4], U_[:, q4], rep(ident, 4), ALU.add).then_inc(dbl_dve, 1)
                for g in range(4):
                    q4 = slice(4 * g, 4 * g + 4)
                    dve.wait_ge(kq_pe, g + 1)
                    tt(T_[:, q4], four(ps[4 + g % 2][:]), U_[:, q4], ALU.mult).then_inc(m_dve, 1)
                    tt(AT[:, q4], four(ps[6 + g % 2][:]), AT[:, q4], ALU.mult).then_inc(at_dve, 1)
                    if g:
                        set_up(g - 1)
                set_up(3)
                st.wait(st.n)
                for l in range(LEVELS):
                    for step in range(3):
                        for g in range(4):
                            q4 = slice(4 * g, 4 * g + 4)
                            if l == LEVELS - 1 and step == 1:
                                continue
                            n = l * 12 + step * 4 + g + 1
                            if l == LEVELS - 1 and step == 2:
                                n -= 4
                            dve.wait_ge(dbl_pe, n)
                            b = four(ps[AUX + g][:])
                            if step == 0:
                                tt(P_[:, q4], b, rep(join[:, l + 1], 4), ALU.mult).then_inc(dbl_dve, 1)
                            else:
                                s = 1 << (l + 1)
                                o = (T_, U_)[step - 1][:, q4].rearrange("p x (n h s) -> p x n h s", h=2, s=s)[:, :, :, step - 1]
                                b = b[:, :, 0:64].rearrange("p x (n s) -> p x n s", s=s)
                                tt(o, o, b, ALU.add).then_inc(dbl_dve, 1)
                tt(tok[:, 0, 16:24], tok[:, 0, 16:24], bc(beta[:, 0:8], HK), ALU.mult).then_inc(scan_dve, 1)
                dve.wait_ge(g_act, 4)
                tt(tok[:, 0, 8:16], tok[:, 0, 8:16], bc(ke[:, 0:8], HK), ALU.mult).then_inc(scan_dve, 1)
                for hb in range(2):
                    dve.wait_ge(scan_pe, 5 + hb)
                    tt(MT[:, 8 + 4 * hb:12 + 4 * hb], four(ps[4 + hb][:]), bc(eg[:, 8 + 4 * hb:12 + 4 * hb], P),
                       ALU.mult).then_inc(scan_dve, 1)
                dve.wait_ge(scan_dve, 4)
                st.do(tt(MT[:, 8:16], tok[:, 1, 16:24], MT[:, 8:16], ALU.subtract))
                tt(T_[:, 8:16], MT[:, 8:16], bc(beta[:, 8:16], P), ALU.mult).then_inc(scan_dve, 1)
                for hb in range(2):
                    dve.wait_ge(scan_pe, 7 + hb)
                    tt(MT[:, 4 * hb:4 + 4 * hb], four(ps[6 + hb][:]), bc(eg[:, 8 + 4 * hb:12 + 4 * hb], P),
                       ALU.mult).then_inc(scan_dve, 1)
                dve.wait_ge(scan_dve, 7)
                for hb in range(2):
                    dve.wait_ge(scan_pe, 13 + hb)
                    tt(tok[:, 1, 4 * hb:4 * hb + 4], four(ps[4 + hb][:]), MT[:, 4 * hb:4 * hb + 4],
                       ALU.add).then_inc(scan_dve, 1)
                dve.wait_ge(scan_dve, 9)
                dve.wait_ge(scan_act, 6)
                for t in range(TT):
                    st.put(tt(MT[:, 8 * t:8 * t + 8], tok[:, t, 0:8], tok[:, t, 0:8], ALU.mult))
                st.wait(st.n)
                st.do(nc.vector.tensor_reduce(r32[:, 0, 0:16], MT[:], AX, ALU.add))
                ts(r32[:, 0, 0:16], r32[:, 0, 0:16], 1.0 / HK, EPS, ALU.mult, ALU.add).then_inc(pw_in, 1)
                dve.wait_ge(pw_out, 2)
                dve.wait_ge(bank_free, BANK["z"] + 4)
                for t in range(TT):
                    o = tok[:, t, 0:8]
                    st.do(tt(o, o, bc(r32[:, 1, 8 * t:8 * t + 8], HK), ALU.mult))
                    st.do(tt(o, o, rep(rows_a[:, 0:128], 8), ALU.mult))
                    last = tt(o, o, zs[:, t].rearrange("p (a b) -> p a b", a=8), ALU.mult)
                last.then_inc(y_rows, 1)
                for b in range(4):
                    dve.wait_ge(y_hi, b + 1)
                    rest(xL[:, 2 * b:2 * b + 2].rearrange("p a b -> p (a b)"), ps[AUX + b][:],
                         xH[:, 2 * b:2 * b + 2].rearrange("p a b -> p (a b)")).then_inc(y_ready, 1)

            def band():
                def maxima(g):
                    b = g % 2
                    dve.wait_ge(b_score, g + 1)
                    if g == 0:
                        dve.wait_ge(slab_masked, 1)
                    for x in range(4):
                        n, o = 4 * g + x, x // 2
                        for t in range(TT):
                            c = slice(0, 256) if t else slice(256, 384)
                            w = ps[4 + x % 2][:, o * 256:(o + 1) * 256] if t else ps[6 + x % 2][:, o * P:(o + 1) * P]
                            s = slab[:, n, ::-1] if t else slab[:, n, P - 1::-1]
                            st.put(nc.vector.tensor_tensor_reduce(p_b[:, b, x, c], w, s, 1.0, -3e38, ALU.add, ALU.max,
                                                                  st_b[:, b, 0, 2 * x + t:2 * x + t + 1]))
                    st.wait(st.n)
                    ts(st_b[:, b, 1], st_b[:, b, 0], -1.0, None, ALU.mult).then_inc(b_max, 1)
                maxima(0)
                for g in range(4):
                    b = g % 2
                    if g < 3:
                        maxima(g + 1)
                    dve.wait_ge(b_exp, 8 * g + 8)
                    st.do(nc.vector.reciprocal(st_b[:, b, 0], st_b[:, b, 2]))
                    r = st_b[:, b, 0].rearrange("p (x t) -> p x t", t=TT)
                    tt(p_b[:, b, :, 0:256], p_b[:, b, :, 0:256], bc(r[:, :, 1], 256), ALU.mult)
                    tt(p_b[:, b, :, 256:384], p_b[:, b, :, 256:384], bc(r[:, :, 0], P), ALU.mult).then_inc(b_prob, 1)
                    dve.wait_ge(b_turn, 3 * g + 2)
                    nc.vector.tensor_copy(pT_b[:, b, 2:4, 0:256], ps[1][:].rearrange("p (x n) -> p x n", x=2)).then_inc(b_tdve, 1)
                    dve.wait_ge(b_turn, 3 * g + 3)
                    dve.wait_ge(y_hi, 4 + g + 1)
                    rest(xL[:, 2 * g:2 * g + 2].rearrange("p a b -> p (a b)"), ps[3][:],
                         xH[:, 2 * g:2 * g + 2].rearrange("p a b -> p (a b)")).then_inc(y_ready, 1)

            def table(name, t=None):
                o, n = TABLES[name]
                return tb[:, o:o + n] if t is None else tb[:, o + t * n // 2:o + (t + 1) * n // 2]

            def mix():
                dve.wait_ge(m_dec, 1)
                dve.wait_ge(bank_free, BANK["wo_c"])
                for d in range(2):
                    for t in range(TT):
                        tt(rope[:, t, d * 512:(d + 1) * 512].rearrange("p (a b) -> p a b", a=4),
                           ckv[:, t, 0:512].rearrange("p (a b) -> p a b", a=4), bc(dec[:, 2 + d, t], P),
                           ALU.mult).then_inc(m_ck, 1)
                dve.wait_ge(m_state, 2)
                for t in range(TT):
                    x = qk_t[:, t].rearrange("p (n c) -> p n c", n=8)
                    o = rope[:, t].rearrange("p (n c) -> p n c", n=8)
                    cos, sin = rep(table("rcos", t), 8), rep(table("rsin", t), 8)
                    u, w = (wt[:, y].rearrange("p (n c) -> p n c", n=8) for y in range(2))
                    st.put(tt(o[:, :, 0:64], x[:, :, 0:64], cos, ALU.mult))
                    st.put(tt(o[:, :, 64:], x[:, :, 0:64], sin, ALU.mult))
                    st.put(tt(u, x[:, :, 64:], sin, ALU.mult))
                    st.do(tt(w, x[:, :, 64:], cos, ALU.mult))
                    st.put(tt(o[:, :, 0:64], o[:, :, 0:64], u, ALU.subtract))
                    tt(o[:, :, 64:], o[:, :, 64:], w, ALU.add).then_inc(m_rope, 1)
                    dve.wait_ge(m_rope, t + 1)
                for b in (1, 3):
                    dve.wait_ge(m_turn, b + 1)
                    o = rkT if b == 3 else rqT
                    nc.vector.tensor_copy(o[:, 2:4].rearrange("p a b -> p (a b)"), ps[AUX + b][:]).then_inc(m_tdve, 1)
                for n in range(RET_H):
                    dve.wait_ge(m_w, n + 1)
                    st.put(tt(wt[:, 0], wt[:, 0], table("ge"), ALU.mult))
                    st.do(tt(wt[:, 1], wt[:, 1], table("le"), ALU.mult))
                    st.do(tt(wt[:, 0], wt[:, 0], wt[:, 1], ALU.add))
                    dve.wait_ge(m_s, n + 1)
                    stt(sT[:, n % 2], ps[4][:], HK ** -0.5, wt[:, 0], ALU.mult, ALU.mult).then_inc(m_sd, 1)
                    dve.wait_ge(m_o, n + 1)
                    st.do(nc.vector.tensor_copy(o_r[:, :, n], ps[6][:, 0:256].rearrange("p (t c) -> p t c", t=TT)))
                    for t in range(TT):
                        st.do(stt(o_r[:, t, n], ps[6][:, 256 + t * P:256 + (t + 1) * P], dec[:, 0, t, n:n + 1],
                                  o_r[:, t, n], ALU.mult, ALU.add))
                    for t in range(TT):
                        last = stt(o_r[:, t, n], ps[7][:, t * P:(t + 1) * P], dec[:, 1, t, n:n + 1],
                                   o_r[:, t, n], ALU.mult, ALU.add)
                    last.then_inc(m_od, 1)
                dve.wait_ge(m_od, RET_H)
                o = o_r[:].rearrange("p t n c -> p (t n) c")
                sq = rope[:, 0].rearrange("p (a b) -> p a b", a=8)
                st.do(nc.vector.tensor_reduce(st_r[:, 0], o, AX, ALU.add))
                st.do(ts(st_r[:, 0], st_r[:, 0], 1.0 / HK, None, ALU.mult))
                st.do(tt(o, o, bc(st_r[:, 0], HK), ALU.subtract))
                st.do(tt(sq, o, o, ALU.mult))
                st.do(nc.vector.tensor_reduce(st_r[:, 1], sq, AX, ALU.add))
                ts(st_r[:, 2], st_r[:, 1], 1.0 / HK, EPS, ALU.mult, ALU.add).then_inc(pw_in, 1)
                dve.wait_ge(pw_out, 3)
                st.do(tt(o, o, bc(st_r[:, 3], HK), ALU.mult))
                o2 = o_r[:].rearrange("p t n c -> p t (n c)")
                st.do(tt(o2, o2, rep(rows_c[:, 0:512], TT), ALU.mult))
                tt(o2, o2, sg[:], ALU.mult).then_inc(y_rows, 1)
                for b in range(2):
                    dve.wait_ge(y_hi, 8 + b + 1)
                    rest(xL[:, 2 * b:2 * b + 2].rearrange("p a b -> p (a b)"), ps[4 + b][:],
                         xH[:, 2 * b:2 * b + 2].rearrange("p a b -> p (a b)")).then_inc(y_ready, 1)
                for t in range(TT):
                    x = aqkv[:, t, 0:640].rearrange("p (n c) -> p n c", c=ATT_D)
                    xc = cakv[:, t, 0:128].rearrange("p (n c) -> p n c", c=ATT_D)
                    st.put(tt(asq[:, 0:10], x, x, ALU.mult))
                    st.do(tt(asq[:, 10:12], xc, xc, ALU.mult))
                    st.do(nc.vector.tensor_reduce(st_a[:, t, 0], asq[:], AX, ALU.add))
                    last = ts(st_a[:, t, 0], st_a[:, t, 0], 1.0 / ATT_D, EPS, ALU.mult, ALU.add)
                    st.put(last) if t == 0 else last.then_inc(pw_in, 1)
                dve.wait_ge(pw_out, 4)
                qn, kn = rows_c[:, 512:576], rows_c[:, 576:640]
                for t in range(TT):
                    x = aqkv[:, t, 0:640].rearrange("p (n c) -> p n c", c=ATT_D)
                    xc = cakv[:, t, 0:128].rearrange("p (n c) -> p n c", c=ATT_D)
                    st.put(tt(x, x, bc(st_a[:, t, 1, 0:10], ATT_D), ALU.mult))
                    st.do(tt(kcn[:, t], xc, bc(st_a[:, t, 1, 10:12], ATT_D), ALU.mult))
                    st.put(tt(x[:, 0:8], x[:, 0:8], rep(qn, 8), ALU.mult))
                    st.put(tt(x[:, 8:10], x[:, 8:10], rep(kn, 2), ALU.mult))
                    st.do(tt(kcn[:, t], kcn[:, t], rep(kn, 2), ALU.mult))
                    cos, sin = rep(table("acos", t), 10), rep(table("asin", t), 10)
                    st.put(tt(rt[:, 0], x[:, :, 0:32], cos, ALU.mult))
                    st.put(tt(rt[:, 1], x[:, :, 32:], sin, ALU.mult))
                    st.put(tt(rt[:, 2], x[:, :, 0:32], sin, ALU.mult))
                    st.do(tt(rt[:, 3], x[:, :, 32:], cos, ALU.mult))
                    for c, y, op in ((0, 0, ALU.subtract), (32, 2, ALU.add)):
                        for s in range(2):
                            st.put(tt(aqn[:, t, s:8:2, c:c + 32], rt[:, y, 4 * s:4 * s + 4], rt[:, y + 1, 4 * s:4 * s + 4], op))
                        last = tt(aqn[:, t, 8:10, c:c + 32], rt[:, y, 8:10], rt[:, y + 1, 8:10], op)
                        st.put(last) if c == 0 else last.then_inc(q_rope, 1)
                    dve.wait_ge(q_rope, t + 1)
                def maxima(j):
                    for n in range(4):
                        dve.wait_ge(s_pe, 4 * j + n + 1)
                        st.do(nc.vector.tensor_reduce(st_p[:, 0, n:n + 1], ps[4 + n][:], AX, ALU.max))
                        ts(st_p[:, 1, n:n + 1], st_p[:, 0, n:n + 1], -ATT_D ** -0.5, None, ALU.mult).then_inc(s_max, 1)

                def probabilities(j):
                    for n in range(4):
                        dve.wait_ge(s_exp, 4 * j + n + 1)
                        st.do(nc.vector.reciprocal(st_p[:, 0, n:n + 1], st_p[:, 2, n:n + 1]))
                        w = ap_[:, n // 2, n % 2]
                        ts(w, w, st_p[:, 0, n:n + 1], None, ALU.mult).then_inc(s_prob, 1)
                maxima(0)
                probabilities(0)
                for j in range(4):
                    for x in (0, 2):
                        n = ATT_BANKS[x]
                        dve.wait_ge(s_turn, 4 * j + x + 1)
                        nc.vector.tensor_copy(apT[:, n // 2, 2 * (n % 2):2 * (n % 2) + 2].rearrange("p a b -> p (a b)"),
                                              ps[n][:]).then_inc(s_tdve, 1)
                    if j < 3:
                        maxima(j + 1)
                        probabilities(j + 1)
                    dve.wait_ge(y_hi, 10 + j + 1)
                    r = 64 * (j % 2)
                    rest(xL[r:r + 64, 4 + j // 2:8:2], ps[0][r:r + 64].rearrange("p (a b) -> p a b", a=2),
                         xH[r:r + 64, 4 + j // 2:8:2]).then_inc(y_ready, 1)

            dve.wait_ge(x_in, 16)
            normed("a", h)
            dve.wait_ge(act_s, 1)
            rest(baL[:], baw[:], baH[:]).then_inc(c_ready, 1)
            for c in range(SPLIT):
                lo(0, 0, c)
            scaled("a", "a", lambda k: col("a_norm", k), None, xH, xL)
            dve.wait_ge(ba_done, 1)
            gates()

            def modulation():
                dve.wait_ge(mod_act, MOD_EARLY)
                st.do(tt(modc[:, 0:16], modc[:, 0:16], bc(col("b_mod", 0, 16), 2), ALU.add))
                st.do(stt(gs1[:], modc[:, 8:16], 1.0, bc(col("norm1", 0, 8), 2), ALU.add, ALU.mult))

            def modulation2():
                dve.wait_ge(mod_act, MOD_GROUPS)
                st.do(tt(modc[:, 16:32], modc[:, 16:32], bc(col("b_mod", 24, 16), 2), ALU.add))
                st.put(stt(gs2[:], modc[:, 24:32, 0], 1.0, col("norm2", 0, 8), ALU.add, ALU.mult))
                st.put(tt(gate1[:], gate1[:], bmrow[:, 0:D], ALU.add))
                st.do(tt(gate2[:], gate2[:], bmrow[:, D:], ALU.add))

            def conv(name, taps, tiles, bias, nextto):
                wname = {"qkv": "a_conv", "up0": "f_conv0", "up1": "f_conv1"}[name]

                def body(i, j):
                    free(name, i, j)
                    n = STAGED[name] + j
                    if name == "qkv" and not (isinstance(i, int) and j < 2):
                        dve.wait_ge(silu_done, i * 4 + (j - 1))
                    m = i * 4 + j
                    marks = [0, 0]
                    for d in range(taps):
                        for f in range(2):
                            o, x = cv[:, n % 2, f], stage[:, n % 2, f]
                            w = cols[:, one(COLS[wname][0] + (taps - 1 - d) * tiles + nextto(m, f))]
                            if d == 0:
                                if bias:
                                    c = ts(o, x, w, cols[:, one(COLS[bias][0] + nextto(m, f))], ALU.mult, ALU.add)
                                else:
                                    c = ts(o, x, w, None, ALU.mult)
                                marks[f] = st.put(c)
                                continue
                            st.wait(marks[f])
                            c = stt(o[:, d:], x[:, 0:SEQ - d], w, o[:, d:], ALU.mult, ALU.add)
                            if d == taps - 1 and f == 1:
                                c.then_inc(unstaged, 1)
                            else:
                                marks[f] = st.put(c)
                return body, 2 * taps - 1

            body, each = conv("qkv", A_TAPS, QKV_TILES, None, lambda m, f: m * 2 + f)
            blocks("qkv", body, each)
            delta_front()
            delta()
            residual("wo_a")

            def ffn(l, before):
                dve.wait_ge(unstaged, before)
                normed(f"f{l}", h)
                scaled(f"f{l}", f"f{l}", lambda k: col(f"f_norm{l}", k), None, xH, xL)
                up = f"up{l}"
                conv_, steps = conv(up, F_TAPS, 2 * F_TILES, f"f_bias{l}", lambda m, f: m + f * F_TILES)
                si = 12 + 22 * l

                def body(i, j):
                    conv_(i, j)
                    ahead(i, U(up) + 2 * j)
                    n = STAGED[up] + j
                    dve.wait_ge(silu_done, i * 4 + (si + j + 1))
                    tt(act_a[:, one(i * 4 + j)].rearrange("p a n -> p (a n)"), cv[:, n % 2, 0], cv[:, n % 2, 1],
                       ALU.mult).then_inc(prod_done, 1)
                turns(dve, BLOCKS[up][1], body, st, steps)
                down(f"down{l}", F_TILES)
            ffn(0, STAGED["wo_a"] + 4)
            dve.wait_ge(res_done, RES["down0"])
            normed("kv", h)
            scaled("kv", "kv", lambda k: col("kv_norm", k), None, xH, xL)
            scaled("q", "kv", lambda k: col("b_norm", k), None, x2H, x2L)
            blocks("k")
            blocks("v")
            blocks("q")
            band()
            residual("wo_b")
            ffn(1, STAGED["wo_b"] + 4)
            dve.wait_ge(res_done, RES["down1"])

            def final(row):
                def o(t):
                    st.do(ts(h[:, t], h[:, t], rstd[:, t:t + 1], None, ALU.mult))
                    tt(h[:, t], h[:, t], row[:], ALU.mult).then_inc(res_done, 1)
                return o
            dve.wait_ge(late_in, 80)
            modulation()
            normed("x2", h, final(row_f1))
            dve.wait_ge(res_done, RES["x2"])
            normed("ctx", ctx_in)
            scaled("ctx", "ctx", lambda k: gs1[:, k, 1:2], lambda k: modc[:, k, 1:2], xcH, xcL)
            normed("n1", h)
            scaled("n1", "n1", lambda k: gs1[:, k, 0:1], lambda k: modc[:, k, 0:1], xH, xL)
            for m in range(11):
                ahead(0, U("win") + 2 * m)
            mix()
            modulation2()
            residual("wo_c", gate1)
            dve.wait_ge(unstaged, STAGED["wo_c"] + 4)
            normed("n2", h)
            scaled("n2", "n2", lambda k: gs2[:, k:k + 1], lambda k: modc[:, 16 + k, 0:1], xH, xL)

            def square(i, j):
                free("ff1", i, j)
                s = stage[:, (STAGED["ff1"] + j) % 2]
                tt(act_a[:, bass.ds((i * 4 + j) * 2, 2)], s, s, ALU.mult).then_inc(unstaged, 1)
            blocks("ff1", square)
            down("ff2", FF2_TILES, gate2)
            dve.wait_ge(res_done, RES["ff2"])
            dve.wait_ge(final_in, 16)
            normed("fin", h, final(rows_f))


def columns(x):
    x = np.asarray(x)
    return x.reshape(-1, P).T


def constants():
    i, j = np.arange(P)[:, None], np.arange(P)[None, :]
    joins = []
    for l in range(7):
        s = 1 << l
        joins.append(-((i // (2 * s) == j // (2 * s)) & (i % (2 * s) >= s) & (j % (2 * s) < s)).astype(np.float32))
    parts = [np.eye(P), np.ones((P, P)), i <= j, np.where(j < i, 0.0, NEG), np.where(j >= i, 0.0, NEG), *joins, joins[0].T]
    return np.concatenate([np.asarray(x, np.float32) for x in parts], axis=1)


def tables():
    p, i = np.arange(P)[:, None], np.arange(SEQ)[None, :]
    rel = np.concatenate([i - (p + P * t) for t in range(TT)], axis=1).astype(np.float32)
    pos = np.concatenate([p, p + P], axis=1).astype(np.float32)
    t = np.arange(SEQ, dtype=np.float32)

    def freqs(n):
        return (np.float32(10000.0) ** (-np.arange(n, dtype=np.float32) / np.float32(n))).astype(np.float32)

    def rows(x):
        return np.concatenate([x[k * P:(k + 1) * P] for k in range(TT)], axis=1)
    ra = (t[:, None] * freqs(64)).astype(np.float64)
    aa = np.concatenate([np.floor(t / 64)[:, None] * freqs(16), (t % 64)[:, None] * freqs(16)], axis=1).astype(np.float64)
    parts = [np.maximum(rel, 0), np.maximum(-rel, 0), rel >= 0, rel <= 0, pos + 1, SEQ - pos, CTX - 1 - pos, pos,
             rows(np.cos(ra)), rows(np.sin(ra)), rows(np.cos(aa)), rows(np.sin(aa))]
    return np.concatenate([np.asarray(x, np.float32) for x in parts], axis=1)


BIG = ("x", "b_rel_bias", "a_w_in", "a_w_out", "w_kv", "b_w_q", "b_w_out", "f_w_up", "f_w_down", "ctx_2", "w_mod_2", "w_in_2",
       "w_out_2", "w_ff1_2", "w_ff2_2")


def lay_out(v):
    g = {n: np.ascontiguousarray(v[n]) for n in BIG}
    order = [v["a_norm"], v["kv_norm"], v["b_norm"], v["f_norm"][0], v["f_norm"][1], v["norm1_g_2"], v["norm2_g_2"],
             v["a_conv"], v["f_conv"][0], v["f_conv"][1], v["f_conv_b"][0], v["f_conv_b"][1], v["b_mod_2"],
             v["c_2"], v["c_ctx_2"]]
    g["cols"] = np.ascontiguousarray(np.concatenate([columns(x) for x in order], axis=1))
    flat = lambda xs: np.ascontiguousarray(np.concatenate([np.asarray(x).reshape(1, -1) for x in xs], axis=1))
    g["rows_a"] = flat([v["a_out_norm"], v["a_A_log"], v["a_dt_bias"], v["ret_log_rate_2"]])
    bm = np.asarray(v["b_mod_2"]).reshape(6, D)
    g["rows_m"] = flat([bm[2], bm[5]])
    g["rows_c"] = flat([v["final_norm"], v["ret_gn_g_2"], v["q_norm_g_2"], v["k_norm_g_2"], v["final_norm_g_2"]])
    g["consts"] = constants()
    g["tables"] = tables()
    return g


def program(nc, arrays):
    aps = {n: nc.dram_tensor(f"in_{n}", x.shape, mybir.dt.from_np(x.dtype), kind="ExternalInput").ap()
           for n, x in arrays.items()}
    out = nc.dram_tensor("out", (1, SEQ, D), F32, kind="ExternalOutput").ap()
    build(nc, aps, out)


def kernel(**inputs):
    import concourse.bacc as bacc
    from concourse.bass_utils import run_bass_kernel_spmd

    arrays = lay_out(inputs)
    nc = bacc.Bacc("TRN2", target_bir_lowering=False, num_devices=1)
    program(nc, arrays)
    r = run_bass_kernel_spmd(nc, [{f"in_{n}": x for n, x in arrays.items()}], core_ids=[0])
    return r.results[0]["out"]
```

```python
from contextlib import ExitStack, contextmanager

import numpy as np

import concourse.bass as bass
from concourse import mybir

F32 = mybir.dt.float32
F32R = mybir.dt.float32r
ALU = mybir.AluOpType
ACT = mybir.ActivationFunctionType
AX = mybir.AxisListType.X

P = 128
SEQ = 256
TT = SEQ // P
D = 1024
KD = D // P
EPS = 1e-6
NEG = -1e30

A_HEADS, HK = 8, 128
QKV_TILES = 3 * A_HEADS
A_TAPS = 4
B_HEADS, BH = 16, 64
FF = 2816
F_TILES = FF // P
F_TAPS = 3
RET_H = 4
ATT_H, ATT_KV, ATT_D = 8, 2, 64
FF2_TILES = 4 * D // P
CTX = 256
LEVELS = 6

RAW = 4
SPLIT = 4
BLOCKS = {}
_n = 0
for _name, _count in (("qkv", 12), ("z", 4), ("wo_a", 4), ("up0", 22), ("down0", 11),
                      ("k", 4), ("v", 4), ("q", 4), ("wo_b", 4), ("up1", 22), ("down1", 11),
                      ("win", 11), ("wo_c", 4), ("ff1", 16), ("ff2", 16)):
    BLOCKS[_name] = (_n, _count)
    _n += _count
UNITS = 2 * _n
CTX_BLOCKS = (2, 3, 4, 5, 10)
WIN_ORDER = (8, 9, 10, 0, 1, 2, 3, 4, 5, 6, 7)
BANK = {}
_e = 0
for _name, (_b, _count) in BLOCKS.items():
    BANK[_name] = _e
    if _name in ("down0", "down1", "ff2"):
        continue
    _e += _count + (len(CTX_BLOCKS) if _name == "win" else 0)
MOD_PLACES = (("wo_a", 5), ("up0", 1), ("k", 1), ("wo_b", 1), ("up1", 1), ("win", 2), ("ff1", 1))
MOD_AT = {}
MOD_CHUNK = []
for _name, _count in MOD_PLACES:
    MOD_AT[_name] = (len(MOD_CHUNK), _count)
    MOD_CHUNK += [_name] * _count

COLS = {}
_c = 0
for _name, _count in (("a_norm", 8), ("kv_norm", 8), ("b_norm", 8), ("f_norm0", 8), ("f_norm1", 8),
                      ("norm1", 8), ("norm2", 8), ("a_conv", A_TAPS * 24), ("f_conv0", F_TAPS * 44),
                      ("f_conv1", F_TAPS * 44), ("f_bias0", 44), ("f_bias1", 44), ("b_mod", 48),
                      ("c", 8), ("c_ctx", 8)):
    COLS[_name] = (_c, _count)
    _c += _count
N_COLS = _c
CONSTS = {}
_c = 0
for _name, _count in (("ident", P), ("ones", P), ("tri", P), ("low", P), ("upT", P), ("join", 7 * P), ("join1T", P)):
    CONSTS[_name] = (_c, _count)
    _c += _count
N_CONSTS = _c
TABLES = {}
_c = 0
for _name, _count in (("fwd", 512), ("bwd", 512), ("ge", 512), ("le", 512), ("pos", 8),
                      ("rcos", 128), ("rsin", 128), ("acos", 64), ("asin", 64)):
    TABLES[_name] = (_c, _count)
    _c += _count
N_TABLES = _c
STAGED = {}
_s = 0
for _name in ("qkv", "wo_a", "up0", "wo_b", "up1", "wo_c", "ff1"):
    STAGED[_name] = _s
    _s += BLOCKS[_name][1]
STAT = {n: i for i, n in enumerate(("a", "f0", "kv", "f1", "ctx", "x2", "n1", "n2", "fin"))}
TURN = {n: i for i, n in enumerate(("a", "f0", "kv", "f1", "ctx", "n1", "n2"))}
SCALED = {n: i for i, n in enumerate(("a", "f0", "kv", "q", "f1", "ctx", "n1", "n2"))}
GAINED = {n: i for i, n in enumerate(("a", "f0", "kv", "q", "f1"))}
SHIFTED = {n: i for i, n in enumerate(("ctx", "n1", "n2"))}
RES = {"down0": 4, "down1": 8, "x2": 10, "ff2": 14, "fin": 16}
PRODS = {"down0": 0, "down1": 22}
ACTS = {"down0": 0, "down1": 22, "ff2": 44}
AUX = 4


TOK_HEAD = [(f, t) for f0 in (16, 8, 0) for f in (f0, f0 + 4) for t in range(TT)]
TOK_BANK = [(6, ()), (7, (("pw", 1),)), (6, (("act", 1),)), (7, (("act", 2),)),
            (4, (("arg", 3),)), (5, (("arg", 4),)), (6, (("act", 3),)), (7, (("act", 4),)),
            (4, (("dve", 1),)), (5, (("dve", 2),)), (6, (("dve", 3),)), (7, (("dve", 4),))]
BACK_HEAD = (8, 10, 12, 14, 0, 2, 4, 6)


ATT_BANKS = (1, 3, 2, 0)


DECAYS = (2, 3, 0, 1)


class Steps:

    def __init__(self, eng, sem):
        self.eng, self.sem, self.n, self.base = eng, sem, 0, 0

    def put(self, ins):
        ins.then_inc(self.sem, 1)
        self.n += 1
        return self.n

    def wait(self, n):
        self.eng.wait_ge(self.sem, self.base + n)

    def do(self, ins):
        self.wait(self.put(ins))

    @contextmanager
    def loop(self, i, turns, each):
        first = self.n
        self.base = i * each
        yield
        assert self.n - first == each, (self.n - first, each)
        self.base = 0
        self.n = first + turns * each


def turns(eng, count, body, steps=None, each=0, between=None, before_last=None):
    head = count % 4 or 4
    for j in range(head):
        body(0, j)
    if between:
        between()
    n = (count - head) // 4
    tail = 4 if n == 1 or before_last else 0
    n -= tail // 4
    if n > 0:
        with eng.Fori(0, n) as i:
            if steps is None:
                for j in range(4):
                    body(i, head + j)
            else:
                with steps.loop(i, n, 4 * each):
                    for j in range(4):
                        body(i, head + j)
    for j in range(count - tail, count) if count > head else ():
        if before_last and j == count - 1:
            before_last()
        body(0, j)


def one(m):
    return bass.ds(m, 1)


def build(nc, a, out):
    with ExitStack() as ctx:
        def sb(name, shape, dt=F32, where=ctx):
            return where.enter_context(nc.sbuf_tensor(name, shape, dt))

        def sem(name):
            return ctx.enter_context(nc.semaphore(name))

        raw = sb("raw", [P, RAW, 1024])
        wH = sb("wH", [P, SPLIT, 1024], F32R)
        wL = sb("wL", [P, SPLIT, 1024], F32R)
        h = sb("h", [P, TT, D])
        xH = sb("xH", [P, KD, SEQ], F32R)
        xL = sb("xL", [P, KD, SEQ], F32R)
        cols = sb("cols", [P, N_COLS])
        cst = sb("cst", [P, N_CONSTS])
        rows_a = sb("rows_a", [P, 152])
        stage = sb("stage", [P, 2, 2, SEQ])
        cv = sb("cv", [P, 2, 2, SEQ])
        gate1 = sb("gate1", [P, D])
        gate2 = sb("gate2", [P, D])
        modc = sb("modc", [P, 32, 2])
        gs1 = sb("gs1", [P, KD, 2])
        gs2 = sb("gs2", [P, KD])
        ssq = sb("ssq", [P, TT])
        ssq_part = sb("ssq_part", [P, TT])
        msq = sb("msq", [P, TT])
        rstd = sb("rstd", [P, TT])
        mhalf = sb("mhalf", [P, 32])
        lg = sb("lg", [P, 8])
        cact = sb("cact", [P, KD, 2])
        mrow = sb("mrow", [2, 2, 512])

        def place(kib, *names):
            with ExitStack() as s:
                if kib:
                    sb(f"pad_{names[0][0]}", [P, kib * 256], where=s)
                return [sb(*n, where=s) for n in names]
        xn, xv, qk_t, rv, sg, aqkv, cakv = place(
            0, ("xn", [P, TT, D]), ("xv", [P, KD, SEQ]), ("qk_t", [P, TT, D]), ("rv", [P, TT, 512]), ("sg", [P, TT, 512]),
            ("aqkv", [P, TT, 768]), ("cakv", [P, TT, 256]))
        akT, dec, st_r, st_a, st_p = place(
            40, ("akT", [P, 512]), ("dec", [P, 4, TT, RET_H]), ("st_r", [P, 4, 8]), ("st_a", [P, TT, 2, 12]), ("st_p", [P, 3, 4]))
        row_f1, bmrow, ctx_in, xcH, xcL, xvc, wt, tb, rows_c = place(
            44, ("row_f1", [P, D]), ("bmrow", [P, 2048]), ("ctx_in", [P, TT, D]), ("xcH", [P, KD, SEQ], F32R),
            ("xcL", [P, KD, SEQ], F32R), ("xvc", [P, KD, SEQ]), ("wt", [P, 2, 512]), ("tb", [P, N_TABLES]),
            ("rows_c", [P, 640]))
        ckv, aqn, asq = place(0, ("ckv", [P, TT, D]), ("aqn", [P, TT, 10, ATT_D]), ("asq", [P, 12, ATT_D]))
        aqT, = place(44, ("aqT", [P, 4, SEQ]))
        rope, = place(56, ("rope", [P, TT, D]))
        rqT, rkT, sT01, o_r, kcn, rt = place(
            64, ("rqT", [P, RET_H, SEQ]), ("rkT", [P, RET_H, SEQ]), ("sT01", [P, 2, 512]), ("o_r", [P, TT, RET_H, P]),
            ("kcn", [P, TT, 2, ATT_D]), ("rt", [P, 4, 10, 32]))
        s_fb, = place(81, ("s_fb", [P, 2, RET_H, P]))
        sT2, = place(13, ("sT2", [P, 512]))
        sT3, = place(86, ("sT3", [P, 512]))
        sT = (sT01[:, 0], sT01[:, 1], sT2[:], sT3[:])
        ap_, = place(16, ("ap_", [P, 2, TT, 512]))
        apT, = place(0, ("apT", [P, 2, 4, SEQ]))
        with ExitStack() as s:
            sb("pad_m", [P, 2 * TT * D], where=s)
            baw = sb("baw", [P, KD, 16], where=s)
            baH = sb("baH", [P, KD, 16], F32R, where=s)
            baL = sb("baL", [P, KD, 16], F32R, where=s)
        with ExitStack() as s:
            tok = sb("tok", [P, TT, QKV_TILES, HK], where=s)
            feat = sb("feat", [P, QKV_TILES, SEQ], where=s)
            T_ = sb("T_", [P, 16, P], where=s)
            MT = sb("MT", [P, 16, P], where=s)
            U_ = sb("U_", [P, 16, P], where=s)
            AT = sb("AT", [P, 16, P], where=s)
            zs = sb("zs", [P, TT, D], where=s)
            sm = sb("sm", [P, 24, 24], where=s)
            r32 = sb("r32", [P, 3, 32], where=s)
        P_ = feat[:, 16:24, :].rearrange("p a (b c) -> p (a b) c", b=2)
        dG = [stage[:, x].rearrange("p a (b c) -> p (a b) c", b=2) for x in range(2)]
        with ExitStack() as s:
            act_a = sb("act_a", [P, FF2_TILES, SEQ], where=s)
            aH = sb("aH", [P, SPLIT, SEQ], F32R, where=s)
            aL = sb("aL", [P, SPLIT, SEQ], F32R, where=s)
            rows_f = sb("rows_f", [P, D], where=s)
        with ExitStack() as s:
            p_b = sb("p_b", [P, 2, 4, 384], where=s)
            pT_b = sb("pT_b", [P, 2, 4, 384], where=s)
            kT = sb("kT", [P, KD, SEQ], where=s)
            qT = sb("qT", [P, KD, SEQ], where=s)
            vt = sb("vt", [P, TT, D], where=s)
            x2H = sb("x2H", [P, KD, SEQ], F32R, where=s)
            x2L = sb("x2L", [P, KD, SEQ], F32R, where=s)
            slab = sb("slab", [P, B_HEADS, SEQ], where=s)
            st_b = sb("st_b", [P, 2, 3, 8], where=s)

        ps = [ctx.enter_context(nc.psum_tensor(f"ps{b}", [P, 512], F32)) for b in range(8)]

        x_in = sem("x_in")
        consts_in = sem("consts_in")
        slab_in = sem("slab_in")
        slab_masked = sem("slab_masked")
        early_in = sem("early_in")
        late_in = sem("late_in")
        final_in = sem("final_in")
        unit_in = [sem(f"unit_in{i}") for i in range(RAW)]
        hi_done = sem("hi_done")
        lo_done = sem("lo_done")
        unit_done = sem("unit_done")
        bank_free = sem("bank_free")
        unstaged = sem("unstaged")
        silu_done = sem("silu_done")
        prod_done = sem("prod_done")
        a_hi = sem("a_hi")
        a_lo = sem("a_lo")
        sq_done = sem("sq_done")
        ms_done = sem("ms_done")
        rstd_done = sem("rstd_done")
        xn_done = sem("xn_done")
        turned = sem("turned")
        val_dve = sem("val_dve")
        x_bank = sem("x_bank")
        x_hi = sem("x_hi")
        x_ready = sem("x_ready")
        res_done = sem("res_done")
        act_s = sem("act_s")
        dve_s = sem("dve_s")
        pool_s = sem("pool_s")
        c_ready = sem("c_ready")
        ba_done = sem("ba_done")
        ba_rows = sem("ba_rows")
        cond_ready = sem("cond_ready")
        mod_in = [sem(f"mod_in{i}") for i in range(RAW)]
        mod_used = sem("mod_used")
        mod_kept = sem("mod_kept")
        mod_out = sem("mod_out")
        mod_act = sem("mod_act")
        out_done = sem("out_done")
        g_act = sem("g_act")
        g_dve = sem("g_dve")
        g_sum = sem("g_sum")
        tok_pe = sem("tok_pe")
        tok_act = sem("tok_act")
        tok_dve = sem("tok_dve")
        tok_sq = sem("tok_sq")
        tok_ss = sem("tok_ss")
        back_pe = sem("back_pe")
        back_act = sem("back_act")
        back_dve = sem("back_dve")
        dg_dve = sem("dg_dve")
        row_pe = sem("row_pe")
        arg_dve = sem("arg_dve")
        exp_act = sem("exp_act")
        kq_pe = sem("kq_pe")
        m_dve = sem("m_dve")
        at_dve = sem("at_dve")
        mt_pe = sem("mt_pe")
        mt_act = sem("mt_act")
        dbl_pe = sem("dbl_pe")
        dbl_dve = sem("dbl_dve")
        scan_pe = sem("scan_pe")
        scan_act = sem("scan_act")
        scan_dve = sem("scan_dve")
        pw_in = sem("pw_in")
        pw_out = sem("pw_out")
        y_rows = sem("y_rows")
        y_pe = sem("y_pe")
        y_hi = sem("y_hi")
        y_ready = sem("y_ready")
        b_score = sem("b_score")
        b_max = sem("b_max")
        b_exp = sem("b_exp")
        b_prob = sem("b_prob")
        b_turn = sem("b_turn")
        b_tact = sem("b_tact")
        b_tdve = sem("b_tdve")
        m_dec = sem("m_dec")
        m_ck = sem("m_ck")
        m_state = sem("m_state")
        m_sact = sem("m_sact")
        m_rope = sem("m_rope")
        m_turn = sem("m_turn")
        m_tact = sem("m_tact")
        m_tdve = sem("m_tdve")
        m_w = sem("m_w")
        m_wd = sem("m_wd")
        m_s = sem("m_s")
        m_sd = sem("m_sd")
        m_o = sem("m_o")
        m_od = sem("m_od")
        gn_act = sem("gn_act")
        gn_dve = sem("gn_dve")
        q_rope = sem("q_rope")
        q_turn = sem("q_turn")
        q_tact = sem("q_tact")
        s_pe = sem("s_pe")
        s_max = sem("s_max")
        s_exp = sem("s_exp")
        s_prob = sem("s_prob")
        s_turn = sem("s_turn")
        s_tact = sem("s_tact")
        s_tdve = sem("s_tdve")

        def U(name):
            return 2 * BLOCKS[name][0]

        def halves(x, l, odd):
            s = 1 << l
            if odd is None:
                return x.rearrange("p (n s) -> p n s", s=s)
            return x.rearrange("p (n h s) -> p n h s", h=2, s=s)[:, :, odd]

        def mod_bank(h):
            name = MOD_CHUNK[h]
            if name == "wo_a":
                return ps[h % 2]
            if name == "wo_b":
                return ps[3]
            return ps[(BANK[name] + 3 - (h - MOD_AT[name][0])) % 4]

        class ModulationSteps:

            def __init__(self, pe):
                self.pe, self.m, self.out = pe, 0, 0

            def units(self, n):
                for _ in range(n):
                    h, u = divmod(self.m, 4)
                    if self.m == 0:
                        self.pe.wait_ge(cond_ready, 1)
                    if u == 0 and h >= 2:
                        self.pe.wait_ge(mod_act, h - 1)
                    name = MOD_CHUNK[h]
                    if u == 0:
                        self.pe.wait_ge(bank_free, BANK[name])
                    self.pe.wait_ge(mod_in[self.m % RAW], 16 * (self.m // RAW + 1))
                    for k in range(2):
                        last = nc.tensor.matmul(mod_bank(h)[0:2, :], cact[:, 2 * u + k],
                                                raw[:, (U(name) + self.m) % RAW, k * 512:(k + 1) * 512],
                                                start=u == 0 and k == 0, stop=u == 3 and k == 1)
                    last.then_inc(mod_used, 1)
                    self.m += 1

            def finish(self):
                h = self.out
                self.out += 1
                self.pe.wait_ge(mod_kept, h + 1)
                if (h // 2) % 3 < 2:
                    for k in range(4):
                        last = nc.tensor.matmul(mod_bank(h)[:, 2 * k:2 * k + 2], mrow[:, h % 2, k * P:(k + 1) * P],
                                                ident[0:2, 0:2], start=True, stop=True)
                else:
                    last = nc.tensor.matmul(mod_bank(h)[:], K_["ones"][0:1, :], mrow[0:1, h % 2], start=True, stop=True)
                last.then_inc(mod_out, 1)

        block = ctx.enter_context(nc.Block())
        K_ = {n: cst[:, o:o + c] for n, (o, c) in CONSTS.items()}
        ident = K_["ident"]

        def col(name, k, n=1):
            return cols[:, COLS[name][0] + k:COLS[name][0] + k + n]

        @block.sync
        def _(sp):
            def unit(i, per, c, src, kk):
                if not (isinstance(i, int) and c < RAW):
                    sp.wait_ge(lo_done, i * per + (c - RAW + 1))
                dst = raw[:, c % RAW]
                if kk > 1:
                    dst = dst.rearrange("p (k n) -> p k n", k=kk)
                sp.dma_start(dst, src).then_inc(unit_in[c % RAW], 16)

            def modulation(name):
                first, count = MOD_AT[name]
                c = U(name) + 4
                for m in range(4 * first, 4 * (first + count)):
                    n = m - 4 * first
                    if n < RAW:
                        sp.wait_ge(lo_done, c + n - RAW + 1)
                    else:
                        sp.wait_ge(mod_used, m - RAW + 1)
                    h, u = divmod(m, 4)
                    src = a["w_mod_2"][0].rearrange("(k p) n -> p k n", p=P)[:, 2 * u:2 * u + 2, h * 512:(h + 1) * 512]
                    sp.dma_start(raw[:, (c + n) % RAW].rearrange("p (k n) -> p k n", k=2), src).then_inc(mod_in[m % RAW], 16)

            def after_modulation(name, c):
                if name in MOD_AT and 4 <= c < 8:
                    sp.wait_ge(mod_used, 4 * sum(MOD_AT[name]) - RAW + c - 3)

            def feature_major(name, w, at):
                wk = w.rearrange("(k p) n -> p k n", p=P)

                def body(i, j):
                    if name in MOD_AT and BLOCKS[name][1] % 4 != 2 and isinstance(i, int) and j == 2:
                        modulation(name)
                    for f in range(2):
                        after_modulation(name, 2 * j + f)
                        unit(i, 8, U(name) + 2 * j + f, wk[:, :, bass.ds(at(i * 4 + j, f), P)], KD)
                turns(sp, BLOCKS[name][1], body,
                      between=(lambda: modulation(name)) if name in MOD_AT and BLOCKS[name][1] % 4 == 2 else None)

            def token_major(name, w, c0):
                wk = w.rearrange("(k p) n -> p k n", p=P)

                def body(i, j):
                    if name in MOD_AT and isinstance(i, int) and j == 2:
                        modulation(name)
                    for g in range(2):
                        after_modulation(name, 2 * j + g)
                        unit(i, 8, U(name) + 2 * j + g,
                             wk[:, 4 * g:4 * g + 4, bass.ds((i * 4 + j) * 256 + (c0(j) if callable(c0) else c0), 256)], 4)
                turns(sp, BLOCKS[name][1], body)

            def rows_of(name, w):
                wk = w.rearrange("(k p) n -> k p n", p=P)

                def body(i, j):
                    unit(i, 4, U(name) + j,
                         wk[one(i * 4 + j)].rearrange("a p n -> p (a n)"), 1)
                turns(sp, 2 * BLOCKS[name][1], body)

            sp.dma_start(h[:], a["x"].rearrange("o (t p) d -> p (o t) d", p=P)).then_inc(x_in, 16)
            sp.dma_start(cst[:], a["consts"]).then_inc(consts_in, 16)
            sp.dma_start(cols[:], a["cols"]).then_inc(consts_in, 16)
            feature_major("qkv", a["a_w_in"][0], lambda m, f: m * 256 + f * P)
            token_major("z", a["a_w_in"][0], 3 * D)
            token_major("wo_a", a["a_w_out"][0], 0)
            feature_major("up0", a["f_w_up"][0], lambda m, f: m * P + f * FF)
            rows_of("down0", a["f_w_down"][0])
            feature_major("k", a["w_kv"], lambda m, f: m * 256 + f * P)
            token_major("v", a["w_kv"], D)
            feature_major("q", a["b_w_q"][0], lambda m, f: m * 256 + f * P)
            token_major("wo_b", a["b_w_out"][0], 0)
            feature_major("up1", a["f_w_up"][1], lambda m, f: m * P + f * FF)
            rows_of("down1", a["f_w_down"][1])
            token_major("win", a["w_in_2"][0], lambda j: 256 * (WIN_ORDER[j] - j))
            token_major("wo_c", a["w_out_2"][0], 0)
            feature_major("ff1", a["w_ff1_2"][0], lambda m, f: m * 256 + f * P)
            rows_of("ff2", a["w_ff2_2"][0])
            for t in range(TT):
                sp.wait_ge(res_done, RES["fin"] - 1 + t)
                sp.dma_start(out[0, t * P:(t + 1) * P, :], h[:, t]).then_inc(out_done, 16)
            sp.wait_ge(out_done, 16 * TT)

        @block.tensor
        def _(pe):
            mm = nc.tensor.matmul

            def three(o, l, r, first, last, check=False):
                mm(o, l[0], r[0], start=first, stop=False, skip_group_check=check)
                mm(o, l[0], r[1], start=False, stop=False, skip_group_check=check)
                return mm(o, l[1], r[0], start=False, stop=last, skip_group_check=check)

            def bank(name, i, j):
                e = BANK[name] + j
                if not (isinstance(i, int) and e < 4):
                    pe.wait_ge(bank_free, i * 4 + (e - 3))
                return ps[e % 4]

            def w_unit(i, per, c):
                pe.wait_ge(lo_done, i * per + (c + 1))
                return [w[:, c % SPLIT] for w in (wH, wL)]

            def feature_major(name, x, between=None, n=None):
                def body(i, j):
                    if name in MOD_AT and isinstance(i, int) and j == 1:
                        pe.wait_ge(mod_act, sum(MOD_AT[name]))
                    b = bank(name, i, j)
                    for f in range(2):
                        w = [y.rearrange("p (k n) -> p k n", k=KD) for y in w_unit(i, 8, U(name) + 2 * j + f)]
                        for k in range(KD):
                            if n and isinstance(i, int) and j == 0 and f == 0 and k % 4 == 0:
                                pe.wait_ge(x_ready, 2 * SCALED[n] + k // 4 + 1)
                            last = three(b[:, f * SEQ:(f + 1) * SEQ], [y[:, k] for y in w],
                                         [y[:, k] for y in x], k == 0, k == KD - 1)
                        last.then_inc(unit_done, 1)
                turns(pe, BLOCKS[name][1], body, between=between)

            def token_block(banks, i, c, xs, n=None):
                for g in range(2):
                    if n:
                        pe.wait_ge(x_ready, 2 * SCALED[n] + g + 1)
                    w = [y.rearrange("p (k n) -> p k n", k=4) for y in w_unit(i, 8, c + g)]
                    for b, x in zip(banks, xs):
                        for t in range(TT):
                            for k in range(4):
                                last = three(b[:, t * 256:(t + 1) * 256],
                                             [y[:, 4 * g + k, t * P:(t + 1) * P] for y in x],
                                             [y[:, k] for y in w], g == 0 and t == 0 and k == 0,
                                             g == 1 and k == 3, check=True)
                    last.then_inc(unit_done, 1)

            def token_major(name, x):
                turns(pe, BLOCKS[name][1],
                      lambda i, j: token_block([bank(name, i, j)], i, U(name) + 2 * j, [x]))

            def down(name, count):
                acc = [ps[AUX + 2 * t + c] for t in range(TT) for c in range(2)]

                def body(i, j):
                    w = w_unit(i, 4, U(name) + j)
                    pe.wait_ge(a_lo, i * 4 + (ACTS[name] + j + 1))
                    first, last = isinstance(i, int) and j == 0, isinstance(i, int) and j == count - 1
                    for t in range(TT):
                        for c in range(2):
                            done = three(acc[2 * t + c][:], [y[:, j % SPLIT, t * P:(t + 1) * P] for y in (aH, aL)],
                                         [y[:, c * 512:(c + 1) * 512] for y in w], first, last, check=True)
                    done.then_inc(unit_done, 1)
                turns(pe, count, body)

            def turn_rows(n, rows=xn):
                for t in range(TT):
                    pe.wait_ge(xn_done, 2 * TURN[n] + t + 1)
                    for k in range(KD):
                        o = (k % 2) * SEQ + t * P
                        tr = nc.tensor.transpose(ps[AUX + k // 2][:, o:o + P], rows[:, t, k * P:(k + 1) * P], ident)
                        if t == 1 and k % 2:
                            tr.then_inc(turned, 1)

            def ready(n):
                pe.wait_ge(x_ready, 2 * SCALED[n] + 2)


            mod = ModulationSteps(pe)

            def delta_front_pe():
                def sums():
                    pe.wait_ge(g_dve, 4)
                    for t in range(TT):
                        mm(ps[7][:, 8 * t:8 * t + 8], K_["tri"], sm[:, 10, 8 * t:8 * t + 8], start=True, stop=True)
                    mm(ps[7][:, 16:24], K_["ones"], sm[:, 10, 0:8], start=True, stop=True).then_inc(g_sum, 1)

                def square_sums():
                    pe.wait_ge(tok_sq, 2)
                    pe.wait_ge(g_dve, 5)
                    for t in range(TT):
                        for n in range(16):
                            sq = (T_, MT)[n // 8].rearrange("p (h t) n -> p h (t n)", t=TT)
                            last = mm(ps[7][:, 32 + 16 * t + n:33 + 16 * t + n], sq[:, n % 8, t * P:(t + 1) * P],
                                      K_["ones"][:, 0:1], start=True, stop=True)
                    last.then_inc(tok_ss, 1)

                def row(g):
                    pe.wait_ge(dg_dve, g + 1)
                    if g >= 2:
                        pe.wait_ge(arg_dve, g - 1)
                    mm(ps[AUX + g % 2][:], K_["ones"], dG[g % 2].rearrange("p a b -> p (a b)"),
                       start=True, stop=True).then_inc(row_pe, 1)

                def to_tok(q):
                    bank, free = TOK_BANK[q]
                    for which, n in free:
                        pe.wait_ge({"act": tok_act, "dve": tok_dve, "arg": arg_dve, "pw": pw_in}[which], n)
                    f0, t = TOK_HEAD[q]
                    for f in range(4):
                        tr = nc.tensor.transpose(ps[bank][:, f * P:(f + 1) * P],
                                                 feat[:, f0 + f, t * P:(t + 1) * P], ident)
                    tr.then_inc(tok_pe, 1)

                def to_feat(q):
                    h0 = BACK_HEAD[q]
                    pe.wait_ge(tok_dve, 4 if h0 >= 8 else 8)
                    if q < 4:
                        pe.wait_ge(tok_dve, 5 + q)
                    else:
                        pe.wait_ge((back_act, back_dve)[q % 2], q // 2 - 1)
                    for f in range(2):
                        for t in range(TT):
                            tr = nc.tensor.transpose(ps[AUX + q % 4][:, f * SEQ + t * P:f * SEQ + (t + 1) * P],
                                                     tok[:, t, h0 + f], ident)
                    tr.then_inc(back_pe, 1)

                def z(j):
                    token_block([bank("z", 0, j)], 0, U("z") + 2 * j, [X])
                sums()
                z(0)
                square_sums()
                row(0)
                row(1)
                for q in range(4):
                    to_tok(q)
                row(2)
                row(3)
                z(1)
                for q in range(4, 8):
                    to_tok(q)
                z(2)
                for q in range(8, 12):
                    to_tok(q)
                z(3)
                for q in range(8):
                    to_feat(q)

            def delta_pe():
                pe.wait_ge(bank_free, BANK["z"] + 4)
                mod.units(4)
                pe.wait_ge(back_act, 4)
                pe.wait_ge(back_dve, 4)

                def products(g):
                    t, h0 = g // 2, 4 * (g % 2)
                    if g >= 2:
                        pe.wait_ge(at_dve, g - 1)
                    for x in range(4):
                        k = feat[:, 8 + h0 + x, t * P:(t + 1) * P]
                        mm(ps[4 + g % 2][:, x * P:(x + 1) * P], k, k, start=True, stop=True)
                        last = mm(ps[6 + g % 2][:, x * P:(x + 1) * P], k, feat[:, h0 + x, t * P:(t + 1) * P],
                                  start=True, stop=True)
                    last.then_inc(kq_pe, 1)

                def turn_m(g):
                    pe.wait_ge(m_dve, g + 1)
                    if g >= 2:
                        pe.wait_ge(mt_act, g - 1)
                    for x in range(4):
                        tr = nc.tensor.transpose(ps[2 + g % 2][:, x * P:(x + 1) * P], T_[:, 4 * g + x], ident)
                    tr.then_inc(mt_pe, 1)
                products(0)
                for g in range(1, 4):
                    products(g)
                    turn_m(g - 1)
                turn_m(3)
                mod.units(4)

                for l in range(LEVELS):
                    for step in range(3):
                        if l == LEVELS - 1 and step == 1:
                            continue
                        for g in range(4):
                            k = l * 12 + step * 4 + g
                            pe.wait_ge(dbl_dve, max(k + 1 - (4 if l == LEVELS - 1 and step == 2 else 0), 4))
                            for x in range(4 * g, 4 * g + 4):
                                lhs, rhs = ((MT, T_), (U_, P_), (P_, U_))[step]
                                o = ps[AUX + g][:, (x % 4) * P:(x % 4 + 1) * P]
                                if step == 0:
                                    last = mm(o, lhs[:, x], rhs[:, x], start=True, stop=True)
                                else:
                                    last = mm(halves(o[:, 0:64], l + 1, None), lhs[:, x], halves(rhs[:, x], l + 1, step - 1),
                                              start=True, stop=True)
                            last.then_inc(dbl_pe, 1)

                def heads(bank, lhs, rhs):
                    for hb in range(2):
                        for x in range(4):
                            n = 4 * hb + x
                            last = mm(ps[bank + hb][:, x * P:(x + 1) * P], lhs(n), rhs(n), start=True, stop=True)
                        last.then_inc(scan_pe, 1)
                pe.wait_ge(dbl_dve, 12 * LEVELS)
                pe.wait_ge(scan_dve, 1)
                heads(4, lambda n: U_[:, n], lambda n: tok[:, 0, 16 + n])
                mod.finish()
                mod.finish()
                pe.wait_ge(scan_act, 2)
                pe.wait_ge(scan_dve, 2)
                heads(6, lambda n: tok[:, 0, 8 + n], lambda n: P_[:, n])
                mod.units(1)
                pe.wait_ge(scan_act, 4)
                heads(4, lambda n: feat[:, 8 + n, P:2 * P], lambda n: T_[:, n])
                heads(6, lambda n: feat[:, n, P:2 * P], lambda n: T_[:, n])
                mod.units(1)
                pe.wait_ge(scan_dve, 4)
                heads(4, lambda n: AT[:, n], lambda n: P_[:, n])
                pe.wait_ge(scan_dve, 7)
                mod.units(1)
                heads(6, lambda n: U_[:, 8 + n], lambda n: T_[:, 8 + n])
                mod.units(1)
                pe.wait_ge(scan_act, 8)
                heads(4, lambda n: AT[:, 8 + n], lambda n: P_[:, 8 + n])
                mod.units(4)
                mod.finish()
                mod.finish()
                mod.units(4)
                pe.wait_ge(y_rows, 1)
                for b in range(4):
                    for k in range(2 * b, 2 * b + 2):
                        for t in range(TT):
                            o = (k % 2) * SEQ + t * P
                            tr = nc.tensor.transpose(ps[AUX + b][:, o:o + P], tok[:, t, k], ident)
                    tr.then_inc(y_pe, 1)
                mod.finish()

            def band_pe():
                pe.wait_ge(bank_free, BANK["q"] + 4)
                pe.wait_ge(slab_masked, 1)

                def scores(g):
                    if g:
                        pe.wait_ge(b_max, g)
                    for x in range(4):
                        n, r, o = 4 * g + x, 64 * (x % 2), x // 2
                        q, k = qT[r:r + 64, n // 2], kT[r:r + 64, n // 2]
                        mm(ps[4 + x % 2][:, o * 256:(o + 1) * 256], q[:, P:], k, start=True, stop=True)
                        last = mm(ps[6 + x % 2][:, o * P:(o + 1) * P], q[:, 0:P], k[:, 0:P], start=True, stop=True)
                    last.then_inc(b_score, 1)
                scores(0)
                scores(1)
                mod.units(4)
                mod.finish()
                for g in range(4):
                    pe.wait_ge(b_prob, g + 1)
                    for d in range(3):
                        if g:
                            pe.wait_ge((b_tact, b_tdve)[d % 2], (2 * g, g)[d % 2])
                        for x in (range(2 * d, 2 * d + 2) if d < 2 else range(4)):
                            for o, c in (((0, 256), (P, 0)) if d < 2 else ((2 * P, P),)):
                                at = (x % 2) * 256 + o if d < 2 else x * P
                                tr = nc.tensor.transpose(ps[d][:, at:at + P], p_b[:, g % 2, x, c:c + P], ident)
                        tr.then_inc(b_turn, 1)
                    if g < 2:
                        scores(g + 2)
                    pe.wait_ge(b_tact, 2 * g + 2)
                    pe.wait_ge(b_tdve, g + 1)
                    if g:
                        pe.wait_ge(y_ready, 4 + g)
                    else:
                        pe.wait_ge(mod_act, sum(MOD_AT["wo_b"]))
                    for x in range(4):
                        n, r, o = 4 * g + x, 64 * (x % 2), (x // 2) * SEQ
                        mm(ps[3][r:r + 64, o:o + SEQ], vt[:, 0, n * BH:(n + 1) * BH], pT_b[:, g % 2, x, 0:256],
                           start=True, stop=False)
                        last = mm(ps[3][r:r + 64, o + P:o + SEQ], vt[:, 1, n * BH:(n + 1) * BH],
                                  pT_b[:, g % 2, x, 256:384], start=False, stop=True)
                    last.then_inc(y_pe, 1)

            def states():
                pe.wait_ge(q_tact, 3)
                pe.wait_ge(m_ck, 4)
                for d in range(2):
                    for n in range(RET_H):
                        for t in range(TT):
                            last = mm(ps[4 + d][:, n * P:(n + 1) * P], rope[:, t, d * 512 + n * P:d * 512 + (n + 1) * P],
                                      ckv[:, t, 512 + n * P:512 + (n + 1) * P], start=t == 0, stop=t == 1)
                    last.then_inc(m_state, 1)

            def turn_ret():
                pe.wait_ge(m_sact, 2)
                pe.wait_ge(m_rope, 2)
                for b in range(4):
                    for f in range(2):
                        for t in range(TT):
                            o = f * SEQ + t * P
                            tr = nc.tensor.transpose(ps[AUX + b][:, o:o + P],
                                                     qk_t[:, t, (2 * b + f) * P:(2 * b + f + 1) * P], ident)
                    tr.then_inc(m_turn, 1)

            def turn_att():
                pe.wait_ge(q_rope, 2)
                for b in range(2):
                    for f in range(2):
                        for t in range(TT):
                            o = f * SEQ + t * P
                            w = 2 * (2 * b + f)
                            tr = nc.tensor.transpose(ps[4 + b][:, o:o + P], aqn[:, t, w:w + 2].rearrange("p a b -> p (a b)"), ident)
                    tr.then_inc(q_turn, 1)
                for t in range(TT):
                    nc.tensor.transpose(ps[6][:, t * P:(t + 1) * P], kcn[:, t].rearrange("p a b -> p (a b)"), ident)
                    tr = nc.tensor.transpose(ps[6][:, SEQ + t * P:SEQ + (t + 1) * P],
                                             aqn[:, t, 8:10].rearrange("p a b -> p (a b)"), ident)
                tr.then_inc(q_turn, 1)

            def mix_pe():
                pe.wait_ge(bank_free, BANK["wo_c"])
                pe.wait_ge(m_tact, 2)
                pe.wait_ge(m_tdve, 2)

                def ret_scores(x):
                    n = DECAYS[x]
                    if x >= 2:
                        pe.wait_ge(m_sd, x - 1)
                    for j in range(TT):
                        last = mm(ps[4 + x % 2][:, j * SEQ:(j + 1) * SEQ], rkT[:, n, j * P:(j + 1) * P], rqT[:, n],
                                  start=True, stop=True)
                    last.then_inc(m_s, 1)

                def ret_outputs(x):
                    n = DECAYS[x]
                    pe.wait_ge(m_sd, x + 1)
                    if x >= 2:
                        pe.wait_ge(m_od, x - 1)
                    b = 0 if x % 2 else 6
                    for t in range(TT):
                        for j in range(TT):
                            mm(ps[b][:, t * P:(t + 1) * P], sT[n][:, j * SEQ + t * P:j * SEQ + (t + 1) * P],
                               rv[:, j, n * P:(n + 1) * P], start=j == 0, stop=j == 1)
                    for d in range(2):
                        for t in range(TT):
                            o = ps[b + d][:, 256 * (1 - d) + t * P:256 * (1 - d) + (t + 1) * P]
                            last = mm(o, rqT[:, n, t * P:(t + 1) * P], s_fb[:, d, n], start=True, stop=True)
                    last.then_inc(m_o, 1)
                ret_scores(0)
                ret_scores(1)
                for n in range(RET_H):
                    ret_outputs(n)
                    if n < 2:
                        ret_scores(n + 2)
                pe.wait_ge(m_sd, RET_H)
                pe.wait_ge(m_od, RET_H - 1)

                def scores(j):
                    if j:
                        pe.wait_ge(s_exp, 4 * j)
                    for s in range(2):
                        for t in range(TT):
                            mm(ps[4 + 2 * s + t][:], aqT[64 * s:64 * s + 64, j, t * P:(t + 1) * P],
                               akT[64 * s:64 * s + 64], start=True, stop=True).then_inc(s_pe, 1)
                scores(0)
                pe.wait_ge(m_od, RET_H)
                for j in range(4):
                    for n in ATT_BANKS:
                        s, kp = n // 2, n % 2
                        pe.wait_ge(s_prob, 4 * j + 2 * s + 2)
                        if j and n == 0:
                            pe.wait_ge(y_ready, 8 + j)
                        for k in range(2):
                            for t in range(TT):
                                o, c = k * SEQ + t * P, (2 * kp + k) * P
                                tr = nc.tensor.transpose(ps[n][:, o:o + P], ap_[:, s, t, c:c + P], ident)
                        tr.then_inc(s_turn, 1)
                    if j < 3:
                        scores(j + 1)
                    else:
                        pe.wait_ge(y_rows, 2)
                        pe.wait_ge(s_exp, 16)
                        for b in range(2):
                            for f in range(2):
                                for t in range(TT):
                                    o = f * SEQ + t * P
                                    tr = nc.tensor.transpose(ps[4 + b][:, o:o + P], o_r[:, t, 2 * b + f], ident)
                            tr.then_inc(y_pe, 1)
                    pe.wait_ge(s_tact, 2 * j + 2)
                    pe.wait_ge(s_tdve, 2 * j + 2)
                    r = 64 * (j % 2)
                    for s in range(2):
                        for k in range(4):
                            v = (cakv[:, k, P + 64 * s:P + 64 * s + 64] if k < 2
                                 else aqkv[:, k - 2, 640 + 64 * s:704 + 64 * s])
                            last = mm(ps[0][r:r + 64, s * SEQ:(s + 1) * SEQ], v, apT[:, s, k], start=k == 0, stop=k == 3)
                    last.then_inc(y_pe, 1)

            X = [xH, xL]
            pe.wait_ge(consts_in, 48)
            turn_rows("a")
            ready("a")
            pe.wait_ge(c_ready, 1)
            for k in range(KD):
                last = three(ps[AUX][0:16, 0:SEQ], [baH[:, k], baL[:, k]], [y[:, k] for y in X], k == 0, k == KD - 1)
            last.then_inc(ba_done, 1)
            pe.wait_ge(ba_rows, 1)
            for t in range(TT):
                last = nc.tensor.transpose(ps[AUX + 1][:, 16 * t:16 * t + 16], stage[0:16, 0, 0, t * P:(t + 1) * P],
                                           ident[0:16, 0:16])
            last.then_inc(ba_done, 1)
            feature_major("qkv", X)
            delta_front_pe()
            delta_pe()
            pe.wait_ge(y_ready, 4)
            pe.wait_ge(mod_act, sum(MOD_AT["wo_a"]))
            token_major("wo_a", X)
            mod.units(3)
            turn_rows("f0")
            mod.units(1)
            mod.finish()
            feature_major("up0", X, n="f0")
            down("down0", F_TILES)
            mod.units(3)
            turn_rows("kv")
            mod.units(1)
            mod.finish()
            feature_major("k", X, n="kv")
            token_major("v", X)
            ready("q")
            feature_major("q", [x2H, x2L])
            band_pe()
            pe.wait_ge(y_ready, 8)
            token_major("wo_b", X)
            mod.units(3)
            turn_rows("f1")
            mod.units(1)
            mod.finish()
            feature_major("up1", X, n="f1", between=lambda: turn_rows("ctx", ctx_in))
            ready("ctx")
            down("down1", F_TILES)
            mod.units(7)
            turn_rows("n1")
            mod.units(1)
            mod.finish()
            mod.finish()
            e = BANK["win"]
            for y, m in enumerate(WIN_ORDER):
                xs = [X, [xcH, xcL]] if m in CTX_BLOCKS else [X]
                pe.wait_ge(bank_free, e + len(xs) - 4)
                if y == 1:
                    pe.wait_ge(mod_act, sum(MOD_AT["win"]))
                token_block([ps[(e + b) % 4] for b in range(len(xs))], 0, U("win") + 2 * y, xs, None if y else "n1")
                e += len(xs)
                if y == 6:
                    turn_att()
                if y == 9:
                    states()
            turn_ret()
            mix_pe()
            pe.wait_ge(y_ready, 8 + 2 + 4)
            token_major("wo_c", X)
            mod.units(3)
            turn_rows("n2")
            mod.units(1)
            mod.finish()
            feature_major("ff1", X, n="n2")
            down("ff2", FF2_TILES)

        @block.scalar
        def _(act):
            st = Steps(act, act_s)
            fn = nc.scalar.activation

            def hi(i, per, c):
                if isinstance(i, int) and c >= UNITS:
                    return
                act.wait_ge(unit_in[c % RAW], i * (16 * per // RAW) + 16 * (c // RAW + 1))
                if not (isinstance(i, int) and c < SPLIT):
                    act.wait_ge(unit_done, i * per + (c - SPLIT + 1))
                fn(wH[:, c % SPLIT], raw[:, c % RAW], ACT.Copy).then_inc(hi_done, 1)

            def ahead(i, c):
                hi(i, 8, c + SPLIT)
                hi(i, 8, c + SPLIT + 1)

            def blocks(name, evacuate, after=None):
                def body(i, j):
                    act.wait_ge(unit_done, i * 8 + (U(name) + 2 * j + 2))
                    evacuate(i, j, ps[(BANK[name] + j) % 4]).then_inc(bank_free, 1)
                    ahead(i, U(name) + 2 * j)
                    if after:
                        after(i, j)
                turns(act, BLOCKS[name][1], body)

            def projected(name):
                def before(i, j):
                    if j == 3:
                        act.wait_ge(unstaged, STAGED[name] + 3)
                        for t in range(TT):
                            fn(xn[:, t, 0:768], h[:, t, 0:768], ACT.Square, accum_out=ssq_part[:, t:t + 1])
                staging(name, before=before)
                act.wait_ge(unstaged, STAGED[name] + 4)
                for t in range(TT):
                    fn(xn[:, t, 768:], h[:, t, 768:], ACT.Square, accum_out=ssq[:, t:t + 1]).then_inc(sq_done, 1)

            def staging(name, func=ACT.Copy, after=None, between=None, before=None, before_last=None):
                def body(i, j):
                    n = STAGED[name] + j
                    if before:
                        before(i, j)
                    act.wait_ge(unit_done, i * 8 + (U(name) + 2 * j + 2))
                    if not (isinstance(i, int) and n < 2):
                        act.wait_ge(unstaged, i * 4 + (n - 1))
                    b = ps[(BANK[name] + j) % 4]
                    fn(stage[:, n % 2].rearrange("p a b -> p (a b)"), b[:], func).then_inc(bank_free, 1)
                    ahead(i, U(name) + 2 * j)
                    if after:
                        after(i, j)
                turns(act, BLOCKS[name][1], body, between=between, before_last=before_last)

            def made(name, m):
                if name == "ff2":
                    act.wait_ge(unstaged, STAGED["ff1"] + m // 2 + 1)
                else:
                    act.wait_ge(prod_done, PRODS[name] + m + 1)

            def first_tiles(name):
                def parts():
                    made(name, SPLIT - 1)
                    for m in range(SPLIT):
                        fn(aH[:, m], act_a[:, m], ACT.Copy).then_inc(a_hi, 1)
                return parts

            def down(name, count):
                def part(i, j):
                    m = j + SPLIT
                    act.wait_ge(unit_done, i * 4 + (U(name) + j + 1))
                    fn(aH[:, m % SPLIT], act_a[:, one(i * 4 + m)].rearrange("p a n -> p (a n)"),
                       ACT.Copy).then_inc(a_hi, 1)

                def body(i, j):
                    hi(i, 4, U(name) + j + SPLIT)
                    part(i, j)
                made(name, count - 1)
                turns(act, count - SPLIT, body)
                for j in range(count - SPLIT, count):
                    hi(0, 4, U(name) + j + SPLIT)

            def squares(n, src, other=xn, after=None):
                for t in range(TT):
                    if after:
                        act.wait_ge(res_done, after(t))
                    fn(other[:, t], src[:, t], ACT.Square, accum_out=ssq[:, t:t + 1]).then_inc(sq_done, 1)

            def scaled(n, turn, gain, bias, oH, xv=xv):
                e = SCALED[n]
                if e:
                    act.wait_ge(x_ready, 2 * e)
                if n in GAINED:
                    for b in range(4):
                        act.wait_ge(turned, 4 * TURN[turn] + b + 1)
                        for k in (2 * b, 2 * b + 1):
                            last = fn(oH[:, k], ps[AUX + b][:, (k % 2) * SEQ:(k % 2 + 1) * SEQ], ACT.Identity, scale=gain(k))
                        last.then_inc(x_bank, 1)
                    return
                e = SHIFTED[n]
                act.wait_ge(turned, 4 * TURN[turn] + 2)
                for k in range(4):
                    s = st.put(fn(xv[:, k], ps[AUX + k // 2][:, (k % 2) * SEQ:(k % 2 + 1) * SEQ],
                                  ACT.Identity, scale=gain(k), bias=bias(k)))
                st.wait(s)
                fn(oH[:, 0:4], xv[:, 0:4], ACT.Copy).then_inc(x_hi, 1)
                act.wait_ge(val_dve, 4 * (e + 1))
                fn(oH[:, 4:8], xv[:, 4:8], ACT.Copy).then_inc(x_hi, 1)

            def no(k):
                return 0.0

            def cp(o, i, **kw):
                return fn(o, i, ACT.Copy, **kw)

            def gates_act():
                act.wait_ge(g_dve, 1)
                ba = sm[:, 12:14, 0:16]
                fn(sm[:, 2, 0:16].rearrange("p (t n) -> p t n", t=TT), ba[:, :, 0:8], ACT.Exp, scale=-1.0)
                fn(sm[:, 14, 0:8], rows_a[:, 128:136], ACT.Exp)
                fn(sm[:, 15, 0:8], rows_a[:, 144:152], ACT.Exp).then_inc(g_act, 1)
                act.wait_ge(g_dve, 2)
                fn(sm[:, 4, 0:16], sm[:, 3, 0:16], ACT.Exp).then_inc(g_act, 1)
                act.wait_ge(g_dve, 3)
                fn(sm[:, 6], sm[:, 5], ACT.Ln).then_inc(g_act, 1)

            def mod_keep():
                h = mods[0]
                mods[0] += 1
                act.wait_ge(mod_used, 4 * (h + 1))
                if h >= 2:
                    act.wait_ge(mod_out, h - 1)
                fn(mrow[:, h % 2], mod_bank(h)[0:2, :], ACT.Copy).then_inc(mod_kept, 1)

            def mod_place():
                h = mods[1]
                mods[1] += 1
                g, half = divmod(h, 2)
                act.wait_ge(mod_out, h + 1)
                if g % 3 < 2:
                    o = 8 * (g if g < 3 else g - 1) + 4 * half
                    last = fn(modc[:, o:o + 4], mod_bank(h)[:, 0:8].rearrange("p (k c) -> p k c", c=2), ACT.Copy)
                else:
                    last = fn((gate1, gate2)[g // 3][:, half * 512:(half + 1) * 512], mod_bank(h)[:], ACT.Copy)
                last.then_inc(mod_act, 1)
            mods = [0, 0]

            def delta_front_act():
                act.wait_ge(silu_done, 12)
                fq = feat[:].rearrange("p h n -> p (h n)")
                for x, o in enumerate((T_, MT)):
                    fn(o[:].rearrange("p h n -> p (h n)"), fq[:, x * 2048:(x + 1) * 2048], ACT.Square).then_inc(tok_sq, 1)

                def z(j):
                    act.wait_ge(unit_done, U("z") + 2 * j + 2)
                    fn(zs[:, :, j * 256:(j + 1) * 256], ps[(BANK["z"] + j) % 4][:].rearrange("p (t n) -> p t n", t=TT),
                       ACT.Silu).then_inc(bank_free, 1)
                    ahead(0, U("z") + 2 * j)

                def decays(g):
                    act.wait_ge(arg_dve, g + 1)
                    fn(U_[:, 4 * g:4 * g + 4], U_[:, 4 * g:4 * g + 4], ACT.Exp)
                    fn(AT[:, 4 * g:4 * g + 4], AT[:, 4 * g:4 * g + 4], ACT.Exp).then_inc(exp_act, 1)

                def v_tok(q):
                    f0, t = TOK_HEAD[q]
                    act.wait_ge(tok_pe, q + 1)
                    cp(tok[:, t, f0:f0 + 4].rearrange("p a b -> p (a b)"), ps[TOK_BANK[q][0]][:]).then_inc(tok_act, 1)
                z(0)
                act.wait_ge(g_dve, 5)
                fn(sm[:, 17, 0:16], sm[:, 16, 0:16], ACT.Exp)
                fn(sm[:, 19, 0:8], sm[:, 18, 0:8], ACT.Exp).then_inc(g_act, 1)
                for q in range(4):
                    v_tok(q)
                decays(0)
                decays(1)
                z(1)
                decays(2)
                decays(3)
                z(2)
                z(3)
                for q in range(0, 8, 2):
                    act.wait_ge(back_pe, q + 1)
                    cp(feat[:, BACK_HEAD[q]:BACK_HEAD[q] + 2].rearrange("p a b -> p (a b)"),
                       ps[AUX + q % 4][:]).then_inc(back_act, 1)

            def delta_act():
                for g in range(4):
                    act.wait_ge(mt_pe, g + 1)
                    cp(MT[:, 4 * g:4 * g + 4].rearrange("p a b -> p (a b)"), ps[2 + g % 2][:]).then_inc(mt_act, 1)
                mod_keep()
                mod_keep()

                def banks(first, bank, o):
                    for hb in range(2):
                        act.wait_ge(scan_pe, first + hb)
                        cp(o(4 * hb), ps[bank + hb][:].rearrange("p (a b) -> p a b", a=4)).then_inc(scan_act, 1)
                banks(1, 4, lambda n: P_[:, n:n + 4])
                mod_place()
                mod_place()
                banks(3, 6, lambda n: T_[:, n:n + 4])
                banks(9, 4, lambda n: tok[:, 0, n:n + 4])
                banks(11, 6, lambda n: P_[:, 8 + n:12 + n])
                mod_keep()
                mod_keep()
                mod_place()
                mod_place()
                mod_keep()
                for b in range(4):
                    act.wait_ge(y_pe, b + 1)
                    cp(xH[:, 2 * b:2 * b + 2].rearrange("p a b -> p (a b)"), ps[AUX + b][:]).then_inc(y_hi, 1)
                mod_place()

            def band_act():
                def exps(g):
                    b = g % 2
                    act.wait_ge(b_max, g + 1)
                    for x in range(4):
                        for t in range(TT):
                            c = slice(0, 256) if t else slice(256, 384)
                            e = fn(p_b[:, b, x, c], p_b[:, b, x, c], ACT.Exp, bias=st_b[:, b, 1, 2 * x + t:2 * x + t + 1],
                                   accum_out=st_b[:, b, 2, 2 * x + t:2 * x + t + 1])
                            e.then_inc(b_exp, 1)
                exps(0)
                exps(1)
                mod_keep()
                mod_place()

                def turned_probs(g):
                    act.wait_ge(b_turn, 3 * g + 1)
                    cp(pT_b[:, g % 2, 0:2, 0:256], ps[0][:].rearrange("p (x n) -> p x n", x=2)).then_inc(b_tact, 1)
                    act.wait_ge(b_turn, 3 * g + 3)
                    cp(pT_b[:, g % 2, :, 256:384], ps[2][:].rearrange("p (x n) -> p x n", x=4)).then_inc(b_tact, 1)
                turned_probs(0)
                for g in range(4):
                    act.wait_ge(y_pe, 4 + g + 1)
                    cp(xH[:, 2 * g:2 * g + 2].rearrange("p a b -> p (a b)"), ps[3][:]).then_inc(y_hi, 1)
                    if g < 3:
                        turned_probs(g + 1)
                    if g < 2:
                        exps(g + 2)

            def decay(x):
                act.wait_ge(m_rope, 2) if x == 0 else act.wait_ge(m_wd, x)
                for d, name in enumerate(("fwd", "bwd")):
                    o, n = TABLES[name][0], DECAYS[x]
                    last = fn(wt[:, d], tb[:, o:o + 512], ACT.Exp, scale=lg[:, 4 * d + n:4 * d + n + 1])
                last.then_inc(m_w, 1)

            def mix_act():
                def exps(j):
                    for s in range(2):
                        for t in range(TT):
                            n = 2 * s + t
                            act.wait_ge(s_max, 4 * j + n + 1)
                            if j:
                                act.wait_ge(s_turn, 4 * j)
                            fn(ap_[:, s, t], ps[4 + n][:], ACT.Exp, bias=st_p[:, 1, n:n + 1], scale=ATT_D ** -0.5,
                               accum_out=st_p[:, 2, n:n + 1]).then_inc(s_exp, 1)
                for b in (0, 2):
                    act.wait_ge(m_turn, b + 1)
                    o = rkT if b else rqT
                    cp(o[:, 0:2].rearrange("p a b -> p (a b)"), ps[AUX + b][:]).then_inc(m_tact, 1)
                decay(2)
                ahead(0, U("win") + 20)
                decay(3)
                junk = rope[:].rearrange("p t (n c) -> p (t n) c", c=P)
                for x, n in enumerate(DECAYS):
                    act.wait_ge(m_od, x + 1)
                    for t in range(TT):
                        last = fn(junk[:, 4 * t + n], o_r[:, t, n], ACT.Copy, accum_out=st_r[:, 0, 4 * t + n:4 * t + n + 1])
                last.then_inc(gn_act, 1)

                def normed(part):
                    act.wait_ge(gn_dve, part)
                    for n in range(RET_H):
                        for t in range(TT):
                            o, c = o_r[:, t, n], slice(4 * t + n, 4 * t + n + 1)
                            if part == 1:
                                last = fn(junk[:, 8 + 4 * t + n], o, ACT.Square, bias=st_r[:, 0, c], accum_out=st_r[:, 1, c])
                            else:
                                last = fn(o, o, ACT.Identity, scale=st_r[:, 3, c], bias=st_r[:, 2, c])
                    last.then_inc(gn_act, 1)
                exps(0)
                normed(1)
                for j in range(4):
                    for x in (1, 3):
                        n = ATT_BANKS[x]
                        act.wait_ge(s_turn, 4 * j + x + 1)
                        cp(apT[:, n // 2, 2 * (n % 2):2 * (n % 2) + 2].rearrange("p a b -> p (a b)"),
                           ps[n][:]).then_inc(s_tact, 1)
                    if j < 3:
                        exps(j + 1)
                    else:
                        for b in range(2):
                            act.wait_ge(y_pe, 11 + b + 1)
                            cp(xH[:, 2 * b:2 * b + 2].rearrange("p a b -> p (a b)"), ps[4 + b][:]).then_inc(y_hi, 1)
                    if j == 1:
                        normed(2)
                    act.wait_ge(y_pe, (9, 10, 11, 14)[j])
                    r = 64 * (j % 2)
                    cp(xH[r:r + 64, 4 + j // 2:8:2], ps[0][r:r + 64].rearrange("p (a b) -> p a b", a=2)).then_inc(y_hi, 1)

            act.dma_start(rows_a[:], a["rows_a"].partition_broadcast(P).rearrange("p a n -> p (a n)")).then_inc(consts_in, 16)
            act.dma_start(baw[:], a["a_w_in"][0].rearrange("(k p) n -> p k n", p=P)[:, :, 4 * D:4 * D + 16]).then_inc(early_in, 16)
            act.wait_ge(x_in, 16)
            squares("a", h)
            act.wait_ge(consts_in, 48)
            fn(cact[:].rearrange("p k a -> p a k"), col("c", 0, 16).rearrange("p (a k) -> p a k", a=2),
               ACT.Silu).then_inc(cond_ready, 1)
            act.wait_ge(early_in, 16)
            st.put(fn(baH[:], baw[:], ACT.Copy))
            hi(0, 0, 0)
            scaled("a", "a", lambda k: col("a_norm", k), no, xH)
            hi(0, 0, 1)
            hi(0, 0, 2)
            hi(0, 0, 3)
            gates_act()

            def silu_a(i, j):
                n = STAGED["qkv"] + j
                act.wait_ge(unstaged, i * 4 + (n + 1))
                fn(feat[:, bass.ds((i * 4 + j) * 2, 2)], cv[:, n % 2], ACT.Silu).then_inc(silu_done, 1)
            staging("qkv", after=silu_a)
            delta_front_act()
            delta_act()
            projected("wo_a")

            def silu_f(which):
                def after(i, j):
                    n = STAGED[which] + j
                    act.wait_ge(unstaged, i * 4 + (n + 1))
                    fn(cv[:, n % 2, 0], cv[:, n % 2, 0], ACT.Silu).then_inc(silu_done, 1)
                return after

            def ffn(l):
                n = f"f{l}"
                if l == 1:
                    act.wait_ge(late_in, 80)
                    act.wait_ge(ms_done, STAT["f1"] + 1)
                    squares("ctx", ctx_in, xvc[:].rearrange("p (t k) n -> p t (k n)", t=TT))
                scaled(n, n, lambda k: col(f"f_norm{l}", k), no, xH)
                mod_keep()
                mod_place()
                staging(f"up{l}", after=silu_f(f"up{l}"), before_last=first_tiles(f"down{l}"), between=None if l == 0 else lambda: scaled(
                    "ctx", "ctx", lambda k: gs1[:, k, 1:2], lambda k: modc[:, k, 1:2], xcH, xvc))
                down(f"down{l}", F_TILES)
            ffn(0)
            squares("kv", h, after=lambda t: RES["down0"] - 2 + 2 * t)
            scaled("kv", "kv", lambda k: col("kv_norm", k), no, xH)
            mod_keep()
            mod_place()
            scaled("q", "kv", lambda k: col("b_norm", k), no, x2H)

            def two(buf, scale=1.0):
                return lambda i, j, b: fn(buf[:, bass.ds((i * 4 + j) * 2, 2)], b[:].rearrange("p (f n) -> p f n", f=2),
                                          ACT.Copy, scale=scale)
            blocks("k", two(kT))
            blocks("v", lambda i, j, b: fn(vt[:, :, bass.ds((i * 4 + j) * 256, 256)],
                                           b[:].rearrange("p (t n) -> p t n", t=TT), ACT.Copy))
            blocks("q", two(qT, BH ** -0.5))
            band_act()
            projected("wo_b")
            ffn(1)
            squares("x2", h, after=lambda t: RES["down1"] - 2 + 2 * t)
            squares("n1", h, after=lambda t: RES["x2"] - 1 + t)
            mod_keep()
            scaled("n1", "n1", lambda k: gs1[:, k, 0:1], lambda k: modc[:, k, 0:1], xH)
            mod_keep()
            mod_place()
            mod_place()
            e = BANK["win"]
            for y, m in enumerate(WIN_ORDER):
                act.wait_ge(unit_done, U("win") + 2 * y + 2)
                b = ps[e % 4][:].rearrange("p (t n) -> p t n", t=TT)
                if m < 4:
                    o, f = qk_t[:, :, m * 256:(m + 1) * 256], ACT.Copy
                elif m < 6:
                    o, f = rv[:, :, (m - 4) * 256:(m - 3) * 256], ACT.Copy
                elif m < 8:
                    o, f = sg[:, :, (m - 6) * 256:(m - 5) * 256], ACT.Silu
                else:
                    o, f = aqkv[:, :, (m - 8) * 256:(m - 7) * 256], ACT.Copy
                fn(o, b, f).then_inc(bank_free, 1)
                e += 1
                if m in CTX_BLOCKS:
                    b = ps[e % 4][:].rearrange("p (t n) -> p t n", t=TT)
                    o = cakv[:] if m == 10 else ckv[:, :, (m - 2) * 256:(m - 1) * 256]
                    fn(o, b, ACT.Copy).then_inc(bank_free, 1)
                    e += 1
                if y < 10:
                    ahead(0, U("win") + 2 * y)
                if y == 3:
                    for k in range(4):
                        for t in range(TT):
                            o = TABLES["pos"][0] + 2 * k + t
                            last = fn(dec[:, k, t], lg[:, 4 * (k % 2):4 * (k % 2) + 4], ACT.Exp, scale=tb[:, o:o + 1])
                    last.then_inc(m_dec, 1)
                if y == 6:
                    for b in range(2):
                        act.wait_ge(q_turn, b + 1)
                        cp(aqT[:, 2 * b:2 * b + 2].rearrange("p a b -> p (a b)"), ps[4 + b][:]).then_inc(q_tact, 1)
                    act.wait_ge(q_turn, 3)
                    cp(akT[:], ps[6][:]).then_inc(q_tact, 1)
                if y == 9:
                    for d in range(2):
                        act.wait_ge(m_state, d + 1)
                        cp(s_fb[:, d].rearrange("p a b -> p (a b)"), ps[4 + d][:], scale=HK ** -0.5).then_inc(m_sact, 1)
                if 7 <= y < 9:
                    decay(y - 7)
            mix_act()
            projected("wo_c")
            scaled("n2", "n2", lambda k: gs2[:, k:k + 1], lambda k: modc[:, 16 + k, 0:1], xH)
            mod_keep()
            mod_place()
            staging("ff1", func=ACT.Relu, before_last=first_tiles("ff2"))
            down("ff2", FF2_TILES)
            squares("fin", h, after=lambda t: RES["ff2"] - 2 + 2 * t)

        @block.gpsimd
        def _(pool):
            def inverse_root(o, i):
                return nc.gpsimd.tensor_tensor(o, i, mhalf[:, 0:i.shape[1]], ALU.pow)

            nc.gpsimd.memset(mhalf[:], -0.5).then_inc(pool_s, 1)
            pool.wait_ge(pool_s, 1)

            def norm(n):
                pool.wait_ge(ms_done, STAT[n] + 1)
                inverse_root(rstd[:], msq[:]).then_inc(rstd_done, 1)

            norm("a")
            pool.wait_ge(pw_in, 1)
            inverse_root(r32[:, 1], r32[:, 0]).then_inc(pw_out, 1)
            pool.wait_ge(pw_in, 2)
            inverse_root(r32[:, 1, 0:16], r32[:, 0, 0:16]).then_inc(pw_out, 1)
            norm("f0")
            pool.wait_ge(unstaged, STAGED["wo_a"] + 4)
            rb = a["b_rel_bias"]
            pool.dma_start(slab[:], bass.AP(tensor=rb.tensor, offset=P + 1, ap=[[1, P], [513, B_HEADS], [1, SEQ]])).then_inc(slab_in, 16)
            pool.wait_ge(slab_in, 16)
            nc.gpsimd.memset(slab[0:64, :, 0:64], NEG).then_inc(slab_masked, 1)
            norm("kv")
            pool.wait_ge(y_ready, 8)
            pool.dma_start(row_f1[:], a["rows_c"][:, 0:1024].partition_broadcast(P).rearrange("p a n -> p (a n)")).then_inc(late_in, 16)
            pool.dma_start(ctx_in[:], a["ctx_2"].rearrange("o (t p) d -> p (o t) d", p=P)).then_inc(late_in, 16)
            pool.dma_start(tb[:], a["tables"]).then_inc(late_in, 16)
            pool.dma_start(rows_c[:], a["rows_c"][:, 1024:1664].partition_broadcast(P).rearrange("p a n -> p (a n)")).then_inc(late_in, 16)
            pool.dma_start(bmrow[:], a["rows_m"].partition_broadcast(P).rearrange("p a n -> p (a n)")).then_inc(late_in, 16)
            norm("f1")
            norm("ctx")
            norm("x2")
            norm("n1")
            pool.wait_ge(pw_in, 3)
            for t in range(TT):
                last = inverse_root(st_a[:, t, 1], st_a[:, t, 0])
            last.then_inc(pw_out, 1)
            pool.wait_ge(pw_in, 4)
            inverse_root(st_r[:, 3], st_r[:, 2]).then_inc(pw_out, 1)
            norm("n2")
            pool.wait_ge(unstaged, STAGED["wo_c"] + 4)
            pool.dma_start(rows_f[:], a["rows_c"][:, 1664:2688].partition_broadcast(P).rearrange("p a n -> p (a n)")).then_inc(final_in, 16)
            norm("fin")

        @block.vector
        def _(dve):
            st = Steps(dve, dve_s)
            tt = nc.vector.tensor_tensor
            ts = nc.vector.tensor_scalar
            stt = nc.vector.scalar_tensor_tensor

            def bc(x, n):
                return x.unsqueeze(2).broadcast_to([x.shape[0], x.shape[1], n])

            def rep(x, n):
                return x.unsqueeze(1).broadcast_to([x.shape[0], n, x.shape[1]])

            def four(x):
                return x.rearrange("p (a b) -> p a b", a=4)

            def rest(o, x, hi):
                return tt(o, x, hi.bitcast(F32), ALU.subtract)

            def lo(i, per, c):
                if isinstance(i, int) and c >= UNITS:
                    return
                dve.wait_ge(hi_done, i * per + (c + 1))
                rest(wL[:, c % SPLIT], raw[:, c % RAW], wH[:, c % SPLIT]).then_inc(lo_done, 1)

            def ahead(i, c):
                lo(i, 8, c + SPLIT)
                lo(i, 8, c + SPLIT + 1)

            def blocks(name, before=None, each=0, before_last=None):
                def body(i, j):
                    if before:
                        before(i, j)
                    ahead(i, U(name) + 2 * j)
                turns(dve, BLOCKS[name][1], body, st, each, before_last=before_last)

            def free(name, i, j):
                dve.wait_ge(bank_free, i * 4 + (BANK[name] + j + 1))

            def normed(n, src, o=None):
                dve.wait_ge(sq_done, 2 * STAT[n] + 2)
                if n in ("f0", "f1", "n2"):
                    st.do(tt(ssq[:], ssq[:], ssq_part[:], ALU.add))
                ts(msq[:], ssq[:], 1.0 / D, EPS, ALU.mult, ALU.add).then_inc(ms_done, 1)
                dve.wait_ge(rstd_done, STAT[n] + 1)
                for t in range(TT):
                    if o is None:
                        ts(xn[:, t], src[:, t], rstd[:, t:t + 1], None, ALU.mult).then_inc(xn_done, 1)
                    else:
                        o(t)

            def scaled(n, turn, gain, bias, oH, oL, xv=xv):
                e = SCALED[n]
                if n in GAINED:
                    for b in range(4):
                        dve.wait_ge(x_bank, 4 * GAINED[n] + b + 1)
                        for k in (2 * b, 2 * b + 1):
                            last = stt(oL[:, k], ps[AUX + b][:, (k % 2) * SEQ:(k % 2 + 1) * SEQ], gain(k),
                                       oH[:, k].bitcast(F32), ALU.mult, ALU.subtract)
                        if b % 2:
                            last.then_inc(x_ready, 1)
                    return
                dve.wait_ge(turned, 4 * TURN[turn] + 4)
                if e:
                    dve.wait_ge(x_ready, 2 * e)
                e = SHIFTED[n]
                for k in range(4, 8):
                    src = ps[AUX + k // 2][:, (k % 2) * SEQ:(k % 2 + 1) * SEQ]
                    if bias:
                        v = ts(xv[:, k], src, gain(k), bias(k), ALU.mult, ALU.add)
                    else:
                        v = ts(xv[:, k], src, gain(k), None, ALU.mult)
                    v.then_inc(val_dve, 1)
                for f in range(2):
                    dve.wait_ge(x_hi, 2 * e + f + 1)
                    rest(oL[:, 4 * f:4 * f + 4], xv[:, 4 * f:4 * f + 4], oH[:, 4 * f:4 * f + 4]).then_inc(x_ready, 1)

            def first_tiles(name):
                def parts():
                    for m in range(SPLIT):
                        dve.wait_ge(a_hi, ACTS[name] + m + 1)
                        rest(aL[:, m], act_a[:, m], aH[:, m]).then_inc(a_lo, 1)
                return parts

            def down(name, count, gate=None):
                def body(i, j):
                    lo(i, 4, U(name) + j + SPLIT)
                    m = j + SPLIT
                    dve.wait_ge(a_hi, i * 4 + (ACTS[name] + m + 1))
                    rest(aL[:, m % SPLIT], act_a[:, one(i * 4 + m)].rearrange("p a n -> p (a n)"),
                         aH[:, m % SPLIT]).then_inc(a_lo, 1)
                turns(dve, count - SPLIT, body)
                for j in range(count - SPLIT, count):
                    lo(0, 4, U(name) + j + SPLIT)
                dve.wait_ge(unit_done, U(name) + count)
                for t in range(TT):
                    for c in range(2):
                        hc = h[:, t, c * 512:(c + 1) * 512]
                        b = ps[AUX + 2 * t + c][:]
                        if gate is not None:
                            tmp = stage[:, c].rearrange("p a b -> p (a b)")
                            st.do(tt(tmp, b, gate[:, c * 512:(c + 1) * 512], ALU.mult))
                            b = tmp
                        tt(hc, hc, b, ALU.add).then_inc(res_done, 1)

            def residual(name, gate=None):
                def body(i, j):
                    free(name, i, j)
                    n = STAGED[name] + j
                    s = stage[:, n % 2]
                    hc = h[:, :, bass.ds((i * 4 + j) * 256, 256)]
                    if gate is not None:
                        st.do(tt(s, s, rep(gate[:, bass.ds((i * 4 + j) * 256, 256)], TT), ALU.mult))
                    tt(hc, hc, s, ALU.add).then_inc(unstaged, 1)
                blocks(name, body, 1 if gate is not None else 0)

            def gates():
                ba = sm[:, 12:14, 0:16]
                v = lambda k: sm[:, k, 0:16].rearrange("p (t n) -> p t n", t=TT)
                nc.vector.tensor_copy(ba, ps[AUX + 1][:, 0:32].rearrange("p (t n) -> p t n", t=TT)).then_inc(g_dve, 1)
                dve.wait_ge(g_dve, 1)
                st.do(tt(v(1), ba[:, :, 8:16], rep(rows_a[:, 136:144], TT), ALU.add))
                st.do(ts(sm[:, 3, 0:16], sm[:, 1, 0:16], -1.0, None, ALU.mult))
                tt(sm[:, 3, 0:16], sm[:, 3, 0:16], sm[:, 1, 0:16], ALU.min).then_inc(g_dve, 1)
                dve.wait_ge(g_act, 1)
                st.do(ts(sm[:, 2, 0:16], sm[:, 2, 0:16], 1.0, None, ALU.add))
                st.do(nc.vector.reciprocal(sm[:, 0, 0:16], sm[:, 2, 0:16]))
                st.do(ts(sm[:, 4, 16:24], sm[:, 15, 0:8], -1.0, None, ALU.mult))
                dve.wait_ge(g_act, 2)
                ts(sm[:, 5], sm[:, 4], 1.0, None, ALU.add).then_inc(g_dve, 1)
                dve.wait_ge(g_dve, 3)
                st.do(ts(sm[:, 7], sm[:, 5], 1.0, None, ALU.is_equal))
                st.do(stt(sm[:, 9], sm[:, 5], -1.0, sm[:, 7], ALU.add, ALU.add))
                st.do(nc.vector.reciprocal(sm[:, 9], sm[:, 9]))
                dve.wait_ge(g_act, 3)
                st.do(tt(sm[:, 8], sm[:, 6], sm[:, 7], ALU.add))
                st.do(tt(sm[:, 8], sm[:, 8], sm[:, 4], ALU.mult))
                st.do(tt(sm[:, 8], sm[:, 8], sm[:, 9], ALU.mult))
                st.put(nc.vector.tensor_copy(lg[:], sm[:, 8, 16:24]))
                st.do(stt(sm[:, 1, 0:16], sm[:, 1, 0:16], 0.0, sm[:, 8, 0:16], ALU.max, ALU.add))
                stt(v(10), v(1), -1.0, rep(sm[:, 14, 0:8], TT), ALU.mult, ALU.mult).then_inc(g_dve, 1)

            gc, beta, g_, eg, ke = (sm[:, k, 0:16] for k in (16, 0, 10, 17, 19))

            def delta_front():
                def spread(g):
                    if g >= 2:
                        dve.wait_ge(row_pe, g - 1)
                    tt(dG[g % 2], rep(K_["tri"], 4), bc(g_[:, 4 * g:4 * g + 4], P), ALU.mult).then_inc(dg_dve, 1)

                def exponents(g):
                    q4 = slice(4 * g, 4 * g + 4)
                    dve.wait_ge(row_pe, g + 1)
                    st.do(tt(AT[:, q4], four(ps[AUX + g % 2][:]), bc(gc[:, q4], P), ALU.subtract))
                    st.do(tt(U_[:, q4], rep(K_["low"], 4), AT[:, q4], ALU.subtract))
                    tt(AT[:, q4], AT[:, q4], rep(K_["upT"], 4), ALU.add).then_inc(arg_dve, 1)

                def qk_tok(q):
                    f0, t = TOK_HEAD[q]
                    dve.wait_ge(tok_pe, q + 1)
                    tt(tok[:, t, f0:f0 + 4], four(ps[TOK_BANK[q][0]][:]), bc(r32[:, 1, 16 * t + f0:16 * t + f0 + 4], HK),
                       ALU.mult).then_inc(tok_dve, 1)
                dve.wait_ge(g_sum, 1)
                st.do(nc.vector.tensor_copy(sm[:, 16, 0:16], ps[7][:, 0:16]))
                tt(sm[:, 18, 0:8], ps[7][:, 16:24], sm[:, 16, 0:8], ALU.subtract).then_inc(g_dve, 1)
                spread(0)
                spread(1)
                ahead(0, U("z"))
                dve.wait_ge(tok_ss, 1)
                ts(r32[:, 0], ps[7][:, 32:64], EPS, None, ALU.add).then_inc(pw_in, 1)
                exponents(0)
                spread(2)
                exponents(1)
                spread(3)
                exponents(2)
                exponents(3)
                ahead(0, U("z") + 2)
                dve.wait_ge(pw_out, 1)
                r = r32[:, 1].rearrange("p (t n) -> p t n", t=TT)
                st.do(ts(r[:, :, 0:8], r[:, :, 0:8], HK ** -0.5, None, ALU.mult))
                for q in range(4, 8):
                    qk_tok(q)
                ahead(0, U("z") + 4)
                for q in range(8, 12):
                    qk_tok(q)
                ahead(0, U("z") + 6)
                for q in range(1, 8, 2):
                    dve.wait_ge(back_pe, q + 1)
                    nc.vector.tensor_copy(feat[:, BACK_HEAD[q]:BACK_HEAD[q] + 2].rearrange("p a b -> p (a b)"),
                                          ps[AUX + q % 4][:]).then_inc(back_dve, 1)

            def delta():
                join = K_["join"].rearrange("p (l n) -> p l n", l=7)
                dve.wait_ge(exp_act, 4)
                st.do(tt(U_[:], U_[:], bc(beta, P), ALU.mult))

                def set_up(g):
                    q4 = slice(4 * g, 4 * g + 4)
                    dve.wait_ge(mt_act, g + 1)
                    st.put(tt(T_[:, q4], T_[:, q4], rep(join[:, 0], 4), ALU.mult))
                    st.do(tt(U_[:, q4], MT[:, q4], rep(K_["join1T"], 4), ALU.mult))
                    st.put(tt(T_[:, q4], T_[:, q4], rep(ident, 4), ALU.add))
                    tt(U_[:, q4], U_[:, q4], rep(ident, 4), ALU.add).then_inc(dbl_dve, 1)
                for g in range(4):
                    q4 = slice(4 * g, 4 * g + 4)
                    dve.wait_ge(kq_pe, g + 1)
                    tt(T_[:, q4], four(ps[4 + g % 2][:]), U_[:, q4], ALU.mult).then_inc(m_dve, 1)
                    tt(AT[:, q4], four(ps[6 + g % 2][:]), AT[:, q4], ALU.mult).then_inc(at_dve, 1)
                    if g:
                        set_up(g - 1)
                set_up(3)
                st.wait(st.n)
                for l in range(LEVELS):
                    for step in range(3):
                        for g in range(4):
                            q4 = slice(4 * g, 4 * g + 4)
                            if l == LEVELS - 1 and step == 1:
                                continue
                            n = l * 12 + step * 4 + g + 1
                            if l == LEVELS - 1 and step == 2:
                                n -= 4
                            dve.wait_ge(dbl_pe, n)
                            b = four(ps[AUX + g][:])
                            if step == 0:
                                tt(P_[:, q4], b, rep(join[:, l + 1], 4), ALU.mult).then_inc(dbl_dve, 1)
                            else:
                                s = 1 << (l + 1)
                                o = (T_, U_)[step - 1][:, q4].rearrange("p x (n h s) -> p x n h s", h=2, s=s)[:, :, :, step - 1]
                                b = b[:, :, 0:64].rearrange("p x (n s) -> p x n s", s=s)
                                tt(o, o, b, ALU.add).then_inc(dbl_dve, 1)
                tt(tok[:, 0, 16:24], tok[:, 0, 16:24], bc(beta[:, 0:8], HK), ALU.mult).then_inc(scan_dve, 1)
                dve.wait_ge(g_act, 4)
                tt(tok[:, 0, 8:16], tok[:, 0, 8:16], bc(ke[:, 0:8], HK), ALU.mult).then_inc(scan_dve, 1)
                for hb in range(2):
                    dve.wait_ge(scan_pe, 5 + hb)
                    tt(MT[:, 8 + 4 * hb:12 + 4 * hb], four(ps[4 + hb][:]), bc(eg[:, 8 + 4 * hb:12 + 4 * hb], P),
                       ALU.mult).then_inc(scan_dve, 1)
                dve.wait_ge(scan_dve, 4)
                st.do(tt(MT[:, 8:16], tok[:, 1, 16:24], MT[:, 8:16], ALU.subtract))
                tt(T_[:, 8:16], MT[:, 8:16], bc(beta[:, 8:16], P), ALU.mult).then_inc(scan_dve, 1)
                for hb in range(2):
                    dve.wait_ge(scan_pe, 7 + hb)
                    tt(MT[:, 4 * hb:4 + 4 * hb], four(ps[6 + hb][:]), bc(eg[:, 8 + 4 * hb:12 + 4 * hb], P),
                       ALU.mult).then_inc(scan_dve, 1)
                dve.wait_ge(scan_dve, 7)
                for hb in range(2):
                    dve.wait_ge(scan_pe, 13 + hb)
                    tt(tok[:, 1, 4 * hb:4 * hb + 4], four(ps[4 + hb][:]), MT[:, 4 * hb:4 * hb + 4],
                       ALU.add).then_inc(scan_dve, 1)
                dve.wait_ge(scan_dve, 9)
                dve.wait_ge(scan_act, 6)
                for t in range(TT):
                    st.put(tt(MT[:, 8 * t:8 * t + 8], tok[:, t, 0:8], tok[:, t, 0:8], ALU.mult))
                st.wait(st.n)
                st.do(nc.vector.tensor_reduce(r32[:, 0, 0:16], MT[:], AX, ALU.add))
                ts(r32[:, 0, 0:16], r32[:, 0, 0:16], 1.0 / HK, EPS, ALU.mult, ALU.add).then_inc(pw_in, 1)
                dve.wait_ge(pw_out, 2)
                dve.wait_ge(bank_free, BANK["z"] + 4)
                for t in range(TT):
                    o = tok[:, t, 0:8]
                    st.do(tt(o, o, bc(r32[:, 1, 8 * t:8 * t + 8], HK), ALU.mult))
                    st.do(tt(o, o, rep(rows_a[:, 0:128], 8), ALU.mult))
                    last = tt(o, o, zs[:, t].rearrange("p (a b) -> p a b", a=8), ALU.mult)
                last.then_inc(y_rows, 1)
                for b in range(4):
                    dve.wait_ge(y_hi, b + 1)
                    rest(xL[:, 2 * b:2 * b + 2].rearrange("p a b -> p (a b)"), ps[AUX + b][:],
                         xH[:, 2 * b:2 * b + 2].rearrange("p a b -> p (a b)")).then_inc(y_ready, 1)

            def band():
                def maxima(g):
                    b = g % 2
                    dve.wait_ge(b_score, g + 1)
                    if g == 0:
                        dve.wait_ge(slab_masked, 1)
                    for x in range(4):
                        n, o = 4 * g + x, x // 2
                        for t in range(TT):
                            c = slice(0, 256) if t else slice(256, 384)
                            w = ps[4 + x % 2][:, o * 256:(o + 1) * 256] if t else ps[6 + x % 2][:, o * P:(o + 1) * P]
                            s = slab[:, n, ::-1] if t else slab[:, n, P - 1::-1]
                            st.put(nc.vector.tensor_tensor_reduce(p_b[:, b, x, c], w, s, 1.0, -3e38, ALU.add, ALU.max,
                                                                  st_b[:, b, 0, 2 * x + t:2 * x + t + 1]))
                    st.wait(st.n)
                    ts(st_b[:, b, 1], st_b[:, b, 0], -1.0, None, ALU.mult).then_inc(b_max, 1)
                def probabilities(g):
                    b = g % 2
                    dve.wait_ge(b_exp, 8 * g + 8)
                    st.do(nc.vector.reciprocal(st_b[:, b, 0], st_b[:, b, 2]))
                    r = st_b[:, b, 0].rearrange("p (x t) -> p x t", t=TT)
                    tt(p_b[:, b, :, 0:256], p_b[:, b, :, 0:256], bc(r[:, :, 1], 256), ALU.mult)
                    tt(p_b[:, b, :, 256:384], p_b[:, b, :, 256:384], bc(r[:, :, 0], P), ALU.mult).then_inc(b_prob, 1)
                maxima(0)
                maxima(1)
                probabilities(0)
                for g in range(4):
                    dve.wait_ge(b_turn, 3 * g + 2)
                    nc.vector.tensor_copy(pT_b[:, g % 2, 2:4, 0:256], ps[1][:].rearrange("p (x n) -> p x n", x=2)).then_inc(b_tdve, 1)
                    if g < 3:
                        probabilities(g + 1)
                    if g < 2:
                        dve.wait_ge(b_turn, 3 * g + 3)
                        maxima(g + 2)
                    dve.wait_ge(y_hi, 4 + g + 1)
                    rest(xL[:, 2 * g:2 * g + 2].rearrange("p a b -> p (a b)"), ps[3][:],
                         xH[:, 2 * g:2 * g + 2].rearrange("p a b -> p (a b)")).then_inc(y_ready, 1)

            def table(name, t=None):
                o, n = TABLES[name]
                return tb[:, o:o + n] if t is None else tb[:, o + t * n // 2:o + (t + 1) * n // 2]

            def context_keys():
                dve.wait_ge(m_dec, 1)
                for d in range(2):
                    for t in range(TT):
                        tt(rope[:, t, d * 512:(d + 1) * 512].rearrange("p (a b) -> p a b", a=4),
                           ckv[:, t, 0:512].rearrange("p (a b) -> p a b", a=4), bc(dec[:, 2 + d, t], P),
                           ALU.mult).then_inc(m_ck, 1)

            def rotate(t):
                x = qk_t[:, t].rearrange("p (n c) -> p n c", n=8)
                x1, x2 = x[:, :, 0:64], x[:, :, 64:]
                cos, sin = rep(table("rcos", t), 8), rep(table("rsin", t), 8)
                u, w = (wt[:, y].rearrange("p (n c) -> p n c", n=8) for y in range(2))
                st.put(tt(u, x2, sin, ALU.mult))
                st.do(tt(w, x1, sin, ALU.mult))
                st.put(tt(x1, x1, cos, ALU.mult))
                st.do(tt(x2, x2, cos, ALU.mult))
                st.put(tt(x1, x1, u, ALU.subtract))
                tt(x2, x2, w, ALU.add).then_inc(m_rope, 1)
                dve.wait_ge(m_rope, t + 1)

            def att_squares():
                for t in range(TT):
                    x = aqkv[:, t, 0:640].rearrange("p (n c) -> p n c", c=ATT_D)
                    xc = cakv[:, t, 0:128].rearrange("p (n c) -> p n c", c=ATT_D)
                    st.put(tt(asq[:, 0:10], x, x, ALU.mult))
                    st.do(tt(asq[:, 10:12], xc, xc, ALU.mult))
                    st.do(nc.vector.tensor_reduce(st_a[:, t, 0], asq[:], AX, ALU.add))
                    last = ts(st_a[:, t, 0], st_a[:, t, 0], 1.0 / ATT_D, EPS, ALU.mult, ALU.add)
                    st.put(last) if t == 0 else last.then_inc(pw_in, 1)

            def att_rotate(t):
                dve.wait_ge(pw_out, 3)
                qn, kn = rows_c[:, 512:576], rows_c[:, 576:640]
                x = aqkv[:, t, 0:640].rearrange("p (n c) -> p n c", c=ATT_D)
                xc = cakv[:, t, 0:128].rearrange("p (n c) -> p n c", c=ATT_D)
                st.put(tt(x, x, bc(st_a[:, t, 1, 0:10], ATT_D), ALU.mult))
                st.do(tt(kcn[:, t], xc, bc(st_a[:, t, 1, 10:12], ATT_D), ALU.mult))
                st.put(tt(x[:, 0:8], x[:, 0:8], rep(qn, 8), ALU.mult))
                st.put(tt(x[:, 8:10], x[:, 8:10], rep(kn, 2), ALU.mult))
                st.do(tt(kcn[:, t], kcn[:, t], rep(kn, 2), ALU.mult))
                cos, sin = rep(table("acos", t), 10), rep(table("asin", t), 10)
                st.put(tt(rt[:, 0], x[:, :, 0:32], cos, ALU.mult))
                st.put(tt(rt[:, 1], x[:, :, 32:], sin, ALU.mult))
                st.put(tt(rt[:, 2], x[:, :, 0:32], sin, ALU.mult))
                st.do(tt(rt[:, 3], x[:, :, 32:], cos, ALU.mult))
                for c, y, op in ((0, 0, ALU.subtract), (32, 2, ALU.add)):
                    for s in range(2):
                        st.put(tt(aqn[:, t, s:8:2, c:c + 32], rt[:, y, 4 * s:4 * s + 4], rt[:, y + 1, 4 * s:4 * s + 4], op))
                    last = tt(aqn[:, t, 8:10, c:c + 32], rt[:, y, 8:10], rt[:, y + 1, 8:10], op)
                    st.put(last) if c == 0 else last.then_inc(q_rope, 1)
                dve.wait_ge(q_rope, t + 1)

            def decay(x):
                dve.wait_ge(m_w, x + 1)
                st.put(tt(wt[:, 0], wt[:, 0], table("ge"), ALU.mult))
                st.do(tt(wt[:, 1], wt[:, 1], table("le"), ALU.mult))
                tt(sT[DECAYS[x]], wt[:, 0], wt[:, 1], ALU.add).then_inc(m_wd, 1)

            def mix():
                dve.wait_ge(bank_free, BANK["wo_c"])
                for b in (1, 3):
                    dve.wait_ge(m_turn, b + 1)
                    o = rkT if b == 3 else rqT
                    nc.vector.tensor_copy(o[:, 2:4].rearrange("p a b -> p (a b)"), ps[AUX + b][:]).then_inc(m_tdve, 1)

                def outputs(x):
                    n = DECAYS[x]
                    dve.wait_ge(m_o, x + 1)
                    b = 0 if x % 2 else 6
                    st.do(nc.vector.tensor_copy(o_r[:, :, n], ps[b][:, 0:256].rearrange("p (t c) -> p t c", t=TT)))
                    for t in range(TT):
                        st.put(stt(o_r[:, t, n], ps[b][:, 256 + t * P:256 + (t + 1) * P], dec[:, 0, t, n:n + 1],
                                   o_r[:, t, n], ALU.mult, ALU.add))
                    st.wait(st.n)
                    for t in range(TT):
                        last = stt(o_r[:, t, n], ps[b + 1][:, t * P:(t + 1) * P], dec[:, 1, t, n:n + 1],
                                   o_r[:, t, n], ALU.mult, ALU.add)
                    last.then_inc(m_od, 1)
                for x, n in enumerate(DECAYS):
                    if x >= 2:
                        decay(x)
                    dve.wait_ge(m_wd, x + 1)
                    dve.wait_ge(m_s, x + 1)
                    stt(sT[n], ps[4 + x % 2][:], HK ** -0.5, sT[n], ALU.mult, ALU.mult).then_inc(m_sd, 1)
                    if x:
                        outputs(x - 1)
                    if x == 1:
                        ahead(0, U("win") + 20)
                outputs(RET_H - 1)

                def maxima(j):
                    for n in range(4):
                        dve.wait_ge(s_pe, 4 * j + n + 1)
                        st.do(nc.vector.tensor_reduce(st_p[:, 0, n:n + 1], ps[4 + n][:], AX, ALU.max))
                        ts(st_p[:, 1, n:n + 1], st_p[:, 0, n:n + 1], -ATT_D ** -0.5, None, ALU.mult).then_inc(s_max, 1)

                def probabilities(j):
                    for n in range(4):
                        dve.wait_ge(s_exp, 4 * j + n + 1)
                        st.do(nc.vector.reciprocal(st_p[:, 0, n:n + 1], st_p[:, 2, n:n + 1]))
                        w = ap_[:, n // 2, n % 2]
                        ts(w, w, st_p[:, 0, n:n + 1], None, ALU.mult).then_inc(s_prob, 1)
                def group_norm(part):
                    dve.wait_ge(gn_act, part + 1)
                    if part == 0:
                        ts(st_r[:, 0], st_r[:, 0], -1.0 / HK, None, ALU.mult).then_inc(gn_dve, 1)
                    elif part == 1:
                        ts(st_r[:, 2], st_r[:, 1], 1.0 / HK, EPS, ALU.mult, ALU.add).then_inc(pw_in, 1)
                        dve.wait_ge(pw_out, 4)
                        tt(st_r[:, 2], st_r[:, 0], st_r[:, 3], ALU.mult).then_inc(gn_dve, 1)
                    else:
                        o2 = o_r[:].rearrange("p t n c -> p t (n c)")
                        st.do(tt(o2, o2, rep(rows_c[:, 0:512], TT), ALU.mult))
                        tt(o2, o2, sg[:], ALU.mult).then_inc(y_rows, 1)
                maxima(0)
                group_norm(0)
                probabilities(0)
                for j in range(4):
                    for x in (0, 2):
                        n = ATT_BANKS[x]
                        dve.wait_ge(s_turn, 4 * j + x + 1)
                        nc.vector.tensor_copy(apT[:, n // 2, 2 * (n % 2):2 * (n % 2) + 2].rearrange("p a b -> p (a b)"),
                                              ps[n][:]).then_inc(s_tdve, 1)
                    if j < 3:
                        maxima(j + 1)
                        probabilities(j + 1)
                        if j == 0:
                            group_norm(1)
                    else:
                        for b in range(2):
                            dve.wait_ge(y_hi, 11 + b + 1)
                            rest(xL[:, 2 * b:2 * b + 2].rearrange("p a b -> p (a b)"), ps[4 + b][:],
                                 xH[:, 2 * b:2 * b + 2].rearrange("p a b -> p (a b)")).then_inc(y_ready, 1)
                    dve.wait_ge(y_hi, (9, 10, 11, 14)[j])
                    r = 64 * (j % 2)
                    rest(xL[r:r + 64, 4 + j // 2:8:2], ps[0][r:r + 64].rearrange("p (a b) -> p a b", a=2),
                         xH[r:r + 64, 4 + j // 2:8:2]).then_inc(y_ready, 1)
                    if j == 1:
                        group_norm(2)

            dve.wait_ge(x_in, 16)
            normed("a", h)
            dve.wait_ge(act_s, 1)
            rest(baL[:], baw[:], baH[:]).then_inc(c_ready, 1)
            lo(0, 0, 0)
            scaled("a", "a", lambda k: col("a_norm", k), None, xH, xL)
            lo(0, 0, 1)
            lo(0, 0, 2)
            lo(0, 0, 3)
            dve.wait_ge(ba_done, 1)
            nc.vector.tensor_copy(stage[0:16, 0, 0], ps[AUX][0:16, 0:SEQ]).then_inc(ba_rows, 1)
            dve.wait_ge(ba_done, 2)
            gates()

            def modulation():
                dve.wait_ge(mod_act, 4)
                st.do(tt(modc[:, 0:16], modc[:, 0:16], bc(col("b_mod", 0, 16), 2), ALU.add))
                st.do(stt(gs1[:], modc[:, 8:16], 1.0, bc(col("norm1", 0, 8), 2), ALU.add, ALU.mult))

            def modulation2():
                dve.wait_ge(mod_act, sum(MOD_AT["win"]))
                st.do(tt(modc[:, 16:32], modc[:, 16:32], bc(col("b_mod", 24, 16), 2), ALU.add))
                st.put(stt(gs2[:], modc[:, 24:32, 0], 1.0, col("norm2", 0, 8), ALU.add, ALU.mult))
                st.put(tt(gate1[:], gate1[:], bmrow[:, 0:D], ALU.add))
                st.do(tt(gate2[:, 0:512], gate2[:, 0:512], bmrow[:, D:D + 512], ALU.add))

            def conv(name, taps, tiles, bias, nextto):
                wname = {"qkv": "a_conv", "up0": "f_conv0", "up1": "f_conv1"}[name]

                def body(i, j):
                    free(name, i, j)
                    n = STAGED[name] + j
                    if name == "qkv" and not (isinstance(i, int) and j < 2):
                        dve.wait_ge(silu_done, i * 4 + (j - 1))
                    m = i * 4 + j
                    marks = [0, 0]
                    for d in range(taps):
                        for f in range(2):
                            o, x = cv[:, n % 2, f], stage[:, n % 2, f]
                            w = cols[:, one(COLS[wname][0] + (taps - 1 - d) * tiles + nextto(m, f))]
                            if d == 0:
                                if bias:
                                    c = ts(o, x, w, cols[:, one(COLS[bias][0] + nextto(m, f))], ALU.mult, ALU.add)
                                else:
                                    c = ts(o, x, w, None, ALU.mult)
                                marks[f] = st.put(c)
                                continue
                            st.wait(marks[f])
                            c = stt(o[:, d:], x[:, 0:SEQ - d], w, o[:, d:], ALU.mult, ALU.add)
                            if d == taps - 1 and f == 1:
                                c.then_inc(unstaged, 1)
                            else:
                                marks[f] = st.put(c)
                return body, 2 * taps - 1

            body, each = conv("qkv", A_TAPS, QKV_TILES, None, lambda m, f: m * 2 + f)
            blocks("qkv", body, each)
            delta_front()
            delta()
            residual("wo_a")

            def ffn(l, before):
                dve.wait_ge(unstaged, before)
                normed(f"f{l}", h)
                if l == 1:
                    dve.wait_ge(xn_done, 2 * TURN["f1"] + 2)
                    modulation()
                    normed("ctx", ctx_in, lambda t: ts(ctx_in[:, t], ctx_in[:, t], rstd[:, t:t + 1], None,
                                                       ALU.mult).then_inc(xn_done, 1))
                scaled(f"f{l}", f"f{l}", lambda k: col(f"f_norm{l}", k), None, xH, xL)
                up = f"up{l}"
                conv_, steps = conv(up, F_TAPS, 2 * F_TILES, f"f_bias{l}", lambda m, f: m + f * F_TILES)
                si = 12 + 22 * l

                def body(i, j):
                    conv_(i, j)
                    ahead(i, U(up) + 2 * j)
                    n = STAGED[up] + j
                    dve.wait_ge(silu_done, i * 4 + (si + j + 1))
                    tt(act_a[:, one(i * 4 + j)].rearrange("p a n -> p (a n)"), cv[:, n % 2, 0], cv[:, n % 2, 1],
                       ALU.mult).then_inc(prod_done, 1)
                turns(dve, BLOCKS[up][1], body, st, steps, before_last=first_tiles(f"down{l}"), between=None if l == 0 else lambda: scaled(
                    "ctx", "ctx", lambda k: gs1[:, k, 1:2], lambda k: modc[:, k, 1:2], xcH, xcL, xvc))
                down(f"down{l}", F_TILES)
            ffn(0, STAGED["wo_a"] + 4)
            dve.wait_ge(res_done, RES["down0"])
            normed("kv", h)
            scaled("kv", "kv", lambda k: col("kv_norm", k), None, xH, xL)
            scaled("q", "kv", lambda k: col("b_norm", k), None, x2H, x2L)
            blocks("k")
            blocks("v")
            blocks("q")
            band()
            residual("wo_b")
            ffn(1, STAGED["wo_b"] + 4)
            dve.wait_ge(res_done, RES["down1"])

            def final(row):
                def o(t):
                    stt(h[:, t], h[:, t], rstd[:, t:t + 1], row[:], ALU.mult, ALU.mult).then_inc(res_done, 1)
                return o
            normed("x2", h, final(row_f1))
            dve.wait_ge(res_done, RES["x2"])
            normed("n1", h)
            scaled("n1", "n1", lambda k: gs1[:, k, 0:1], lambda k: modc[:, k, 0:1], xH, xL)
            for y in range(len(WIN_ORDER)):
                if y < 10:
                    ahead(0, U("win") + 2 * y)
                if y == 2:
                    dve.wait_ge(bank_free, BANK["win"] + 4)
                    att_squares()
                if y in (3, 4):
                    att_rotate(y - 3)
                if y in (6, 7):
                    dve.wait_ge(bank_free, BANK["win"] + 10)
                    rotate(y - 6)
                if y == 8:
                    context_keys()
                    decay(0)
                if y == 9:
                    decay(1)
            mix()
            modulation2()
            residual("wo_c", gate1)
            dve.wait_ge(unstaged, STAGED["wo_c"] + 4)
            normed("n2", h)
            scaled("n2", "n2", lambda k: gs2[:, k:k + 1], lambda k: modc[:, 16 + k, 0:1], xH, xL)

            def square(i, j):
                free("ff1", i, j)
                s = stage[:, (STAGED["ff1"] + j) % 2]
                tt(act_a[:, bass.ds((i * 4 + j) * 2, 2)], s, s, ALU.mult).then_inc(unstaged, 1)
            dve.wait_ge(mod_act, len(MOD_CHUNK))
            st.do(tt(gate2[:, 512:], gate2[:, 512:], bmrow[:, D + 512:], ALU.add))
            blocks("ff1", square, before_last=first_tiles("ff2"))
            down("ff2", FF2_TILES, gate2)
            dve.wait_ge(res_done, RES["ff2"])
            dve.wait_ge(final_in, 16)
            normed("fin", h, final(rows_f))


def columns(x):
    x = np.asarray(x)
    return x.reshape(-1, P).T


def constants():
    i, j = np.arange(P)[:, None], np.arange(P)[None, :]
    joins = []
    for l in range(7):
        s = 1 << l
        joins.append(-((i // (2 * s) == j // (2 * s)) & (i % (2 * s) >= s) & (j % (2 * s) < s)).astype(np.float32))
    parts = [np.eye(P), np.ones((P, P)), i <= j, np.where(j < i, 0.0, NEG), np.where(j >= i, 0.0, NEG), *joins, joins[0].T]
    return np.concatenate([np.asarray(x, np.float32) for x in parts], axis=1)


def tables():
    p, i = np.arange(P)[:, None], np.arange(SEQ)[None, :]
    rel = np.concatenate([i - (p + P * t) for t in range(TT)], axis=1).astype(np.float32)
    pos = np.concatenate([p, p + P], axis=1).astype(np.float32)
    t = np.arange(SEQ, dtype=np.float32)

    def freqs(n):
        return (np.float32(10000.0) ** (-np.arange(n, dtype=np.float32) / np.float32(n))).astype(np.float32)

    def rows(x):
        return np.concatenate([x[k * P:(k + 1) * P] for k in range(TT)], axis=1)
    ra = (t[:, None] * freqs(64)).astype(np.float64)
    aa = np.concatenate([np.floor(t / 64)[:, None] * freqs(16), (t % 64)[:, None] * freqs(16)], axis=1).astype(np.float64)
    parts = [np.maximum(rel, 0), np.maximum(-rel, 0), rel >= 0, rel <= 0, pos + 1, SEQ - pos, CTX - 1 - pos, pos,
             rows(np.cos(ra)), rows(np.sin(ra)), rows(np.cos(aa)), rows(np.sin(aa))]
    return np.concatenate([np.asarray(x, np.float32) for x in parts], axis=1)


BIG = ("x", "b_rel_bias", "a_w_in", "a_w_out", "w_kv", "b_w_q", "b_w_out", "f_w_up", "f_w_down", "ctx_2", "w_mod_2", "w_in_2",
       "w_out_2", "w_ff1_2", "w_ff2_2")


def lay_out(v):
    g = {n: np.ascontiguousarray(v[n]) for n in BIG}
    order = [v["a_norm"], v["kv_norm"], v["b_norm"], v["f_norm"][0], v["f_norm"][1], v["norm1_g_2"], v["norm2_g_2"],
             v["a_conv"], v["f_conv"][0], v["f_conv"][1], v["f_conv_b"][0], v["f_conv_b"][1], v["b_mod_2"],
             v["c_2"], v["c_ctx_2"]]
    g["cols"] = np.ascontiguousarray(np.concatenate([columns(x) for x in order], axis=1))
    flat = lambda xs: np.ascontiguousarray(np.concatenate([np.asarray(x).reshape(1, -1) for x in xs], axis=1))
    g["rows_a"] = flat([v["a_out_norm"], v["a_A_log"], v["a_dt_bias"], v["ret_log_rate_2"]])
    bm = np.asarray(v["b_mod_2"]).reshape(6, D)
    g["rows_m"] = flat([bm[2], bm[5]])
    g["rows_c"] = flat([v["final_norm"], v["ret_gn_g_2"], v["q_norm_g_2"], v["k_norm_g_2"], v["final_norm_g_2"]])
    g["consts"] = constants()
    g["tables"] = tables()
    return g


def program(nc, arrays):
    aps = {n: nc.dram_tensor(f"in_{n}", x.shape, mybir.dt.from_np(x.dtype), kind="ExternalInput").ap()
           for n, x in arrays.items()}
    out = nc.dram_tensor("out", (1, SEQ, D), F32, kind="ExternalOutput").ap()
    build(nc, aps, out)


def kernel(**inputs):
    import concourse.bacc as bacc
    from concourse.bass_utils import run_bass_kernel_spmd

    arrays = lay_out(inputs)
    nc = bacc.Bacc("TRN2", target_bir_lowering=False, num_devices=1)
    program(nc, arrays)
    r = run_bass_kernel_spmd(nc, [{f"in_{n}": x for n, x in arrays.items()}], core_ids=[0])
    return r.results[0]["out"]
```
